# Optimizing a Trainium2 kernel written in Bass

```python
import jax, jax.numpy as jnp
from jax import lax
import numpy as np

D_MODEL = 1024
BATCH = 1
SEQ = 512
DEPTH = 1

CHUNK = 64
D_MIX = D_MODEL
D_MLSTM = D_MIX // 2
N_MLSTM_HEADS = 4
DH_MLSTM = D_MLSTM // N_MLSTM_HEADS
CONV_W = 4
D_GMLP = D_MIX - D_MLSTM
N_GMLP_GROUPS = 8
DG_GMLP = D_GMLP // N_GMLP_GROUPS
GMLP_BLOCK = 128
D_IN = 4 * D_MLSTM + 2 * N_MLSTM_HEADS + 2 * D_GMLP
N_EXPERT_GROUPS = 4
EXPERTS_PER_GROUP = 8
N_EXPERTS = N_EXPERT_GROUPS * EXPERTS_PER_GROUP
TOP_K = 2
D_FF_EXPERT = 512
MOE_BLOCK = 128
EPS = 1e-6


def rms_norm(x, g):
    xf = x.astype(jnp.float32)
    y = xf * lax.rsqrt(jnp.mean(xf * xf, axis=-1, keepdims=True) + EPS)
    return (y * g.astype(jnp.float32)).astype(x.dtype)

def head_rms(x):
    xf = x.astype(jnp.float32)
    return xf * lax.rsqrt(jnp.mean(xf * xf, axis=-1, keepdims=True) + EPS)

def causal_depthwise_conv(x, w):
    k = w.shape[0]
    s = x.shape[1]
    xp = jnp.pad(x, ((0, 0), (k - 1, 0), (0, 0)))
    y = w[0] * xp[:, 0:s]
    for i in range(1, k):
        y = y + w[i] * xp[:, i:i + s]
    return y

def mlstm_chunkwise(q, k, v, i_pre, f_pre):
    b_, s_, h_, dh = q.shape
    nc = s_ // CHUNK

    def to_chunks(a):
        a = a.reshape((b_, nc, CHUNK, h_) + a.shape[3:])
        return jnp.moveaxis(a, (1, 3), (0, 2))

    log_f = jax.nn.log_sigmoid(f_pre)
    xs = (to_chunks(q), to_chunks(k), to_chunks(v), to_chunks(i_pre), to_chunks(log_f))
    causal = jnp.tril(jnp.ones((CHUNK, CHUNK), dtype=bool))

    def step(carry, inp):
        c_st, n_st, m_st = carry
        qc, kc, vc, ic, lfc = inp
        bcum = jnp.cumsum(lfc, axis=-1)
        d = jnp.where(causal, bcum[..., :, None] - bcum[..., None, :] + ic[..., None, :], -jnp.inf)
        inter = bcum + m_st[..., None]
        m_t = jnp.maximum(inter, jnp.max(d, axis=-1))
        s = jnp.einsum('bhld,bhsd->bhls', qc, kc) * jnp.exp(d - m_t[..., None])
        w_inter = jnp.exp(inter - m_t)
        numer = jnp.einsum('bhls,bhsd->bhld', s, vc) + w_inter[..., None] * jnp.einsum('bhvd,bhld->bhlv', c_st, qc)
        nq = jnp.sum(s, axis=-1) + w_inter * jnp.einsum('bhd,bhld->bhl', n_st, qc)
        h = numer / jnp.maximum(jnp.abs(nq), jnp.exp(-m_t))[..., None]
        b_last = bcum[..., -1]
        w_state = b_last[..., None] - bcum + ic
        m_new = jnp.maximum(b_last + m_st, jnp.max(w_state, axis=-1))
        decay = jnp.exp(b_last + m_st - m_new)
        ws = jnp.exp(w_state - m_new[..., None])
        c_new = decay[..., None, None] * c_st + jnp.einsum('bhl,bhlv,bhld->bhvd', ws, vc, kc)
        n_new = decay[..., None] * n_st + jnp.einsum('bhl,bhld->bhd', ws, kc)
        return (c_new, n_new, m_new), h

    init = (jnp.zeros((b_, h_, dh, dh), jnp.float32), jnp.zeros((b_, h_, dh), jnp.float32),
            jnp.zeros((b_, h_), jnp.float32))
    _, hs = lax.scan(step, init, xs)
    return jnp.moveaxis(hs, (0, 2), (1, 3)).reshape(b_, s_, h_, dh)

def hybrid_mixer(xn, w_in, conv_qk, b_igate, b_fgate, g_mlstm_out, g_gmlp_v, w_spatial, b_spatial, g_gmlp_out, w_out):
    b_, s_, _ = xn.shape
    hh = N_MLSTM_HEADS
    proj = jnp.einsum('bsd,de->bse', xn, w_in)
    cuts = [2 * D_MLSTM, 3 * D_MLSTM, 4 * D_MLSTM, 4 * D_MLSTM + 2 * hh, 4 * D_MLSTM + 2 * hh + D_GMLP]
    qk, v_m, o_pre, if_pre, u_g, v_g = jnp.split(proj, cuts, axis=-1)

    qk = jax.nn.silu(causal_depthwise_conv(qk, conv_qk))
    q, k = jnp.split(qk.astype(jnp.float32), 2, axis=-1)
    q = q.reshape(b_, s_, hh, DH_MLSTM)
    k = k.reshape(b_, s_, hh, DH_MLSTM) * (DH_MLSTM ** -0.5)
    vm = v_m.astype(jnp.float32).reshape(b_, s_, hh, DH_MLSTM)
    i_pre = if_pre[..., :hh].astype(jnp.float32) + b_igate.astype(jnp.float32)
    f_pre = if_pre[..., hh:].astype(jnp.float32) + b_fgate.astype(jnp.float32)
    h_m = mlstm_chunkwise(q, k, vm, i_pre, f_pre)
    h_m = jax.nn.sigmoid(o_pre.astype(jnp.float32)).reshape(b_, s_, hh, DH_MLSTM) * h_m
    y_m = (head_rms(h_m).reshape(b_, s_, D_MLSTM) * g_mlstm_out.astype(jnp.float32)).astype(xn.dtype)

    nb = s_ // GMLP_BLOCK
    u = jax.nn.gelu(u_g)
    vg = rms_norm(jax.nn.gelu(v_g), g_gmlp_v)
    vb = vg.reshape(b_, nb, GMLP_BLOCK, N_GMLP_GROUPS, DG_GMLP)
    tri = jnp.tril(jnp.ones((GMLP_BLOCK, GMLP_BLOCK), dtype=w_spatial.dtype))
    mix = jnp.einsum('gts,bnsgc->bntgc', w_spatial * tri, vb) + b_spatial.T[:, :, None]
    gated = u.reshape(b_, nb, GMLP_BLOCK, N_GMLP_GROUPS, DG_GMLP) * mix
    y_g = (head_rms(gated).reshape(b_, s_, D_GMLP) * g_gmlp_out.astype(jnp.float32)).astype(xn.dtype)

    y = jnp.concatenate([y_m, y_g], axis=-1)
    return jnp.einsum('bse,ed->bsd', y, w_out)

def hierarchical_moe(xn, w_rg, b_rg, w_re, b_re, w_gate, w_up, w_down):
    b_, s_, d = xn.shape
    t = b_ * s_
    xf = xn.reshape(t, d)
    p_g = jax.nn.softmax((xf @ w_rg).astype(jnp.float32) + b_rg.astype(jnp.float32), axis=-1)
    g_sel = jnp.argmax(p_g, axis=-1)
    p_gsel = jnp.take_along_axis(p_g, g_sel[:, None], axis=-1)[:, 0]
    le = ((xf @ w_re).astype(jnp.float32) + b_re.astype(jnp.float32)).reshape(t, N_EXPERT_GROUPS, EXPERTS_PER_GROUP)
    le = jnp.take_along_axis(le, g_sel[:, None, None], axis=1)[:, 0]
    top_p, top_i = lax.top_k(jax.nn.softmax(le, axis=-1), TOP_K)
    top_p = top_p / jnp.sum(top_p, axis=-1, keepdims=True)
    weights = p_gsel[:, None] * top_p
    experts = (g_sel[:, None] * EXPERTS_PER_GROUP + top_i).astype(jnp.int32)

    n_pairs = t * TOP_K
    e_flat = experts.reshape(-1)
    tok_flat = jnp.repeat(jnp.arange(t, dtype=jnp.int32), TOP_K)
    w_flat = weights.reshape(-1)
    order = jnp.argsort(e_flat)
    e_sorted = e_flat[order]
    counts = jnp.zeros((N_EXPERTS,), jnp.int32).at[e_flat].add(1)
    padded = (counts + MOE_BLOCK - 1) // MOE_BLOCK * MOE_BLOCK
    starts = jnp.cumsum(counts) - counts
    pad_ends = jnp.cumsum(padded)
    pad_starts = pad_ends - padded
    dest = pad_starts[e_sorted] + jnp.arange(n_pairs, dtype=jnp.int32) - starts[e_sorted]
    n_blocks = n_pairs // MOE_BLOCK + N_EXPERTS
    n_rows = n_blocks * MOE_BLOCK
    row_tok = jnp.full((n_rows,), t, jnp.int32).at[dest].set(tok_flat[order])
    row_w = jnp.zeros((n_rows,), jnp.float32).at[dest].set(w_flat[order])
    block_e = jnp.minimum(jnp.searchsorted(pad_ends, jnp.arange(n_blocks, dtype=jnp.int32) * MOE_BLOCK, side='right'),
                          N_EXPERTS - 1)
    x_pad = jnp.concatenate([xf, jnp.zeros((1, d), xf.dtype)], axis=0)
    xb = x_pad[row_tok].reshape(n_blocks, MOE_BLOCK, d)

    def expert_block(args):
        xblk, e = args
        hid = jax.nn.silu(xblk @ w_gate[e]) * (xblk @ w_up[e])
        return hid @ w_down[e]

    yb = lax.map(expert_block, (xb, block_e)).reshape(n_rows, d)
    y = jax.ops.segment_sum(yb * row_w[:, None].astype(yb.dtype), row_tok, num_segments=t + 1)[:t]
    return y.reshape(b_, s_, d)

def first_inputs(seed: int = 0) -> dict:
    key = jax.random.key(seed)
    ks = jax.random.split(key, 20)
    f32 = jnp.float32
    nrm = lambda k, shape, scale: jax.random.normal(k, shape, f32) * scale
    return {
        "x": nrm(ks[0], (BATCH, SEQ, D_MODEL), 1.0),
        "norm1_g": 1.0 + nrm(ks[1], (DEPTH, D_MODEL), 0.02),
        "w_in": nrm(ks[2], (DEPTH, D_MODEL, D_IN), D_MODEL ** -0.5),
        "conv_qk": nrm(ks[3], (DEPTH, CONV_W, 2 * D_MLSTM), CONV_W ** -0.5),
        "b_igate": nrm(ks[4], (DEPTH, N_MLSTM_HEADS), 0.1),
        "b_fgate": jnp.linspace(3.0, 6.0, N_MLSTM_HEADS, dtype=f32)[None, :] + nrm(ks[5], (DEPTH, N_MLSTM_HEADS), 0.1),
        "g_mlstm_out": 1.0 + nrm(ks[6], (DEPTH, D_MLSTM), 0.02),
        "g_gmlp_v": 1.0 + nrm(ks[7], (DEPTH, D_GMLP), 0.02),
        "w_spatial": nrm(ks[8], (DEPTH, N_GMLP_GROUPS, GMLP_BLOCK, GMLP_BLOCK), 0.5 * GMLP_BLOCK ** -0.5),
        "b_spatial": 1.0 + nrm(ks[9], (DEPTH, N_GMLP_GROUPS, GMLP_BLOCK), 0.01),
        "g_gmlp_out": 1.0 + nrm(ks[10], (DEPTH, D_GMLP), 0.02),
        "w_out": nrm(ks[11], (DEPTH, D_MIX, D_MODEL), D_MIX ** -0.5),
        "norm2_g": 1.0 + nrm(ks[12], (DEPTH, D_MODEL), 0.02),
        "w_router_group": nrm(ks[13], (DEPTH, D_MODEL, N_EXPERT_GROUPS), D_MODEL ** -0.5),
        "b_router_group": nrm(ks[14], (DEPTH, N_EXPERT_GROUPS), 0.01),
        "w_router_expert": nrm(ks[15], (DEPTH, D_MODEL, N_EXPERTS), D_MODEL ** -0.5),
        "b_router_expert": nrm(ks[16], (DEPTH, N_EXPERTS), 0.01),
        "w_gate": nrm(ks[17], (DEPTH, N_EXPERTS, D_MODEL, D_FF_EXPERT), D_MODEL ** -0.5),
        "w_up": nrm(ks[18], (DEPTH, N_EXPERTS, D_MODEL, D_FF_EXPERT), D_MODEL ** -0.5),
        "w_down": nrm(ks[19], (DEPTH, N_EXPERTS, D_FF_EXPERT, D_MODEL), D_FF_EXPERT ** -0.5),
        "final_g": 1.0 + nrm(jax.random.fold_in(key, 99), (D_MODEL,), 0.02),
    }

def first_block(x, norm1_g, w_in, conv_qk, b_igate, b_fgate, g_mlstm_out, g_gmlp_v, w_spatial, b_spatial,
              g_gmlp_out, w_out, norm2_g, w_router_group, b_router_group, w_router_expert, b_router_expert,
              w_gate, w_up, w_down, final_g):
    h = x
    for l in range(DEPTH):
        h = h + hybrid_mixer(rms_norm(h, norm1_g[l]), w_in[l], conv_qk[l], b_igate[l], b_fgate[l],
                             g_mlstm_out[l], g_gmlp_v[l], w_spatial[l], b_spatial[l], g_gmlp_out[l], w_out[l])
        h = h + hierarchical_moe(rms_norm(h, norm2_g[l]), w_router_group[l], b_router_group[l],
                                 w_router_expert[l], b_router_expert[l], w_gate[l], w_up[l], w_down[l])
    return rms_norm(h, final_g)


DEPTH_2 = 2

N_MIXERS = 2
N_HGRN_LAYERS = (DEPTH_2 + 1) // 2
N_ATTN_LAYERS = DEPTH_2 // 2

HGRN_EXPAND = 128
HGRN_HEADS = D_MODEL // HGRN_EXPAND
HGRN_KEY_DIM = HGRN_EXPAND
HGRN_VAL_DIM = D_MODEL // HGRN_HEADS
HGRN_QK_WIDTH = HGRN_HEADS * HGRN_KEY_DIM
HGRN_V_WIDTH = HGRN_HEADS * HGRN_VAL_DIM
HGRN_IN_WIDTH = 2 * HGRN_QK_WIDTH + 2 * HGRN_V_WIDTH
HGRN_CHUNK = 64

ATTN_HEAD_DIM = 128
DILATED_GROUPS = ((128, 1), (512, 4), (2048, 16))
HEADS_PER_GROUP = 4
N_GROUPS = len(DILATED_GROUPS)
ATTN_HEADS = HEADS_PER_GROUP * N_GROUPS
ATTN_WIDTH = ATTN_HEADS * ATTN_HEAD_DIM
ROPE_THETA = 10000.0

D_FF = ((8 * D_MODEL // 3 + 255) // 256) * 256

NORM_EPS = 1e-6


def rmsnorm(x, gain):
    xf = x.astype(jnp.float32)
    y = xf * lax.rsqrt(jnp.mean(xf * xf, axis=-1, keepdims=True) + NORM_EPS)
    return (y * gain.astype(jnp.float32)).astype(x.dtype)

def rope_tables(seq_len):
    inv_freq = 1.0 / (ROPE_THETA ** (jnp.arange(0, ATTN_HEAD_DIM, 2, dtype=jnp.float32) / ATTN_HEAD_DIM))
    pos = jnp.arange(seq_len, dtype=jnp.float32)
    ang = pos[:, None] * inv_freq[None, :]
    return jnp.cos(ang)[:, None, :], jnp.sin(ang)[:, None, :]

def apply_rope(x, cos, sin):
    xf = x.astype(jnp.float32)
    x1, x2 = jnp.split(xf, 2, axis=-1)
    out = jnp.concatenate([x1 * cos - x2 * sin, x2 * cos + x1 * sin], axis=-1)
    return out.astype(x.dtype)

def hgrn2_mixer(u, w_in, lower_bound, out_gain, w_out):
    B, S, _ = u.shape
    H, K, V, C = HGRN_HEADS, HGRN_KEY_DIM, HGRN_VAL_DIM, HGRN_CHUNK
    proj = u @ w_in
    q, f, i, g = jnp.split(proj, [HGRN_QK_WIDTH, 2 * HGRN_QK_WIDTH, 2 * HGRN_QK_WIDTH + HGRN_V_WIDTH], axis=-1)
    lb = lower_bound.astype(jnp.float32)
    forget = lb + (1.0 - lb) * jax.nn.sigmoid(f.astype(jnp.float32))
    key = 1.0 - forget
    log_f = jnp.log(forget)
    query = jax.nn.silu(q.astype(jnp.float32))
    value = i.astype(jnp.float32)

    def to_chunks(t, d):
        return t.reshape(B, S // C, C, H, d).transpose(1, 0, 3, 2, 4)

    xs = (to_chunks(query, K), to_chunks(key, K), to_chunks(value, V), to_chunks(log_f, K))
    causal = jnp.tril(jnp.ones((C, C), dtype=bool))[:, :, None]

    def chunk_step(state, inp):
        qc, kc, vc, gc = inp
        b = jnp.cumsum(gc, axis=2)
        o_inter = jnp.einsum('bhck,bhkv->bhcv', qc * jnp.exp(b), state)
        diff = b[:, :, :, None, :] - b[:, :, None, :, :]
        decay = jnp.exp(jnp.where(causal, diff, -jnp.inf))
        scores = jnp.einsum('bhtk,bhsk,bhtsk->bhts', qc, kc, decay)
        o_intra = jnp.einsum('bhts,bhsv->bhtv', scores, vc)
        b_last = b[:, :, -1, :]
        k_to_end = kc * jnp.exp(b_last[:, :, None, :] - b)
        new_state = jnp.exp(b_last)[..., None] * state + jnp.einsum('bhck,bhcv->bhkv', k_to_end, vc)
        return new_state, o_inter + o_intra

    state0 = jnp.zeros((B, H, K, V), dtype=jnp.float32)
    _, o = lax.scan(chunk_step, state0, xs)
    o = o.transpose(1, 0, 3, 2, 4).reshape(B, S, H, V)
    o = rmsnorm(o, out_gain)
    o = o * jax.nn.silu(g.astype(jnp.float32)).reshape(B, S, H, V)
    return o.reshape(B, S, H * V).astype(u.dtype) @ w_out

def dilated_window_group(q, k, v, window, dilation):
    B, S, Hg, D = q.shape
    span = window // dilation
    L = S // dilation
    nb = -(-L // span)
    Lp = nb * span

    def to_blocks(t):
        t = t.reshape(B, L, dilation, Hg, D).transpose(0, 2, 3, 1, 4)
        t = jnp.pad(t, ((0, 0), (0, 0), (0, 0), (0, Lp - L), (0, 0)))
        return t.reshape(B, dilation, Hg, nb, span, D)

    qb, kb, vb = to_blocks(q), to_blocks(k), to_blocks(v)

    def with_prev(t):
        prev = jnp.pad(t, ((0, 0), (0, 0), (0, 0), (1, 0), (0, 0), (0, 0)))[:, :, :, :-1]
        return jnp.concatenate([prev, t], axis=4)

    kw, vw = with_prev(kb), with_prev(vb)
    scores = jnp.einsum('bdhnqe,bdhnke->bdhnqk', qb, kw, preferred_element_type=jnp.float32) * (D ** -0.5)
    blk = jnp.arange(nb)[:, None, None] * span
    qpos = blk + jnp.arange(span)[None, :, None]
    kpos = blk - span + jnp.arange(2 * span)[None, None, :]
    mask = (kpos <= qpos) & (kpos >= qpos - span) & (kpos >= 0)
    scores = jnp.where(mask, scores, -jnp.inf)
    m = jnp.max(scores, axis=-1, keepdims=True)
    p = jnp.exp(scores - m)
    l = jnp.sum(p, axis=-1, keepdims=True)
    out = jnp.einsum('bdhnqk,bdhnke->bdhnqe', p, vw.astype(jnp.float32)) / l
    lse = (m + jnp.log(l))[..., 0]
    out = out.reshape(B, dilation, Hg, Lp, D)[:, :, :, :L].transpose(0, 3, 1, 2, 4).reshape(B, S, Hg, D)
    lse = lse.reshape(B, dilation, Hg, Lp)[:, :, :, :L].transpose(0, 3, 1, 2).reshape(B, S, Hg)
    return out, lse

def dilated_attention_mixer(u, w_qkv, w_out, cos, sin):
    B, S, _ = u.shape
    qkv = (u @ w_qkv).reshape(B, S, 3, ATTN_HEADS, ATTN_HEAD_DIM)
    q = apply_rope(qkv[:, :, 0], cos, sin)
    k = apply_rope(qkv[:, :, 1], cos, sin)
    v = qkv[:, :, 2]
    outs, lses = [], []
    for gi, (window, dilation) in enumerate(DILATED_GROUPS):
        hs = slice(gi * HEADS_PER_GROUP, (gi + 1) * HEADS_PER_GROUP)
        o_g, lse_g = dilated_window_group(q[:, :, hs], k[:, :, hs], v[:, :, hs], window, dilation)
        outs.append(o_g)
        lses.append(lse_g)
    o = jnp.stack(outs, axis=2)
    lse = jnp.stack(lses, axis=2)
    alpha = jax.nn.softmax(lse, axis=2)
    o = (o * alpha[..., None]).reshape(B, S, ATTN_WIDTH).astype(u.dtype)
    return o @ w_out

def swiglu_ffn(u, w_in, w_down):
    gate, up = jnp.split(u @ w_in, 2, axis=-1)
    return (jax.nn.silu(gate) * up) @ w_down

def second_inputs(seed: int = 0) -> dict:
    key = jax.random.key(seed)
    ks = jax.random.split(key, 13)
    f32 = jnp.float32

    def dense(k, shape, fan_in):
        return jax.random.normal(k, shape, f32) * (fan_in ** -0.5)

    def gain(k, shape):
        return 1.0 + 0.02 * jax.random.normal(k, shape, f32)

    return {
        "x": jax.random.normal(ks[0], (BATCH, SEQ, D_MODEL), f32),
        "norm_mix": gain(ks[1], (DEPTH_2, D_MODEL)),
        "norm_ffn": gain(ks[2], (DEPTH_2, D_MODEL)),
        "hgrn_w_in": dense(ks[3], (N_HGRN_LAYERS, D_MODEL, HGRN_IN_WIDTH), D_MODEL),
        "hgrn_lb_logits": 0.5 * jax.random.normal(ks[4], (DEPTH_2 + 1, HGRN_QK_WIDTH), f32),
        "hgrn_out_norm": gain(ks[5], (N_HGRN_LAYERS, HGRN_VAL_DIM)),
        "hgrn_w_out": dense(ks[6], (N_HGRN_LAYERS, HGRN_V_WIDTH, D_MODEL), HGRN_V_WIDTH),
        "attn_w_qkv": dense(ks[7], (N_ATTN_LAYERS, D_MODEL, 3 * ATTN_WIDTH), D_MODEL),
        "attn_w_out": dense(ks[8], (N_ATTN_LAYERS, ATTN_WIDTH, D_MODEL), ATTN_WIDTH),
        "ffn_w_in": dense(ks[9], (DEPTH_2, D_MODEL, 2 * D_FF), D_MODEL),
        "ffn_w_down": dense(ks[10], (DEPTH_2, D_FF, D_MODEL), D_FF),
        "final_norm": gain(ks[11], (D_MODEL,)),
    }

def second_block(x, norm_mix, norm_ffn, hgrn_w_in, hgrn_lb_logits, hgrn_out_norm, hgrn_w_out,
              attn_w_qkv, attn_w_out, ffn_w_in, ffn_w_down, final_norm):
    lb_table = jnp.cumsum(jax.nn.softmax(hgrn_lb_logits.astype(jnp.float32), axis=0), axis=0)
    cos, sin = rope_tables(x.shape[1])
    h = x
    for layer in range(DEPTH_2):
        u = rmsnorm(h, norm_mix[layer])
        if layer % N_MIXERS == 0:
            a = layer // N_MIXERS
            mix = hgrn2_mixer(u, hgrn_w_in[a], lb_table[layer], hgrn_out_norm[a], hgrn_w_out[a])
        else:
            a = layer // N_MIXERS
            mix = dilated_attention_mixer(u, attn_w_qkv[a], attn_w_out[a], cos, sin)
        h = h + mix
        h = h + swiglu_ffn(rmsnorm(h, norm_ffn[layer]), ffn_w_in[layer], ffn_w_down[layer])
    return rmsnorm(h, final_norm)


def setup_inputs(seed=0):
    out = dict(first_inputs(seed))
    for name, value in second_inputs(seed + 1).items():
        if name != "x":
            out[name + "_2"] = value
    return out


def reference(
    x, norm1_g, w_in, conv_qk, b_igate, b_fgate, g_mlstm_out, g_gmlp_v, w_spatial, b_spatial,
    g_gmlp_out, w_out, norm2_g, w_router_group, b_router_group, w_router_expert,
    b_router_expert, w_gate, w_up, w_down, final_g, norm_mix_2, norm_ffn_2, hgrn_w_in_2,
    hgrn_lb_logits_2, hgrn_out_norm_2, hgrn_w_out_2, attn_w_qkv_2, attn_w_out_2, ffn_w_in_2,
    ffn_w_down_2, final_norm_2,
):
    x = first_block(
        x, norm1_g, w_in, conv_qk, b_igate, b_fgate, g_mlstm_out, g_gmlp_v, w_spatial,
        b_spatial, g_gmlp_out, w_out, norm2_g, w_router_group, b_router_group, w_router_expert,
        b_router_expert, w_gate, w_up, w_down, final_g,
    )
    return second_block(
        x, norm_mix_2, norm_ffn_2, hgrn_w_in_2, hgrn_lb_logits_2, hgrn_out_norm_2, hgrn_w_out_2,
        attn_w_qkv_2, attn_w_out_2, ffn_w_in_2, ffn_w_down_2, final_norm_2,
    )


_drawn_inputs = setup_inputs


def setup_inputs(seed=0):
    import zlib

    import numpy as np

    out = dict(_drawn_inputs(seed))
    spreads = {}
    factors = {'b_igate': 64.0,
     'g_gmlp_v': 128.384,
     'b_spatial': 200.0,
     'b_router_group': 3.001,
     'b_router_expert': 3.042,
     'norm_mix_2': 3.174,
     'norm_ffn_2': 3.084,
     'hgrn_lb_logits_2': 2.816,
     'hgrn_out_norm_2': 4.092,
     'final_norm_2': 7.119}
    for name, (base, spread) in spreads.items():
        noise = np.random.default_rng([zlib.crc32(name.encode()), seed]).standard_normal(out[name].shape)
        drawn = base * np.exp(spread * noise) if base else spread * noise
        out[name] = __import__('jax').numpy.asarray(drawn.astype(out[name].dtype))
    for name, factor in factors.items():
        out[name] = (out[name] * factor).astype(out[name].dtype)
    return out
```

```python
from contextlib import ExitStack

import numpy as np

import concourse.bass as bass
from concourse import mybir

ALU = mybir.AluOpType
ACT = mybir.ActivationFunctionType
AX = mybir.AxisListType
F32 = mybir.dt.float32
F32R = mybir.dt.float32r
I32 = mybir.dt.int32
U32 = mybir.dt.uint32

P = 128
T = 512
TB = T // P
D = 1024
KC = D // P
EPS = 1e-6
H1 = 4
HALF = D // 2
NG = 8
NE = 32
EG = 4
PER = NE // EG
FE = 512
HH = 8
FF = 2816
FC = FF // P
AH = 4
DIL = (1, 4, 16)
STEP = (1, 4, 4)
AW = 3 * AH * P
DH_SCALE = float(P) ** -0.5
NEG = -1.0e30
UNIT = 2048
RAW = 4
FA = 12

U_IN = 0
N_IN = 12
U_OUT = U_IN + N_IN
N_OUT = 4
U_MOE = U_OUT + N_OUT
PER_EXPERT = 6
U_HG = U_MOE + NE * PER_EXPERT
U_HGO = U_HG + 16
U_FF0 = U_HGO + 4
N_FF = FC + 12
U_QKV = U_FF0 + N_FF
U_AO = U_QKV + 18
U_FF1 = U_AO + 6
N_UNITS = U_FF1 + N_FF

def columns(*sizes):
    at, out = 0, {}
    for name, n in sizes:
        out[name] = (at, n)
        at += n
    return out, at

C_COLS, C_N = columns(("ident", P), ("upper", P), ("strict", P), ("ones", P), ("blocks64", P), ("negmask", P),
                      ("sel", H1 * P), ("eps", 1), ("iota32", NE))
P1_COLS, P1_N = columns(("n1g", KC), ("conv", 4 * KC), ("b_i", 1), ("b_f", 1), ("g_ml", 4), ("g_v", 4), ("g_gm", 4),
                        ("b_sp", 4 * P), ("w_sp", NG * P), ("w_if", KC * P), ("one_row", T))
P2_COLS, P2_N = columns(("n2g", D), ("w_r", KC * 36), ("b_r", 36), ("fg", KC), ("pairs", 4 * TB))
P3_COLS, P3_N = columns(("n_mix", 2 * KC), ("n_ffn", 2 * KC), ("lb", 3 * KC), ("og", 1), ("fin", D),
                        ("levels", 8 * P), ("cos", T), ("sin", T), ("band", 3 * 256), ("reset", T))


class Count:

    def __init__(self, sem):
        self.sem, self.n, self.per_trip, self.trip, self.start = sem, 0, 0, None, 0

    def value(self, back=0):
        n = self.n - back
        return n if self.trip is None else self.trip * self.per_trip + n

    def mark(self, instruction):
        instruction.then_inc(self.sem, 1)
        self.n += 1
        return self.value()

    def enter(self, trip, per_trip, first=0):
        self.trip, self.per_trip, self.start = trip, per_trip, self.n
        self.n -= first * per_trip

    def leave(self, trips, first=0):
        assert self.n + first * self.per_trip - self.start == self.per_trip, (self.n, self.start, self.per_trip)
        self.trip = None
        self.n = self.start + trips * self.per_trip


def build(nc, x_in, weights_in, constants_in, phase1_in, phase2_in, phase3_in, out):
    with ExitStack() as ctx:
        def sem(name):
            return ctx.enter_context(nc.semaphore(name))

        arena_at = nc.sbuf_base + -nc.sbuf_base % 32
        at_raw = arena_at
        at_hi = at_raw + RAW * UNIT * 4
        at_lo = at_hi + 2 * UNIT * 4
        at_res = at_lo + 2 * UNIT * 4
        at_con = at_res + TB * D * 4
        at_par = at_con + (C_N * 4 + 31) // 32 * 32
        at_a = at_par + (max(P1_N, P2_N, P3_N) * 4 + 31) // 32 * 32
        at_b = at_a + 24 * T * 4
        at_x = at_b + 28 * T * 4
        arena_end = at_x + 608
        ctx.enter_context(nc.sbuf_tensor("arena", [P, arena_end - arena_at], mybir.dt.uint8))

        def place(name, shape, at, dt=F32):
            return nc.alloc_sbuf_tensor_at(name, [P] + shape, dt, offset=at)

        KB2 = T * 4
        raw = place("raw", [RAW, UNIT], at_raw)
        w_hi = place("w_hi", [2, UNIT], at_hi, F32R)
        w_lo = place("w_lo", [2, UNIT], at_lo, F32R)
        res = place("res", [TB, D], at_res)
        con = place("con", [C_N], at_con)
        par1 = place("par1", [P1_N], at_par)

        def cols(tile, table, name):
            at, n = table[name]
            return tile[:, at:at + n]

        ident, ones = cols(con, C_COLS, "ident"), cols(con, C_COLS, "ones")
        eps = cols(con, C_COLS, "eps")

        u_hi = place("u_hi", [KC, T], at_a, F32R)
        u_lo = place("u_lo", [KC, T], at_a + KC * KB2, F32R)
        at_a2 = at_a + 16 * KB2

        xs = place("xs", [TB, D], at_b)
        qk = place("qk", [KC, T], at_b)
        so = place("so", [4, T], at_b + 8 * KB2)
        ug = place("ug", [4, T], at_b + 12 * KB2)
        vm = place("vm", [TB, HALF], at_b + 16 * KB2)
        vg = place("vg", [TB, HALF], at_b + 20 * KB2)
        junk = place("junk", [D], at_b + 20 * KB2)
        dec = place("dec", [TB, T], at_b + 24 * KB2)
        wif_hi = place("wif_hi", [KC, P], at_b + 24 * KB2, F32R)
        wif_lo = place("wif_lo", [KC, P], at_b + 26 * KB2, F32R)
        neg_m = place("neg_m", [T], at_a2)
        e_neg_m = place("e_neg_m", [T], at_a2 + KB2)
        r_f, r_i, r_e, r_sum = [place(f"row{n}", [T], at_a2 + (2 + n) * KB2) for n in range(4)]
        ml_a, ml_b, gm_a, gm_b = [place(f"tile{n}", [T], at_a2 + (2 + n) * KB2) for n in range(4)]
        g_col = place("g_col", [TB, H1], at_a2 + 6 * KB2)
        small = place("small", [16, TB], at_a2 + 6 * KB2 + 64)
        y_tmp = place("y_tmp", [T], at_a2 + 7 * KB2)


        par2 = place("par2", [P2_N], at_par)
        xn = place("xn", [TB, D], at_b)
        x_rows = place("x_rows", [2, D], at_b + 8 * KB2)
        xe_hi = place("xe_hi", [KC, P], at_b + 12 * KB2, F32R)
        xe_lo = place("xe_lo", [KC, P], at_b + 14 * KB2, F32R)
        gate = place("gate", [FE], at_b + 16 * KB2)
        hid = place("hid", [FE], at_b + 17 * KB2)
        hid_hi = place("hid_hi", [4, P], at_b + 18 * KB2, F32R)
        hid_lo = place("hid_lo", [4, P], at_b + 19 * KB2, F32R)
        y_rows = place("y_rows", [2, D], at_b + 20 * KB2)
        wr_hi = place("wr_hi", [KC, 36], at_b + 24 * KB2, F32R)
        wr_lo = place("wr_lo", [KC, 36], at_b + 24 * KB2 + 1152, F32R)
        at_r = [at_a2]

        def overflowing(eng):
            eng.wait_ge(dest_ready, 1)
            return eng.value_load(over_int[0:1, N_OVER:N_OVER + 1]) > 0

        def tiny(name, shape, dt=F32):
            t = place(name, shape, at_r[0], dt)
            at_r[0] += -(-int(np.prod(shape)) * 4 // 32) * 32
            assert at_r[0] <= at_b
            return t

        rms2 = tiny("rms2", [8, TB])
        logit, gap = tiny("logit", [TB, 36]), tiny("gap", [TB, EG])
        in_group, chosen = tiny("in_group", [TB, EG]), tiny("chosen", [TB, EG, PER])
        le1, le2 = tiny("le1", [TB, PER]), tiny("le2", [TB, PER])
        first, second = tiny("first", [TB, PER]), tiny("second", [TB, PER])
        best = tiny("best", [8, TB])
        weight = tiny("weight", [2, TB])
        owns = tiny("owns", [2, TB, NE])
        both, row, lift = tiny("both", [TB, NE]), tiny("row", [TB, NE]), tiny("lift", [TB, NE])
        blocks, over = tiny("blocks", [TB, NE]), tiny("over", [TB, NE])
        n_over, over_end, over_start = tiny("n_over", [NE]), tiny("over_end", [NE]), tiny("over_start", [NE])
        over_cmp, over_e = tiny("over_cmp", [8, NE]), tiny("over_e", [8])
        over_int = tiny("over_int", [16], I32)
        dest_f, dest = tiny("dest_f", [2, TB]), tiny("dest", [2, TB], I32)
        pairs = tiny("pairs", [TB, 2, 2], I32)
        slots = tiny("slots", [NE + 1, 2], I32)
        over_slots = tiny("over_slots", [8, 2], I32)
        y_pairs = place("y_pairs", [TB, 2, D], at_a)

        MAIN = P * NE
        N_OVER = 8
        NO_PAIR = 4096
        token_rows = nc.dram_tensor("token_rows", [T, D], F32, kind="Internal").ap()
        pair_rows = nc.dram_tensor("pair_rows", [2 * T, D], F32, kind="Internal").ap()
        slot_table = nc.dram_tensor("slot_table", [MAIN + N_OVER * P, 2], I32, kind="Internal").ap()
        hs = place("hs", [KC, T], at_res)

        over_weights = place("over_weights", [4, UNIT], at_a)
        over_xe = place("over_xe", [KC, P], at_b + 12 * KB2)
        over_hidt = place("over_hidt", [4, P], at_b + 18 * KB2)

        no_pairs = place("no_pairs", [80], at_x, I32)
        y_mark = place("y_mark", [8], at_x + 320, I32)

        par3 = place("par3", [P3_N], at_par)
        sq = [place(f"sq{n}", [T], at_a2 + n * KB2) for n in range(2)]
        rms = place("rms", [T], at_a2 + 2 * KB2)
        u_tmp = place("u_tmp", [T], at_a2 + 3 * KB2)
        o_hi = place("o_hi", [HH, T], at_b, F32R)
        o_lo = place("o_lo", [HH, T], at_b + 8 * KB2, F32R)
        fx = place("fx", [2, T], at_b + 16 * KB2)
        key = place("key", [2, T], at_b + 18 * KB2)
        run = place("run", [2, T], at_b + 20 * KB2)
        qry = place("qry", [2, T], at_b + 22 * KB2)
        sg = place("sg", [2, T], at_b + 24 * KB2)
        val = place("val", [TB, 256], at_b + 26 * KB2)
        ws = place("ws", [TB, T], at_a2)
        k_dec = [place(f"k_dec{n}", [T], at_a2 + (4 + 2 * n) * KB2) for n in range(2)]
        q_dec = [place(f"q_dec{n}", [T], at_a2 + (5 + 2 * n) * KB2) for n in range(2)]
        b_exp = place("b_exp", [2], at_x + 352)
        turn = place("turn", [8], at_x + 576)
        lbs = [place(f"lbs{n}", [KC], at_x + 384 + 32 * n) for n in range(6)]
        hid2_hi = place("hid2_hi", [FA, T], at_b, F32R)
        hid2_lo = place("hid2_lo", [FA, T], at_b + FA * KB2, F32R)
        f_gate = [place(f"f_gate{n}", [T], at_a2 + (4 + n) * KB2) for n in range(2)]
        f_hid = [place(f"f_hid{n}", [T], at_a2 + (6 + n) * KB2) for n in range(2)]
        prob = place("prob", [8192], at_b)
        vals = place("vals", [3, TB, AH * P], at_b + 16 * KB2)
        q_rot = [place(f"q_rot{n}", [T], at_a2 + n * KB2) for n in range(2)]
        k_rot = [place(f"k_rot{n}", [T], at_a2 + (2 + n) * KB2) for n in range(2)]
        r_cos = [place(f"r_cos{n}", [T], at_a2 + (4 + n) * KB2) for n in range(2)]
        r_sin = [place(f"r_sin{n}", [T], at_a2 + (6 + n) * KB2) for n in range(2)]
        ao_hi = place("ao_hi", [3 * AH, T], at_a, F32R)
        ao_lo = place("ao_lo", [3 * AH, T], at_a + 3 * AH * KB2, F32R)
        at_stat = at_par + P3_COLS["levels"][0] * 4
        at_stat += -at_stat % 32
        stat = [place(f"stat{g}", [TB, 8], at_stat + 128 * g) for g in range(3)]
        stat_nat = [place(f"stat_nat{g}", [TB, 8], at_stat + 384 + 128 * g) for g in range(3)]
        share = place("share", [3, TB, AH], at_stat + 768)
        share_g = [place(f"share_g{g}", [TB, AH], at_stat + 960 + 64 * g) for g in range(3)]
        top = place("top", [TB, AH], at_stat + 1152)
        den = place("den", [TB, AH], at_stat + 1216)
        out_tile = [place(f"out_tile{n}", [D], at_b + 2 * n * KB2) for n in range(2)]
        out_sq = place("out_sq", [T], at_b + 4 * KB2)
        out_rms = place("out_rms", [8, TB], at_b + 5 * KB2)
        stat_rows = nc.dram_tensor("stat_rows", [2, T, 8], F32, kind="Internal").ap()
        share_rows = nc.dram_tensor("share_rows", [2, T, AH], F32, kind="Internal").ap()

        def prob_of(g, h):
            width = (256, P, P)[g]
            at = h * 1024 if g == 0 else 4096 + (g - 1) * 2048 + h * 512
            return prob[:, at:at + TB * width].rearrange("p (b s) -> p b s", b=TB)

        def group_order(ap, g):
            return ap.rearrange("q (r p) -> q p r", r=STEP[g])

        def natural_order(ap, g):
            return ap.rearrange("q (p r) -> q p r", r=STEP[g])

        lb_tile = cols(par3, P3_COLS, "lb")
        HG_STEPS = 2 + 2 * 4
        PROJ_ATTN = 4 * (HH // 2) + FC

        def norm_bank(k):
            return bank[0 if k else 7]

        def query_part(pool, p, hh, n):
            w = 64 >> n
            pool.wait_ge(lev_exp, p * 14 + (7 * hh + n + 1))
            if n >= 2:
                pool.wait_ge(lev_ready, p * 16 + (8 * hh + n - 1))

            def view(ap):
                return ap.rearrange("p (n t) -> p n t", t=2 * w)[:, :, w:]
            nc.gpsimd.tensor_tensor(view(q_dec[n % 2][:]), view(fx[:, n % 2]), view(qry[:, hh]), ALU.mult).then_inc(q_ready, 1)

        bank = [ctx.enter_context(nc.psum_tensor(f"bank{n}", [P, T], F32)) for n in range(8)]

        raw_landed = [sem(f"raw_landed{n}") for n in range(RAW)]
        hi_ready, lo_ready, unit_used = sem("hi_ready"), sem("lo_ready"), sem("unit_used")
        x_landed, con_landed, params_landed = sem("x_landed"), sem("con_landed"), sem("params_landed")
        act_step, dve_step = sem("act_step"), sem("dve_step")
        out_stored = [sem("out_stored0"), sem("out_stored1")]
        sq_ready, rms_arg, root_ready, xs_ready = sem("sq_ready"), sem("rms_arg"), sem("root_ready"), sem("xs_ready")
        turned, u_hi_ready, u_lo_ready = sem("turned"), sem("u_hi_ready"), sem("u_lo_ready")
        narrow_hi, narrow_lo, gates_ready = sem("narrow_hi"), sem("narrow_lo"), sem("gates_ready")
        in_ready, in_conv, in_act, qk_ready = sem("in_ready"), sem("in_conv"), sem("in_act"), sem("qk_ready")
        soft_arg, soft_log, rows_ready, em_ready = sem("soft_arg"), sem("soft_log"), sem("rows_ready"), sem("em_ready")
        g_turned, g_col_ready = sem("g_turned"), sem("g_col_ready")
        vg_ready, wsp_ready = sem("vg_ready"), sem("wsp_ready")
        m_spread, s_ready, dec_arg, dec_ready, s_weighted = (sem("m_spread"), sem("s_ready"), sem("dec_arg"),
                                                             sem("dec_ready"), sem("s_weighted"))
        num_ready, nq_abs, h_ready, h_sq, h_ss, h_root, ym_ready, ym_hi = [
            sem(n) for n in ("num_ready", "nq_abs", "h_ready", "h_sq", "h_ss", "h_root", "ym_ready", "ym_hi")]
        mix_ready, gated_ready, gated_sq, gated_ss, gated_root, yg_ready, yg_hi, y_lo_ready = [
            sem(n) for n in ("mix_ready", "gated_ready", "gated_sq", "gated_ss", "gated_root", "yg_ready", "yg_hi",
                             "y_lo_ready")]
        out1_ready, res1_ready = sem("out1_ready"), sem("res1_ready")


        xn_ready, tokens_stored = sem("xn_ready"), sem("tokens_stored")
        logits_ready, router_arg, router_exp = sem("logits_ready"), sem("router_arg"), sem("router_exp")
        owns_ready, before_ready, dest_ready = sem("owns_ready"), sem("before_ready"), sem("dest_ready")
        table_written, slots_landed = sem("table_written"), sem("slots_landed")
        rows_set = sem("rows_set")
        x_gathered = [sem("x_gathered0"), sem("x_gathered1")]
        y_free = [sem("y_free0"), sem("y_free1")]
        xe_turned, xe_hi_ready, xe_lo_ready = sem("xe_turned"), sem("xe_hi_ready"), sem("xe_lo_ready")
        silu_ready, hid_ready, hid_turned, hid_hi_ready, hid_lo_ready = [
            sem(n) for n in ("silu_ready", "hid_ready", "hid_turned", "hid_hi_ready", "hid_lo_ready")]
        y_act, y_dve, y_landed, res2_ready = sem("y_act"), sem("y_dve"), sem("y_landed"), sem("res2_ready")
        h_turned, h0_ready = sem("h_turned"), sem("h0_ready")
        over_x, over_w, over_stored = sem("over_x"), sem("over_w"), sem("over_stored")
        over_products, over_copies, over_hid = sem("over_products"), sem("over_copies"), sem("over_hid")

        n_sq, n_sum, n_root, u_ready = sem("n_sq"), sem("n_sum"), sem("n_root"), sem("u_ready")
        h_added = sem("h_added")
        lb_arg, lb_exp, lb_ready = sem("lb_arg"), sem("lb_exp"), sem("lb_ready")
        proj_ready, f_sig, f_ready, f_log, run_ready = (sem("proj_ready"), sem("f_sig"), sem("f_ready"), sem("f_log"),
                                                        sem("run_ready"))
        q_taken, v_taken, g_taken = sem("q_taken"), sem("v_taken"), sem("g_taken")
        set_up, gap_to_ref, lev_exp, k_ready, q_ready = (sem("set_up"), sem("gap_to_ref"), sem("lev_exp"),
                                                         sem("k_ready"), sem("q_ready"))
        lev_ready, lev_taken = sem("lev_ready"), sem("lev_taken")
        far_exp, far_kq, far_ready, far_taken = sem("far_exp"), sem("far_kq"), sem("far_ready"), sem("far_taken")
        o_sum, o_sq, o_ss, o_root, o_ready, o_hi_ready, o_lo_ready = [
            sem(n) for n in ("o_sum", "o_sq", "o_ss", "o_root", "o_ready", "o_hi_ready", "o_lo_ready")]
        f_silu, f_prod, f_hi, f_lo = sem("f_silu"), sem("f_prod"), sem("f_hi"), sem("f_lo")
        v_ready, rope_mul, rope_ready, sc_ready, sc_max, sc_gap, sc_exp, sc_sum = [
            sem(n) for n in ("v_ready", "rope_mul", "rope_ready", "sc_ready", "sc_max", "sc_gap", "sc_exp", "sc_sum")]
        order_stored, order_landed, share_arg, share_exp, share_ready = [
            sem(n) for n in ("order_stored", "order_landed", "share_arg", "share_exp", "share_ready")]
        p_ready, p_turned, pt_ready, ao_sum, ao_hi_ready, ao_lo_ready = [
            sem(n) for n in ("p_ready", "p_turned", "pt_ready", "ao_sum", "ao_hi_ready", "ao_lo_ready")]
        fin_turned, fin_ready = sem("fin_turned"), sem("fin_ready")
        block = ctx.enter_context(nc.Block())
        STREAM_END = N_UNITS

        @block.sync
        def _(sp):
            sp.dma_start(res[:], x_in.rearrange("(b p) d -> p b d", p=P)).then_inc(x_landed, 16)
            sp.dma_start(con[:], constants_in).then_inc(con_landed, 16)
            sp.dma_start(par1[:], phase1_in).then_inc(con_landed, 16)
            for n in range(RAW):
                sp.dma_start(raw[:, n], weights_in[n]).then_inc(raw_landed[n], 16)
            with sp.Fori(1, STREAM_END // RAW) as i:
                for j in range(RAW):
                    sp.wait_ge(lo_ready, i * RAW + (j + 1 - RAW))
                    sp.dma_start(raw[:, j], weights_in[bass.ds(i * RAW + j, 1)].rearrange("u p n -> p (u n)")) \
                        .then_inc(raw_landed[j], 16)

            for b in range(TB):
                sp.wait_ge(fin_ready, b + 1)
                sp.dma_start(out[b * P:(b + 1) * P, :], out_tile[b % 2][:]).then_inc(out_stored[b % 2], 16)
            for n in range(2):
                sp.wait_ge(out_stored[n], 32)

        @block.tensor
        def _(pe):
            def unit_wait(n):
                pe.wait_ge(hi_ready, n + 1)
                pe.wait_ge(lo_ready, n + 1)

            def product(out_ap, a_hi, a_lo, b_hi, b_lo, first, last):
                nc.tensor.matmul(out_ap, a_hi, b_hi, start=first, stop=False)
                nc.tensor.matmul(out_ap, a_hi, b_lo, start=False, stop=False)
                return nc.tensor.matmul(out_ap, a_lo, b_hi, start=False, stop=last)

            def feature_chunk(out_ap, s, m):
                for k in range(KC):
                    w = slice(k * 256 + m * P, k * 256 + m * P + P)
                    mm = product(out_ap, w_hi[:, s, w], w_lo[:, s, w], u_hi[:, k], u_lo[:, k], k == 0, k == KC - 1)
                return mm

            def token_chunk(out_ap, s, tokens):
                for k in range(KC):
                    w = slice(k * 256, k * 256 + 256)
                    mm = product(out_ap, u_hi[:, k, tokens], u_lo[:, k, tokens], w_hi[:, s, w], w_lo[:, s, w],
                                 k == 0, k == KC - 1)
                return mm

            pe.wait_ge(con_landed, 32)
            pe.wait_ge(xs_ready, TB)
            for c in range(KC):
                if c >= 4:
                    pe.wait_ge(u_lo_ready, c - 3)
                for b in range(TB):
                    mm = nc.tensor.transpose(bank[c % 4][:, b * P:b * P + P], xs[:, b, c * P:c * P + P], ident)
                mm.then_inc(turned, 1)

            pe.wait_ge(narrow_lo, 1)
            pe.wait_ge(u_hi_ready, KC)
            pe.wait_ge(u_lo_ready, KC)
            for k in range(KC):
                mm = product(bank[4][:], wif_hi[:, k], wif_lo[:, k], u_hi[:, k], u_lo[:, k], k == 0, k == KC - 1)
            mm.then_inc(gates_ready, 1)

            def slot_free(q):
                old = q - 4
                if old >= 8:
                    pe.wait_ge(in_act, old - 7)
                elif old >= 0:
                    pe.wait_ge(in_conv, old + 1)

            for n in range(N_IN):
                unit_wait(n)
                if n in (4, 5, 10, 11):
                    for half in range(2):
                        q = 2 * n + half
                        slot_free(q)
                        for b in range(2):
                            tokens = slice((2 * half + b) * P, (2 * half + b) * P + P)
                            mm = token_chunk(bank[q % 4][:, b * 256:b * 256 + 256], n % 2, tokens)
                            if b == 0:
                                continue
                            if half == 0:
                                mm.then_inc(in_ready, 1)
                            else:
                                mm.then_inc(unit_used, 1)
                else:
                    for m in range(2):
                        q = 2 * n + m
                        slot_free(q)
                        mm = feature_chunk(bank[q % 4][:], n % 2, m)
                        mm.then_inc(in_ready if m == 0 else unit_used, 1)

            pe.wait_ge(rows_ready, 1)
            for b in range(TB):
                mm = nc.tensor.transpose(bank[4][:, b * H1:b * H1 + H1], r_i[0:H1, b * P:b * P + P], ident[0:H1, 0:H1])
            mm.then_inc(g_turned, 1)

            pe.wait_ge(in_act, 16)
            pe.wait_ge(qk_ready, KC)
            pe.wait_ge(vg_ready, TB)
            pe.wait_ge(wsp_ready, 1)
            sel = cols(con, C_COLS, "sel")
            for h in range(H1):
                if h:
                    pe.wait_ge(h_ready, h)
                nc.tensor.matmul(bank[0][:], sel[0:H1, h * P:h * P + P], neg_m[0:H1, :], start=True, stop=True) \
                    .then_inc(m_spread, 1)
                for j in range(TB):
                    at = (bank[1][:], bank[2][:, 0:384], bank[3][:, 0:256], bank[3][:, 256:384])[j]
                    mm = nc.tensor.matmul(at, qk[:, 4 + h, j * P:j * P + P], qk[:, h, j * P:], start=True, stop=True)
                mm.then_inc(s_ready, 1)
                if h:
                    pe.wait_ge(gated_root, h)
                for b in range(TB):
                    for g in range(2):
                        mm = nc.tensor.matmul(bank[7][64 * g:64 * g + 64, b * P:b * P + P],
                                              vg[:, b, h * P + 64 * g:h * P + 64 * g + 64],
                                              cols(par1, P1_COLS, "w_sp")[:, (2 * h + g) * P:(2 * h + g + 1) * P],
                                              start=True, stop=True)
                mm.then_inc(mix_ready, 1)
                pe.wait_ge(s_weighted, 3 * h + 3)
                if h:
                    pe.wait_ge(h_root, h)
                for j in range(TB):
                    nc.tensor.matmul(bank[4][:, j * P:], vm[:, j, h * P:h * P + P], dec[:, j, j * P:],
                                     start=j == 0, stop=j == TB - 1)
                for j in range(TB):
                    nc.tensor.matmul(bank[5][:, j * P:], ones, dec[:, j, j * P:], start=j == 0, stop=j == TB - 1)
                pe.wait_ge(em_ready, 1)
                nc.tensor.matmul(bank[0][:], sel[0:H1, h * P:h * P + P], e_neg_m[0:H1, :], start=True, stop=True) \
                    .then_inc(num_ready, 1)
                pe.wait_ge(gated_sq, h + 1)
                nc.tensor.matmul(bank[7][:], cols(con, C_COLS, "blocks64"), gm_b[:], start=True, stop=True) \
                    .then_inc(gated_ss, 1)
                pe.wait_ge(h_sq, h + 1)
                nc.tensor.matmul(bank[6][:], ones, ml_b[:], start=True, stop=True).then_inc(h_ss, 1)

            pe.wait_ge(y_lo_ready, 8)
            pe.wait_ge(h_root, H1)
            pe.wait_ge(gated_root, H1)
            for half in range(2):
                for part in range(2):
                    n = U_OUT + 2 * half + part
                    unit_wait(n)
                    for b in range(TB):
                        for k in range(4):
                            y = (4 * part + k, slice(b * P, b * P + P))
                            w = slice(k * 512, k * 512 + 512)
                            mm = product(bank[4 * half + b][:], u_hi[:, y[0], y[1]], u_lo[:, y[0], y[1]],
                                         w_hi[:, n % 2, w], w_lo[:, n % 2, w], part == 0 and k == 0,
                                         part == 1 and k == 3)
                    mm.then_inc(unit_used, 1)


            pe.wait_ge(xn_ready, TB)
            for c in range(KC):
                if c >= 4:
                    pe.wait_ge(u_lo_ready, KC + c - 3)
                for b in range(TB):
                    mm = nc.tensor.transpose(bank[c % 4][:, b * P:b * P + P], xn[:, b, c * P:c * P + P], ident)
                mm.then_inc(turned, 1)
            pe.wait_ge(narrow_hi, 2)
            pe.wait_ge(narrow_lo, 2)
            pe.wait_ge(u_hi_ready, 2 * KC)
            pe.wait_ge(u_lo_ready, 2 * KC)
            for b in range(TB):
                for k in range(KC):
                    mm = product(bank[4][:, b * 36:b * 36 + 36], u_hi[:, k, b * P:b * P + P], u_lo[:, k, b * P:b * P + P],
                                 wr_hi[:, k], wr_lo[:, k], k == 0, k == KC - 1)
            mm.then_inc(logits_ready, 1)
            pe.wait_ge(owns_ready, 1)
            for b in range(TB):
                for earlier in range(b):
                    nc.tensor.matmul(bank[5][:, b * NE:b * NE + NE], ones, both[:, earlier], start=earlier == 0, stop=False)
                nc.tensor.matmul(bank[5][:, b * NE:b * NE + NE], cols(con, C_COLS, "strict"), both[:, b],
                                 start=b == 0, stop=True)
            for b in range(TB):
                mm = nc.tensor.matmul(bank[5][:, TB * NE:TB * NE + NE], ones, both[:, b], start=b == 0, stop=b == TB - 1)
            mm.then_inc(before_ready, 1)

            def turn_rows(b):
                for c in range(KC):
                    mm = nc.tensor.transpose(bank[c // 4][:, (c % 4) * P:(c % 4) * P + P],
                                             x_rows[:, b, c * P:c * P + P], ident)
                mm.then_inc(xe_turned, 1)

            def up_units(s_of, wait, mark):
                for j in range(4):
                    wait(j)
                    s = s_of(j)
                    for k in range(4):
                        c = 4 * (j % 2) + k
                        w = slice(k * FE, k * FE + FE)
                        mm = product(bank[2 + j // 2][:], xe_hi[:, c], xe_lo[:, c], w_hi[:, s, w], w_lo[:, s, w],
                                     c == 0, c == KC - 1)
                    mm.then_inc(mark, 1)

            def turn_hidden():
                for c in range(4):
                    mm = nc.tensor.transpose(bank[4][:, c * P:c * P + P], hid[:, c * P:c * P + P], ident)
                mm.then_inc(hid_turned, 1)

            def down_units(s_of, wait, mark):
                for j in range(2):
                    wait(4 + j)
                    s = s_of(4 + j)
                    for k in range(2):
                        c = 2 * j + k
                        for half in range(2):
                            w = slice(k * D + half * 512, k * D + half * 512 + 512)
                            mm = product(bank[5 + half][:], hid_hi[:, c], hid_lo[:, c], w_hi[:, s, w], w_lo[:, s, w],
                                         c == 0, c == 3)
                    mm.then_inc(mark, 1)

            pe.wait_ge(dest_ready, 1)
            pe.wait_ge(x_gathered[0], 16)
            turn_rows(0)
            with pe.Fori(0, NE // 2) as i:
                for b in range(2):
                    n0 = U_MOE + PER_EXPERT * b
                    e = i * 2 + b

                    def wait(j):
                        pe.wait_ge(hi_ready, i * (2 * PER_EXPERT) + (n0 + j + 1))
                        pe.wait_ge(lo_ready, i * (2 * PER_EXPERT) + (n0 + j + 1))

                    pe.wait_ge(xe_hi_ready, e + 1)
                    pe.wait_ge(xe_lo_ready, e + 1)
                    up_units(lambda j: j % 2, wait, unit_used)
                    pe.wait_ge(x_gathered[1 - b], i * 16 + 16 * (b + 1))
                    turn_rows(1 - b)
                    pe.wait_ge(hid_ready, e + 1)
                    turn_hidden()
                    pe.wait_ge(hid_hi_ready, e + 1)
                    pe.wait_ge(hid_lo_ready, e + 1)
                    down_units(lambda j: j % 2, wait, unit_used)

            with pe.If(overflowing(pe)):
                with pe.Fori(0, N_OVER) as v:
                    pe.wait_ge(over_x, v * 16 + 16)
                    for c in range(KC):
                        mm = nc.tensor.transpose(bank[c // 4][:, (c % 4) * P:(c % 4) * P + P],
                                                 x_rows[:, 0, c * P:c * P + P], ident)
                    mm.then_inc(over_products, 1)
                    pe.wait_ge(over_w, v * 32 + 16)
                    pe.wait_ge(over_copies, v * 4 + 1)
                    for j in range(4):
                        for k in range(4):
                            c = 4 * (j % 2) + k
                            mm = nc.tensor.matmul(bank[2 + j // 2][:], over_xe[:, c], over_weights[:, j, k * FE:k * FE + FE],
                                                  start=c == 0, stop=c == KC - 1)
                    mm.then_inc(over_products, 1)
                    pe.wait_ge(over_hid, v + 1)
                    for c in range(4):
                        mm = nc.tensor.transpose(bank[4][:, c * P:c * P + P], hid[:, c * P:c * P + P], ident)
                    mm.then_inc(over_products, 1)
                    pe.wait_ge(over_w, v * 32 + 32)
                    pe.wait_ge(over_copies, v * 4 + 3)
                    for c in range(4):
                        for half in range(2):
                            w = (c % 2) * D + half * 512
                            mm = nc.tensor.matmul(bank[5 + half][:], over_hidt[:, c], over_weights[:, c // 2, w:w + 512],
                                                  start=c == 0, stop=c == 3)
                    mm.then_inc(over_products, 1)
            pe.wait_ge(xn_ready, 2 * TB)
            for c in range(KC):
                if c >= 4:
                    pe.wait_ge(h0_ready, c - 3)
                for b in range(TB):
                    mm = nc.tensor.transpose(bank[c % 4][:, b * P:b * P + P], xn[:, b, c * P:c * P + P], ident)
                mm.then_inc(h_turned, 1)


            def norm(k):
                at = norm_bank(k)
                for c in range(KC):
                    pe.wait_ge(n_sq, KC * k + c + 1)
                    nc.tensor.matmul(at[:], ones, sq[c % 2][:], start=c == 0, stop=c == KC - 1).then_inc(n_sum, 1)

            def normed(k):
                pe.wait_ge(u_hi_ready, (2 + k) * KC + KC)
                pe.wait_ge(u_lo_ready, (2 + k) * KC + KC)

            def out_rows(n0, n_chunks, src_hi, src_lo):
                for half in range(2):
                    for q in range(-(-n_chunks // 4)):
                        n = n0 + half * -(-n_chunks // 4) + q
                        unit_wait(n)
                        for d in range(4):
                            for k in range(min(4, n_chunks - 4 * q)):
                                c = 4 * q + k
                                w = slice(k * 512 + d * P, k * 512 + d * P + P)
                                mm = product(bank[4 * half + d][:], w_hi[:, n % 2, w], w_lo[:, n % 2, w], src_hi[:, c],
                                             src_lo[:, c], c == 0, c == n_chunks - 1)
                        mm.then_inc(unit_used, 1)

            norm(0)
            normed(0)
            pe.wait_ge(set_up, 5)
            with pe.Fori(0, HH // 2) as p:
                for j in range(4):
                    pe.wait_ge(hi_ready, p * 4 + (U_HG + j + 1))
                    pe.wait_ge(lo_ready, p * 4 + (U_HG + j + 1))
                    if j == 2:
                        pe.wait_ge(f_ready, p * 2 + 2)
                    if j == 3:
                        pe.wait_ge(q_taken, p * 2 + 2)
                    for half in range(2):
                        out_bank = bank[(2 * j + half) % 4]
                        if j == 2:
                            for b in range(2):
                                tokens = slice((2 * half + b) * P, (2 * half + b) * P + P)
                                mm = token_chunk(out_bank[:, b * 256:b * 256 + 256], j % 2, tokens)
                        else:
                            mm = feature_chunk(out_bank[:], j % 2, half)
                        mm.then_inc(proj_ready if half == 0 else unit_used, 1)
                for hh in range(2):
                    for n in range(8):
                        if n < 7:
                            pe.wait_ge(k_ready, p * 14 + (7 * hh + n + 1))
                            pe.wait_ge(q_ready, p * 14 + (7 * hh + n + 1))
                        if n >= 2:
                            pe.wait_ge(lev_taken, p * 16 + (8 * hh + n - 1))
                        for b in range(TB):
                            t = slice(b * P, b * P + P)
                            left, right = (k_dec[n % 2][:, t], q_dec[n % 2][:, t]) if n < 7 else (key[:, hh, t], qry[:, hh, t])
                            mm = nc.tensor.matmul(bank[4 + n % 2][:, t], left, right, start=True, stop=True)
                        mm.then_inc(lev_ready, 1)
                    pe.wait_ge(far_kq, p * 2 + (hh + 1))
                    k_far, q_far = k_dec[0], q_dec[0]
                    nc.tensor.matmul(bank[6][:, 0:128], k_far[:, 0:128], q_far[:, 0:128], start=True, stop=True)
                    nc.tensor.matmul(bank[6][:, 128:384], k_far[:, 384:512], q_far[:, 128:384], start=True, stop=True)
                    nc.tensor.matmul(bank[7][:, 0:256], k_far[:, 128:256], q_far[:, 128:384], start=True, stop=True)
                    nc.tensor.matmul(bank[7][:, 256:384], k_far[:, 256:384], q_far[:, 384:512], start=True, stop=True) \
                        .then_inc(far_ready, 1)
                    pe.wait_ge(lev_taken, p * 16 + (8 * hh + 8))
                    pe.wait_ge(far_taken, p * 2 + (hh + 1))
                    if hh == 0:
                        pe.wait_ge(v_taken, p * 2 + 2)
                    for b in range(TB):
                        mm = nc.tensor.matmul(bank[6][:, b * P:], val[:, b, hh * P:hh * P + P], ws[:, b, 0:T - b * P],
                                              start=b == 0, stop=b == TB - 1)
                    mm.then_inc(o_sum, 1)
                    pe.wait_ge(o_sq, p * 2 + (hh + 1))
                    nc.tensor.matmul(bank[7][:], ones, fx[:, 0], start=True, stop=True).then_inc(o_ss, 1)
            pe.wait_ge(o_hi_ready, HH)
            pe.wait_ge(o_lo_ready, HH)
            out_rows(U_HGO, HH, o_hi, o_lo)

            def ffn(l, u0):
                norm(1 + 2 * l)
                normed(1 + 2 * l)

                def unit(n, done, i=None):
                    def at(v):
                        return v if i is None else i * 4 + v
                    s = n % 2
                    pe.wait_ge(hi_ready, at(n + 1))
                    pe.wait_ge(lo_ready, at(n + 1))
                    if not (l == 0 and done < 2 and i is None):
                        pe.wait_ge(f_prod, at(done - 1))
                    feature_chunk(bank[2 * s][:], s, 0).then_inc(proj_ready, 1)
                    feature_chunk(bank[2 * s + 1][:], s, 1).then_inc(unit_used, 1)

                base = l * FC
                pe.wait_ge(h_added, 8 + 24 * l)
                for j in range(4):
                    unit(u0 + j, base + j)
                with pe.Fori(1, FA // 4) as i:
                    for j in range(4):
                        unit(u0 + j, base + j, i)
                pe.wait_ge(f_hi, base + FA)
                pe.wait_ge(f_lo, base + FA)
                out_rows(u0 + FA, FA, hid2_hi, hid2_lo)
                pe.wait_ge(h_added, 16 + 24 * l)
                u1 = u0 + FA + 6
                with pe.Fori(0, 2) as i:
                    for j in range(4):
                        unit(u1 + j, base + FA + j, i)
                for j in range(8, FC - FA):
                    unit(u1 + j, base + FA + j)
                pe.wait_ge(f_hi, base + FC)
                pe.wait_ge(f_lo, base + FC)
                out_rows(u1 + FC - FA, FC - FA, hid2_hi, hid2_lo)

            ffn(0, U_FF0)

            norm(2)
            normed(2)
            pe.wait_ge(h_added, 24)

            def tokens_of(tile, k, g, b):
                if g == 0:
                    return tile[:, k, b * P:b * P + P]
                return tile[:, k].rearrange("q (p r) -> q r p", r=STEP[g])[:, b]

            for g in range(3):
                for half in range(2):
                    n = U_QKV + 6 * g + half
                    unit_wait(n)
                    if g or half:
                        pe.wait_ge(v_ready, 2 * (2 * g + half))
                    if g:
                        pe.wait_ge(rope_mul, 8 * g)
                    for b in range(TB):
                        for k in range(KC):
                            w = slice(k * 256, k * 256 + 256)
                            mm = product(bank[b // 2][:, b % 2 * 256:b % 2 * 256 + 256], tokens_of(u_hi, k, g, b),
                                         tokens_of(u_lo, k, g, b), w_hi[:, n % 2, w], w_lo[:, n % 2, w], k == 0, k == KC - 1)
                    mm.then_inc(unit_used, 1)
                for pair in range(2):
                    first_chunk = 8 * g + 4 * pair
                    for kind in range(2):
                        n = U_QKV + 6 * g + 2 + 2 * pair + kind
                        unit_wait(n)
                        if kind == 0:
                            pe.wait_ge(v_ready, 4 * (g + 1))
                        if first_chunk:
                            pe.wait_ge(rope_mul, first_chunk - 2 + 2 * kind)
                        feature_chunk(bank[2 * kind][:], n % 2, 0).then_inc(proj_ready, 1)
                        feature_chunk(bank[2 * kind + 1][:], n % 2, 1).then_inc(unit_used, 1)
                    for half in range(2):
                        m = AH * g + 2 * pair + half
                        pe.wait_ge(rope_ready, first_chunk + 4)
                        if m >= 2:
                            pe.wait_ge(sc_max, m - 1)
                        at = 4 + 2 * (m % 2)
                        for b in range(TB):
                            q = q_rot[half][:, b * P:b * P + P]
                            if g == 0:
                                s0 = max(b - 1, 0) * P
                                mm = nc.tensor.matmul(bank[at + b // 2][:, b % 2 * 256:b % 2 * 256 + 256], q,
                                                      k_rot[half][:, s0:s0 + 256], start=True, stop=True)
                            else:
                                mm = nc.tensor.matmul(bank[at][:, b * P:b * P + P], q, k_rot[half][:, b * P:b * P + P],
                                                      start=True, stop=True)
                        mm.then_inc(sc_ready, 1)
            pe.wait_ge(sc_max, 3 * AH)
            for m in range(3 * AH):
                g, h = m // AH, m % AH
                at = 4 * (m % 2)
                pe.wait_ge(p_ready, m + 1)
                if m >= 2:
                    pe.wait_ge(ao_lo_ready, m - 1)
                pr = prob_of(g, h)
                tiles = [(b, s) for b in range(TB) for s in range(2 if g == 0 and b else 1)]
                for n, (b, s) in enumerate(tiles):
                    mm = nc.tensor.transpose(bank[at + n // 4][:, n % 4 * P:n % 4 * P + P], pr[:, b, s * P:s * P + P], ident)
                mm.then_inc(p_turned, 1)
                pe.wait_ge(pt_ready, m + 1)
                flat = pr.rearrange("p b s -> p (b s)")
                for n, (b, s) in enumerate(tiles):
                    from_block = b - 1 + s if g == 0 and b else b
                    mm = nc.tensor.matmul(bank[at + 2][:, b * P:b * P + P], vals[:, g, from_block, h * P:h * P + P],
                                          flat[:, n * P:n * P + P], start=s == 0, stop=s == 1 or not (g == 0 and b))
                mm.then_inc(ao_sum, 1)
            pe.wait_ge(ao_hi_ready, 3 * AH)
            pe.wait_ge(ao_lo_ready, 3 * AH)
            out_rows(U_AO, 3 * AH, ao_hi, ao_lo)

            ffn(1, U_FF1)
            pe.wait_ge(h_added, 48)
            for b in range(TB):
                for c in range(KC):
                    mm = nc.tensor.transpose(bank[2 * b + c // 4][:, c % 4 * P:c % 4 * P + P], hs[:, c, b * P:b * P + P], ident)
                mm.then_inc(fin_turned, 1)

        @block.scalar
        def _(act):
            steps = Count(act_step)

            def chain(instruction):
                act.wait_ge(act_step, steps.mark(instruction))

            def split(n):
                act.wait_ge(raw_landed[n % RAW], 16 * (n // RAW + 1))
                if n >= 2:
                    act.wait_ge(unit_used, n - 1)
                nc.scalar.activation(w_hi[:, n % 2], raw[:, n % RAW], ACT.Copy).then_inc(hi_ready, 1)

            act.wait_ge(x_landed, 16)
            for b in range(TB):
                if b:
                    act.wait_ge(sq_ready, b)
                nc.scalar.activation(junk[:], res[:, b], ACT.Square, accum_out=small[:, 0, b:b + 1]).then_inc(sq_ready, 1)
            act.wait_ge(rms_arg, 1)
            nc.scalar.activation(small[:, 2], small[:, 1], ACT.Sqrt).then_inc(root_ready, 1)
            act.wait_ge(con_landed, 32)
            nc.scalar.activation(wif_hi[:], cols(par1, P1_COLS, "w_if").rearrange("p (k c) -> p k c", k=KC), ACT.Copy) \
                .then_inc(narrow_hi, 1)
            split(0)
            for c in range(KC):
                act.wait_ge(turned, c + 1)
                nc.scalar.activation(u_hi[:, c], bank[c % 4][:], ACT.Copy,
                                     scale=cols(par1, P1_COLS, "n1g")[:, c:c + 1]).then_inc(u_hi_ready, 1)

            for n in range(N_IN):
                split(n + 1)
                for half in range(2):
                    q = 2 * n + half
                    ready = (in_ready, n + 1) if half == 0 else (unit_used, n + 1)
                    if q < 8:
                        act.wait_ge(in_conv, q + 1)
                        nc.scalar.activation(qk[:, q], qk[:, q], ACT.Silu).then_inc(qk_ready, 1)
                        continue
                    act.wait_ge(*ready)
                    if n in (4, 5):
                        dst = vg[:, 2 * half:2 * half + 2, (n - 4) * 256:(n - 4) * 256 + 256]
                        src, f = bank[q % 4][:].rearrange("p (b c) -> p b c", b=2), ACT.Gelu_apprx_tanh
                    elif n in (6, 7):
                        dst, src, f = ug[:, q - 12], bank[q % 4][:], ACT.Gelu_apprx_tanh
                    elif n in (8, 9):
                        dst, src, f = so[:, q - 16], bank[q % 4][:], ACT.Sigmoid
                    else:
                        dst = vm[:, 2 * half:2 * half + 2, (n - 10) * 256:(n - 10) * 256 + 256]
                        src, f = bank[q % 4][:].rearrange("p (b c) -> p b c", b=2), ACT.Copy
                    nc.scalar.activation(dst, src, f).then_inc(in_act, 1)
                if n == 1:
                    act.wait_ge(soft_arg, 1)
                    chain(nc.scalar.activation(r_e[0:H1, :], r_e[0:H1, :], ACT.Exp))
                    nc.scalar.activation(r_e[0:H1, :], r_e[0:H1, :], ACT.Ln, bias=1.0).then_inc(soft_log, 1)
                if n == 3:
                    act.wait_ge(rows_ready, 1)
                    nc.scalar.activation(e_neg_m[0:H1, :], e_neg_m[0:H1, :], ACT.Exp, scale=-1.0).then_inc(em_ready, 1)
                if n == 5:
                    act.wait_ge(in_act, 4)
                    for b in range(TB):
                        if b:
                            act.wait_ge(sq_ready, TB + b)
                        nc.scalar.activation(y_tmp[:], vg[:, b], ACT.Square, accum_out=small[:, 4, b:b + 1]) \
                            .then_inc(sq_ready, 1)
                if n == 7:
                    act.wait_ge(rms_arg, 2)
                    nc.scalar.activation(small[:, 6], small[:, 5], ACT.Sqrt).then_inc(root_ready, 1)

            for h in range(H1):
                act.wait_ge(dec_arg, 4 * h + 4)
                for j in range(TB):
                    last = nc.scalar.activation(dec[:, j, j * P:], dec[:, j, j * P:], ACT.Exp)
                last.then_inc(dec_ready, 1)
                act.wait_ge(gated_ready, h + 1)
                nc.scalar.activation(gm_b[:], gm_a[:], ACT.Square).then_inc(gated_sq, 1)
                act.wait_ge(num_ready, h + 1)
                nc.scalar.activation(ml_a[:], bank[5][:], ACT.Abs).then_inc(nq_abs, 1)
                act.wait_ge(gated_ss, h + 1)
                nc.scalar.activation(gm_b[:], bank[7][:], ACT.Sqrt, scale=1.0 / 64, bias=eps).then_inc(gated_root, 1)
                act.wait_ge(h_ready, h + 1)
                nc.scalar.activation(ml_b[:], ml_a[:], ACT.Square).then_inc(h_sq, 1)
                act.wait_ge(yg_ready, h + 1)
                nc.scalar.activation(u_hi[:, 4 + h], gm_a[:], ACT.Copy).then_inc(yg_hi, 1)
                act.wait_ge(h_ss, h + 1)
                nc.scalar.activation(ml_b[:], bank[6][:], ACT.Sqrt, scale=1.0 / P, bias=eps).then_inc(h_root, 1)
                act.wait_ge(ym_ready, h + 1)
                nc.scalar.activation(u_hi[:, h], ml_a[:], ACT.Copy).then_inc(ym_hi, 1)
            for n in range(U_OUT, U_OUT + N_OUT):
                if n + 1 < STREAM_END:
                    split(n + 1)


            for b in range(TB):
                act.wait_ge(res1_ready, TB + b + 1)
                if b:
                    act.wait_ge(sq_ready, 2 * TB + b)
                nc.scalar.activation(y_rows[:, 0], res[:, b], ACT.Square, accum_out=rms2[:, 0, b:b + 1]).then_inc(sq_ready, 1)
            act.wait_ge(rms_arg, 3)
            nc.scalar.activation(rms2[:, 2], rms2[:, 1], ACT.Sqrt).then_inc(root_ready, 1)
            act.wait_ge(params_landed, 16)
            nc.scalar.activation(wr_hi[:], cols(par2, P2_COLS, "w_r").rearrange("p (k c) -> p k c", k=KC), ACT.Copy) \
                .then_inc(narrow_hi, 1)
            for c in range(KC):
                act.wait_ge(turned, KC + c + 1)
                nc.scalar.activation(u_hi[:, c], bank[c % 4][:], ACT.Copy).then_inc(u_hi_ready, 1)
            act.wait_ge(router_arg, 1)
            nc.scalar.activation(gap[:], gap[:], ACT.Exp).then_inc(router_exp, 1)
            act.wait_ge(router_arg, 2)
            nc.scalar.activation(best[:, 5], best[:, 4], ACT.Exp).then_inc(router_exp, 1)

            def expert_tokens():
                nc.scalar.activation(xe_hi[:, 0:4], bank[0][:].rearrange("p (c t) -> p c t", c=4), ACT.Copy)
                nc.scalar.activation(xe_hi[:, 4:8], bank[1][:].rearrange("p (c t) -> p c t", c=4), ACT.Copy) \
                    .then_inc(xe_hi_ready, 1)

            act.wait_ge(xe_turned, 1)
            expert_tokens()
            with act.Fori(0, NE // 2) as i:
                for b in range(2):
                    e = i * 2 + b
                    u0 = i * (2 * PER_EXPERT) + (U_MOE + PER_EXPERT * b)

                    def split_at(j):
                        c = PER_EXPERT * b + j
                        act.wait_ge(raw_landed[c % RAW], i * (16 * 2 * PER_EXPERT // RAW) + 16 * ((U_MOE + c) // RAW + 1))
                        act.wait_ge(unit_used, i * (2 * PER_EXPERT) + (U_MOE + c - 1))
                        nc.scalar.activation(w_hi[:, j % 2], raw[:, c % RAW], ACT.Copy).then_inc(hi_ready, 1)

                    split_at(1)
                    split_at(2)
                    split_at(3)
                    act.wait_ge(unit_used, u0 + 2)
                    nc.scalar.activation(gate[:], bank[2][:], ACT.Silu).then_inc(silu_ready, 1)
                    split_at(4)
                    act.wait_ge(xe_turned, e + 2)
                    expert_tokens()
                    split_at(5)
                    act.wait_ge(hid_turned, e + 1)
                    nc.scalar.activation(hid_hi[:], bank[4][:].rearrange("p (c t) -> p c t", c=4), ACT.Copy) \
                        .then_inc(hid_hi_ready, 1)
                    split_at(6)
                    act.wait_ge(y_free[b], i * 16 + 16)
                    act.wait_ge(unit_used, u0 + 6)
                    nc.scalar.activation(y_rows[:, b, 0:512], bank[5][:], ACT.Copy).then_inc(y_act, 1)

            with act.If(overflowing(act)):
                with act.Fori(0, N_OVER) as v:
                    act.wait_ge(over_products, v * 4 + 1)
                    nc.scalar.activation(over_xe[:, 0:4], bank[0][:].rearrange("p (c t) -> p c t", c=4), ACT.Copy)
                    nc.scalar.activation(over_xe[:, 4:8], bank[1][:].rearrange("p (c t) -> p c t", c=4), ACT.Copy) \
                        .then_inc(over_copies, 1)
                    act.wait_ge(over_products, v * 4 + 2)
                    nc.scalar.activation(gate[:], bank[2][:], ACT.Silu).then_inc(over_copies, 1)
                    act.wait_ge(over_products, v * 4 + 3)
                    nc.scalar.activation(over_hidt[:], bank[4][:].rearrange("p (c t) -> p c t", c=4), ACT.Copy) \
                        .then_inc(over_copies, 1)
                    act.wait_ge(over_products, v * 4 + 4)
                    nc.scalar.activation(y_rows[:, 0, 0:512], bank[5][:], ACT.Copy)
                    nc.scalar.activation(y_rows[:, 0, 512:1024], bank[6][:], ACT.Copy).then_inc(over_copies, 1)
            for b in range(TB):
                act.wait_ge(res2_ready, b + 1)
                if b:
                    act.wait_ge(sq_ready, 3 * TB + b)
                nc.scalar.activation(x_rows[:, 0], res[:, b], ACT.Square, accum_out=rms2[:, 4, b:b + 1]).then_inc(sq_ready, 1)
            act.wait_ge(rms_arg, 4)
            nc.scalar.activation(rms2[:, 6], rms2[:, 5], ACT.Sqrt).then_inc(root_ready, 1)


            def norm(k, wait_chunk):
                for c in range(KC):
                    wait_chunk(c)
                    if c >= 2:
                        act.wait_ge(n_sum, KC * k + c - 1)
                    nc.scalar.activation(sq[c % 2][:], hs[:, c], ACT.Square).then_inc(n_sq, 1)
                act.wait_ge(n_sum, KC * k + KC)
                nc.scalar.activation(rms[:], norm_bank(k)[:], ACT.Sqrt, scale=1.0 / D, bias=eps).then_inc(n_root, 1)
                for c in range(KC):
                    act.wait_ge(u_ready, KC * k + c + 1)
                    nc.scalar.activation(u_hi[:, c], u_tmp[:], ACT.Copy).then_inc(u_hi_ready, 1)

            def split_trip(n, i, per):
                act.wait_ge(raw_landed[n % RAW], i * (16 * per // RAW) + 16 * (n // RAW + 1))
                act.wait_ge(unit_used, i * per + (n - 1))
                nc.scalar.activation(w_hi[:, n % 2], raw[:, n % RAW], ACT.Copy).then_inc(hi_ready, 1)

            norm(0, lambda c: act.wait_ge(h0_ready, c + 1))
            act.wait_ge(lb_arg, 1)
            nc.scalar.activation(lb_tile, lb_tile, ACT.Exp).then_inc(lb_exp, 1)

            with act.Fori(0, HH // 2) as p:
                split_trip(U_HG + 1, p, 4)
                act.wait_ge(lo_ready, p * 4 + (U_HG + 2))
                act.wait_ge(proj_ready, p * 4 + 1)
                nc.scalar.activation(fx[:, 0], bank[0][:], ACT.Sigmoid).then_inc(f_sig, 1)
                act.wait_ge(unit_used, p * 4 + (U_HG + 1))
                nc.scalar.activation(fx[:, 1], bank[1][:], ACT.Sigmoid).then_inc(f_sig, 1)
                split_trip(U_HG + 2, p, 4)
                for hh in range(2):
                    act.wait_ge(f_ready, p * 2 + (hh + 1))
                    nc.scalar.activation(fx[:, hh], fx[:, hh], ACT.Ln).then_inc(f_log, 1)
                act.wait_ge(unit_used, p * 4 + (U_HG + 2))
                for hh in range(2):
                    nc.scalar.activation(qry[:, hh], bank[2 + hh][:], ACT.Silu).then_inc(q_taken, 1)
                split_trip(U_HG + 3, p, 4)
                act.wait_ge(unit_used, p * 4 + (U_HG + 3))
                for hh in range(2):
                    nc.scalar.activation(val[:, 2 * hh:2 * hh + 2], bank[hh][:].rearrange("p (b c) -> p b c", b=2), ACT.Copy) \
                        .then_inc(v_taken, 1)
                split_trip(U_HG + 4, p, 4)
                act.wait_ge(unit_used, p * 4 + (U_HG + 4))
                for hh in range(2):
                    nc.scalar.activation(sg[:, hh], bank[2 + hh][:], ACT.Silu).then_inc(g_taken, 1)
                for hh in range(2):
                    for n in range(7):
                        act.wait_ge(gap_to_ref, p * 14 + (7 * hh + n + 1))
                        nc.scalar.activation(fx[:, n % 2], fx[:, n % 2], ACT.Exp).then_inc(lev_exp, 1)
                    act.wait_ge(k_ready, p * 14 + (7 * hh + 7))
                    act.wait_ge(q_ready, p * 14 + (7 * hh + 7))
                    nc.scalar.activation(fx[:, 0, 0:384], run[:, hh, 128:512], ACT.Exp)
                    for b in range(3):
                        end = run[:, hh, b * P + P - 1:b * P + P]
                        nc.scalar.activation(fx[:, 1, b * P:b * P + P], run[:, hh, b * P:b * P + P], ACT.Exp, bias=end, scale=-1.0)
                    nc.scalar.activation(b_exp[:], run[:, hh, 255:384:128], ACT.Exp).then_inc(far_exp, 1)
                    act.wait_ge(far_ready, p * 2 + (hh + 1))
                    nc.scalar.activation(ws[:, 0, 128:512], bank[6][:, 0:384], ACT.Copy)
                    nc.scalar.activation(ws[:, 1, 128:384], bank[7][:, 0:256], ACT.Copy)
                    nc.scalar.activation(ws[:, 2, 128:256], bank[7][:, 256:384], ACT.Copy).then_inc(far_taken, 1)
                    act.wait_ge(o_sum, p * 2 + (hh + 1))
                    nc.scalar.activation(fx[:, 0], bank[6][:], ACT.Square).then_inc(o_sq, 1)
                    act.wait_ge(o_ss, p * 2 + (hh + 1))
                    nc.scalar.activation(fx[:, 1], bank[7][:], ACT.Sqrt, scale=1.0 / P, bias=eps).then_inc(o_root, 1)
                    act.wait_ge(o_ready, p * 2 + (hh + 1))
                    nc.scalar.activation(o_hi[:, bass.ds(p * 2 + hh, 1)].rearrange("p h t -> p (h t)"), fx[:, 0], ACT.Copy) \
                        .then_inc(o_hi_ready, 1)
            for n in range(U_HGO, U_HGO + 4):
                split(n + 1)

            def ffn(l, u0):
                base = l * FC
                norm(1 + 2 * l, lambda c: act.wait_ge(h_added, 24 * l + c + 1))

                def unit(n, chunk, slot, i=None):
                    def at(v):
                        return v if i is None else i * 4 + v
                    if i is None:
                        split(n + 1)
                    else:
                        split_trip(n + 1, i, 4)
                    s = n % 2
                    act.wait_ge(unit_used, at(n + 1))
                    nc.scalar.activation(f_gate[s][:], bank[2 * s][:], ACT.Silu).then_inc(f_silu, 1)
                    act.wait_ge(f_prod, at(chunk + 1))
                    dst = hid2_hi[:, slot] if i is None else hid2_hi[:, bass.ds(i * 4 + slot, 1)].rearrange("p c t -> p (c t)")
                    nc.scalar.activation(dst, f_hid[s][:], ACT.Copy).then_inc(f_hi, 1)

                with act.Fori(0, FA // 4) as i:
                    for j in range(4):
                        unit(u0 + j, base + j, j, i)
                for n in range(u0 + FA, u0 + FA + 6):
                    split(n + 1)
                u1 = u0 + FA + 6
                with act.Fori(0, 2) as i:
                    for j in range(4):
                        unit(u1 + j, base + FA + j, j, i)
                for j in range(8, FC - FA):
                    unit(u1 + j, base + FA + j, j)
                for n in range(u1 + FC - FA, u1 + FC - FA + 6):
                    if n + 1 < N_UNITS:
                        split(n + 1)

            ffn(0, U_FF0)

            norm(2, lambda c: act.wait_ge(h_added, 16 + c + 1))
            for g in range(3):
                for half in range(2):
                    n = U_QKV + 6 * g + half
                    split(n + 1)
                    act.wait_ge(unit_used, n + 1)
                    for b in range(2):
                        nc.scalar.activation(vals[:, g, 2 * b:2 * b + 2, half * 256:half * 256 + 256],
                                             bank[b][:].rearrange("p (b c) -> p b c", b=2), ACT.Copy).then_inc(v_ready, 1)
                for pair in range(2):
                    for kind in range(2):
                        split(U_QKV + 6 * g + 2 + 2 * pair + kind + 1)
                    for half in range(2):
                        m = AH * g + 2 * pair + half
                        act.wait_ge(sc_gap, m + 1)
                        pr = prob_of(g, 2 * pair + half)
                        nc.scalar.activation(pr, pr, ACT.Exp, scale=DH_SCALE).then_inc(sc_exp, 1)
            act.wait_ge(share_arg, 1)
            for g in range(3):
                last = nc.scalar.activation(share[:, g], share[:, g], ACT.Exp, scale=DH_SCALE)
            last.then_inc(share_exp, 1)
            for m in range(3 * AH):
                g, h = m // AH, m % AH
                at = 4 * (m % 2)
                act.wait_ge(p_turned, m + 1)
                flat = prob_of(g, h).rearrange("p b s -> p (b s)")
                last = nc.scalar.activation(flat[:, 0:T], bank[at][:], ACT.Copy)
                if g == 0:
                    last = nc.scalar.activation(flat[:, T:T + 384], bank[at + 1][:, 0:384], ACT.Copy)
                last.then_inc(pt_ready, 1)
                act.wait_ge(ao_sum, m + 1)
                nc.scalar.activation(natural_order(ao_hi[:, m], g), group_order(bank[at + 2][:], g), ACT.Copy) \
                    .then_inc(ao_hi_ready, 1)
            for n in range(U_AO, U_AO + 6):
                split(n + 1)

            ffn(1, U_FF1)
            for b in range(TB):
                act.wait_ge(fin_turned, b + 1)
                for half in range(2):
                    if b or half:
                        act.wait_ge(sq_ready, 4 * TB + 2 * b + half)
                    nc.scalar.activation(out_sq[:], bank[2 * b + half][:], ACT.Square,
                                         accum_out=out_rms[:, half, b:b + 1]).then_inc(sq_ready, 1)
            act.wait_ge(rms_arg, 5)
            nc.scalar.activation(out_rms[:, 4], out_rms[:, 3], ACT.Sqrt).then_inc(root_ready, 1)

        @block.vector
        def _(dve):
            steps = Count(dve_step)

            def chain(instruction):
                dve.wait_ge(dve_step, steps.mark(instruction))

            def split(n):
                dve.wait_ge(hi_ready, n + 1)
                nc.vector.tensor_tensor(w_lo[:, n % 2], raw[:, n % RAW], w_hi[:, n % 2].bitcast(F32), ALU.subtract) \
                    .then_inc(lo_ready, 1)

            dve.wait_ge(sq_ready, TB)
            nc.vector.tensor_scalar(small[:, 1], small[:, 0], 1.0 / D, EPS, ALU.mult, ALU.add).then_inc(rms_arg, 1)
            dve.wait_ge(root_ready, 1)
            chain(nc.vector.reciprocal(small[:, 3], small[:, 2]))
            for b in range(TB):
                nc.vector.tensor_scalar(xs[:, b], res[:, b], small[:, 3, b:b + 1], None, ALU.mult).then_inc(xs_ready, 1)
            dve.wait_ge(narrow_hi, 1)
            nc.vector.tensor_tensor(wif_lo[:], cols(par1, P1_COLS, "w_if").rearrange("p (k c) -> p k c", k=KC),
                                    wif_hi[:].bitcast(F32), ALU.subtract).then_inc(narrow_lo, 1)
            split(0)
            for c in range(KC):
                dve.wait_ge(u_hi_ready, c + 1)
                nc.vector.scalar_tensor_tensor(u_lo[:, c], bank[c % 4][:], cols(par1, P1_COLS, "n1g")[:, c:c + 1],
                                               u_hi[:, c].bitcast(F32), ALU.mult, ALU.subtract).then_inc(u_lo_ready, 1)
            nc.vector.tensor_tensor(cols(par1, P1_COLS, "w_sp").rearrange("p (g t) -> p g t", g=NG),
                                    cols(par1, P1_COLS, "w_sp").rearrange("p (g t) -> p g t", g=NG),
                                    cols(con, C_COLS, "upper").unsqueeze(1).to_broadcast([P, NG, P]), ALU.mult) \
                .then_inc(wsp_ready, 1)

            def gate_rows_first():
                dve.wait_ge(gates_ready, 1)
                chain(nc.vector.tensor_scalar(r_f[0:H1, :], bank[4][32:36, :], cols(par1, P1_COLS, "b_f")[32:36], None,
                                              ALU.add))
                nc.vector.tensor_scalar(r_i[0:H1, :], bank[4][0:H1, :], cols(par1, P1_COLS, "b_i")[0:H1], None, ALU.add)
                nc.vector.scalar_tensor_tensor(r_e[0:H1, :], r_f[0:H1, :], -1.0, r_f[0:H1, :], ALU.mult, ALU.min) \
                    .then_inc(soft_arg, 1)

            def gate_rows_second():
                one = cols(par1, P1_COLS, "one_row")[0:H1]
                dve.wait_ge(soft_log, 1)
                chain(nc.vector.scalar_tensor_tensor(r_f[0:H1, :], r_f[0:H1, :], 0.0, r_e[0:H1, :], ALU.min, ALU.subtract))
                chain(nc.vector.tensor_tensor_scan(r_sum[0:H1, :], one, r_f[0:H1, :], 0.0, ALU.mult, ALU.add))
                chain(nc.vector.tensor_tensor(r_i[0:H1, :], r_i[0:H1, :], r_sum[0:H1, :], ALU.subtract))
                chain(nc.vector.tensor_tensor_scan(neg_m[0:H1, :], one, r_i[0:H1, :], 0.0, ALU.mult, ALU.max))
                chain(nc.vector.tensor_tensor(e_neg_m[0:H1, :], r_sum[0:H1, :], neg_m[0:H1, :], ALU.add))
                nc.vector.tensor_scalar(neg_m[0:H1, :], neg_m[0:H1, :], -1.0, None, ALU.mult).then_inc(rows_ready, 1)

            for n in range(N_IN):
                split(n + 1)
                for half in range(2):
                    q = 2 * n + half
                    if q >= 8:
                        continue
                    dve.wait_ge(in_ready if half == 0 else unit_used, n + 1)
                    src = bank[q % 4]
                    tap = [cols(par1, P1_COLS, "conv")[:, i * KC + q:i * KC + q + 1] for i in range(4)]
                    chain(nc.vector.tensor_scalar(qk[:, q], src[:], tap[3], None, ALU.mult))
                    for back in (1, 2, 3):
                        last = nc.vector.scalar_tensor_tensor(qk[:, q, back:], src[:, 0:T - back], tap[3 - back],
                                                              qk[:, q, back:], ALU.mult, ALU.add)
                        if back < 3:
                            chain(last)
                    last.then_inc(in_conv, 1)
                if n == 0:
                    gate_rows_first()
                if n == 2:
                    gate_rows_second()
                if n == 6:
                    dve.wait_ge(sq_ready, 2 * TB)
                    nc.vector.tensor_scalar(small[:, 5], small[:, 4], 1.0 / HALF, EPS, ALU.mult, ALU.add) \
                        .then_inc(rms_arg, 1)
                if n == 8:
                    dve.wait_ge(root_ready, 2)
                    chain(nc.vector.reciprocal(small[:, 7], small[:, 6]))
                    for b in range(TB):
                        nc.vector.tensor_scalar(vg[:, b], vg[:, b], small[:, 7, b:b + 1], None, ALU.mult) \
                            .then_inc(vg_ready, 1)
            dve.wait_ge(g_turned, 1)
            chain(nc.vector.tensor_copy(g_col[:], bank[4][:, 0:TB * H1].rearrange("p (b h) -> p b h", b=TB)))

            for h in range(H1):
                dve.wait_ge(m_spread, h + 1)
                if h:
                    dve.wait_ge(num_ready, h)
                for j in range(TB):
                    g = g_col[:, j, h:h + 1]
                    if j < TB - 1:
                        nc.vector.tensor_scalar(dec[:, j, (j + 1) * P:], bank[0][:, (j + 1) * P:], g, None, ALU.add)
                    nc.vector.scalar_tensor_tensor(dec[:, j, j * P:(j + 1) * P], bank[0][:, j * P:(j + 1) * P], g,
                                                   cols(con, C_COLS, "negmask"), ALU.add, ALU.add).then_inc(dec_arg, 1)
                dve.wait_ge(mix_ready, h + 1)
                if h:
                    dve.wait_ge(yg_hi, h)
                bias = cols(par1, P1_COLS, "b_sp")[:, h * P:(h + 1) * P].unsqueeze(1).to_broadcast([P, TB, P])
                chain(nc.vector.scalar_tensor_tensor(gm_a[:].rearrange("p (b t) -> p b t", b=TB),
                                                     bank[7][:].rearrange("p (b t) -> p b t", b=TB),
                                                     cols(par1, P1_COLS, "g_v")[:, h:h + 1], bias, ALU.mult, ALU.add))
                nc.vector.tensor_tensor(gm_a[:], gm_a[:], ug[:, h], ALU.mult).then_inc(gated_ready, 1)
                dve.wait_ge(s_ready, h + 1)
                dve.wait_ge(dec_ready, h + 1)
                for j in range(TB):
                    at = (bank[1][:], bank[2][:, 0:384], bank[3][:, 0:256], bank[3][:, 256:384])[j]
                    last = nc.vector.scalar_tensor_tensor(dec[:, j, j * P:], at, DH_SCALE, dec[:, j, j * P:],
                                                          ALU.mult, ALU.mult)
                    if j:
                        last.then_inc(s_weighted, 1)
                dve.wait_ge(gated_root, h + 1)
                chain(nc.vector.reciprocal(gm_b[:], gm_b[:]))
                nc.vector.scalar_tensor_tensor(gm_a[:], gm_a[:], cols(par1, P1_COLS, "g_gm")[:, h:h + 1], gm_b[:],
                                               ALU.mult, ALU.mult).then_inc(yg_ready, 1)
                dve.wait_ge(nq_abs, h + 1)
                chain(nc.vector.tensor_tensor(ml_a[:], ml_a[:], bank[0][:], ALU.max))
                chain(nc.vector.reciprocal(ml_a[:], ml_a[:]))
                chain(nc.vector.tensor_tensor(ml_a[:], bank[4][:], ml_a[:], ALU.mult))
                nc.vector.tensor_tensor(ml_a[:], ml_a[:], so[:, h], ALU.mult).then_inc(h_ready, 1)
                dve.wait_ge(yg_hi, h + 1)
                nc.vector.tensor_tensor(u_lo[:, 4 + h], gm_a[:], u_hi[:, 4 + h].bitcast(F32), ALU.subtract) \
                    .then_inc(y_lo_ready, 1)
                dve.wait_ge(h_root, h + 1)
                chain(nc.vector.reciprocal(ml_b[:], ml_b[:]))
                nc.vector.scalar_tensor_tensor(ml_a[:], ml_a[:], cols(par1, P1_COLS, "g_ml")[:, h:h + 1], ml_b[:],
                                               ALU.mult, ALU.mult).then_inc(ym_ready, 1)
                dve.wait_ge(ym_hi, h + 1)
                nc.vector.tensor_tensor(u_lo[:, h], ml_a[:], u_hi[:, h].bitcast(F32), ALU.subtract) \
                    .then_inc(y_lo_ready, 1)

            for half in range(2):
                for part in range(2):
                    n = U_OUT + 2 * half + part
                    if n + 1 < STREAM_END:
                        split(n + 1)
                dve.wait_ge(unit_used, U_OUT + 2 * half + 2)
                for b in range(TB):
                    c = slice(half * 512, half * 512 + 512)
                    nc.vector.tensor_tensor(res[:, b, c], bank[4 * half + b][:], res[:, b, c], ALU.add) \
                        .then_inc(res1_ready, 1)

            dve.wait_ge(sq_ready, 3 * TB)
            nc.vector.tensor_scalar(rms2[:, 1], rms2[:, 0], 1.0 / D, EPS, ALU.mult, ALU.add).then_inc(rms_arg, 1)
            dve.wait_ge(root_ready, 3)
            chain(nc.vector.reciprocal(rms2[:, 3], rms2[:, 2]))
            dve.wait_ge(params_landed, 16)
            for b in range(TB):
                nc.vector.scalar_tensor_tensor(xn[:, b], res[:, b], rms2[:, 3, b:b + 1], cols(par2, P2_COLS, "n2g"),
                                               ALU.mult, ALU.mult).then_inc(xn_ready, 1)
            dve.wait_ge(narrow_hi, 2)
            nc.vector.tensor_tensor(wr_lo[:], cols(par2, P2_COLS, "w_r").rearrange("p (k c) -> p k c", k=KC),
                                    wr_hi[:].bitcast(F32), ALU.subtract).then_inc(narrow_lo, 1)
            for c in range(KC):
                dve.wait_ge(u_hi_ready, KC + c + 1)
                nc.vector.tensor_tensor(u_lo[:, c], bank[c % 4][:], u_hi[:, c].bitcast(F32), ALU.subtract) \
                    .then_inc(u_lo_ready, 1)

            def over_last(tile, n):
                return tile.unsqueeze(2).to_broadcast([P, TB, n])

            def iota(n):
                return cols(con, C_COLS, "iota32")[:, 0:n].unsqueeze(1).to_broadcast([P, TB, n])

            def first_largest(out, values, largest, n):
                chain(nc.vector.tensor_tensor(out, values, over_last(largest, n), ALU.is_equal))
                chain(nc.vector.scalar_tensor_tensor(out, out, -64.0, iota(n), ALU.mult, ALU.add))
                chain(nc.vector.tensor_reduce(best[:, 7], out, AX.X, ALU.min))
                chain(nc.vector.tensor_tensor(out, out, over_last(best[:, 7], n), ALU.is_equal))

            chain(nc.vector.tensor_copy(pairs[:], cols(par2, P2_COLS, "pairs").rearrange("p (b k c) -> p b k c", b=TB, k=2)))
            dve.wait_ge(logits_ready, 1)
            chain(nc.vector.tensor_tensor(logit[:], bank[4][:, 0:TB * 36].rearrange("p (b c) -> p b c", b=TB),
                                          cols(par2, P2_COLS, "b_r").unsqueeze(1).to_broadcast([P, TB, 36]), ALU.add))
            chain(nc.vector.tensor_reduce(best[:, 0], logit[:, :, 0:EG], AX.X, ALU.max))
            nc.vector.tensor_tensor(gap[:], logit[:, :, 0:EG], over_last(best[:, 0], EG), ALU.subtract).then_inc(router_arg, 1)
            first_largest(in_group[:], logit[:, :, 0:EG], best[:, 0], EG)
            chain(nc.vector.tensor_tensor(chosen[:], logit[:, :, EG:].rearrange("p b (g j) -> p b g j", g=EG),
                                          in_group[:].unsqueeze(3).to_broadcast([P, TB, EG, PER]), ALU.mult))
            chain(nc.vector.tensor_reduce(le1[:], chosen[:].rearrange("p b g j -> p b j g"), AX.X, ALU.add))
            chain(nc.vector.tensor_reduce(best[:, 2], le1[:], AX.X, ALU.max))
            first_largest(first[:], le1[:], best[:, 2], PER)
            chain(nc.vector.scalar_tensor_tensor(le2[:], first[:], NEG, le1[:], ALU.mult, ALU.add))
            chain(nc.vector.tensor_reduce(best[:, 3], le2[:], AX.X, ALU.max))
            nc.vector.tensor_tensor(best[:, 4], best[:, 3], best[:, 2], ALU.subtract).then_inc(router_arg, 1)
            first_largest(second[:], le2[:], best[:, 3], PER)
            for k, choice in enumerate((first, second)):
                chain(nc.vector.tensor_tensor(owns[:, k].rearrange("p b (g j) -> p b g j", g=EG),
                                              in_group[:].unsqueeze(3).to_broadcast([P, TB, EG, PER]),
                                              choice[:].unsqueeze(2).to_broadcast([P, TB, EG, PER]), ALU.mult))
            nc.vector.tensor_tensor(both[:], owns[:, 0], owns[:, 1], ALU.add).then_inc(owns_ready, 1)
            dve.wait_ge(router_exp, 1)
            chain(nc.vector.tensor_reduce(best[:, 1], gap[:], AX.X, ALU.add))
            dve.wait_ge(router_exp, 2)
            chain(nc.vector.scalar_tensor_tensor(best[:, 6], best[:, 5], 1.0, best[:, 1], ALU.add, ALU.mult))
            chain(nc.vector.reciprocal(weight[:, 0], best[:, 6]))
            chain(nc.vector.tensor_tensor(weight[:, 1], weight[:, 0], best[:, 5], ALU.mult))

            dve.wait_ge(before_ready, 1)
            before = bank[5][:, 0:TB * NE].rearrange("p (b e) -> p b e", b=TB)
            count = bank[5][:, TB * NE:TB * NE + NE]
            chain(nc.vector.tensor_scalar(n_over[:], count, float(P), None, ALU.is_gt))
            chain(nc.vector.scalar_tensor_tensor(n_over[:], count, float(2 * P), n_over[:], ALU.is_gt, ALU.add))
            chain(nc.vector.scalar_tensor_tensor(n_over[:], count, float(3 * P), n_over[:], ALU.is_gt, ALU.add))
            chain(nc.vector.tensor_tensor_scan(over_end[:], ones[:, 0:NE], n_over[:], 0.0, ALU.mult, ALU.add))
            chain(nc.vector.tensor_tensor(over_start[:], over_end[:], n_over[:], ALU.subtract))
            chain(nc.vector.tensor_scalar(blocks[:], before, float(P), None, ALU.is_ge))
            chain(nc.vector.tensor_scalar(over[:], blocks[:], 1.0, None, ALU.mult))
            for n in (2, 3):
                chain(nc.vector.scalar_tensor_tensor(blocks[:], before, float(n * P), blocks[:], ALU.is_ge, ALU.add))
            chain(nc.vector.scalar_tensor_tensor(lift[:], blocks[:], -float(P), before, ALU.mult, ALU.add))
            chain(nc.vector.scalar_tensor_tensor(lift[:], lift[:], float(N_OVER), blocks[:], ALU.mult, ALU.add))
            chain(nc.vector.scalar_tensor_tensor(lift[:], lift[:], float(MAIN - 1),
                                                 over_start[:].unsqueeze(1).to_broadcast([P, TB, NE]), ALU.add, ALU.add))
            chain(nc.vector.scalar_tensor_tensor(row[:], before, float(NE), iota(NE), ALU.mult, ALU.add))
            chain(nc.vector.tensor_tensor(lift[:], lift[:], row[:], ALU.subtract))
            chain(nc.vector.tensor_tensor(lift[:], lift[:], over[:], ALU.mult))
            chain(nc.vector.tensor_tensor(row[:], row[:], lift[:], ALU.add))
            for k in range(2):
                chain(nc.vector.tensor_tensor(lift[:], owns[:, k], row[:], ALU.mult))
                chain(nc.vector.tensor_reduce(dest_f[:, k], lift[:], AX.X, ALU.add))
            chain(nc.vector.tensor_tensor(over_cmp[:], over_end[:].unsqueeze(1).to_broadcast([P, 8, NE]),
                                          cols(con, C_COLS, "iota32")[:, 0:8].unsqueeze(2).to_broadcast([P, 8, NE]), ALU.is_le))
            chain(nc.vector.tensor_reduce(over_e[:], over_cmp[:], AX.X, ALU.add))
            chain(nc.vector.tensor_scalar(over_e[:], over_e[:], float(NE - 1), None, ALU.min))
            chain(nc.vector.tensor_copy(over_int[:, 0:8], over_e[:]))
            chain(nc.vector.tensor_copy(over_int[:, 8:9], over_end[:, NE - 1:NE]))
            nc.vector.tensor_copy(dest[:], dest_f[:]).then_inc(dest_ready, 1)

            def expert_tokens():
                nc.vector.tensor_tensor(xe_lo[:, 0:4], bank[0][:].rearrange("p (c t) -> p c t", c=4),
                                        xe_hi[:, 0:4].bitcast(F32), ALU.subtract)
                nc.vector.tensor_tensor(xe_lo[:, 4:8], bank[1][:].rearrange("p (c t) -> p c t", c=4),
                                        xe_hi[:, 4:8].bitcast(F32), ALU.subtract).then_inc(xe_lo_ready, 1)

            dve.wait_ge(xe_hi_ready, 1)
            expert_tokens()
            with dve.Fori(0, NE // 2) as i:
                for b in range(2):
                    e = i * 2 + b
                    u0 = i * (2 * PER_EXPERT) + (U_MOE + PER_EXPERT * b)

                    def split_at(j):
                        dve.wait_ge(hi_ready, u0 + (j + 1))
                        nc.vector.tensor_tensor(w_lo[:, j % 2], raw[:, (PER_EXPERT * b + j) % RAW],
                                                w_hi[:, j % 2].bitcast(F32), ALU.subtract).then_inc(lo_ready, 1)

                    split_at(1)
                    split_at(2)
                    split_at(3)
                    split_at(4)
                    dve.wait_ge(silu_ready, e + 1)
                    dve.wait_ge(unit_used, u0 + 4)
                    nc.vector.tensor_tensor(hid[:], gate[:], bank[3][:], ALU.mult).then_inc(hid_ready, 1)
                    dve.wait_ge(xe_hi_ready, e + 2)
                    expert_tokens()
                    split_at(5)
                    dve.wait_ge(hid_hi_ready, e + 1)
                    nc.vector.tensor_tensor(hid_lo[:], bank[4][:].rearrange("p (c t) -> p c t", c=4),
                                            hid_hi[:].bitcast(F32), ALU.subtract).then_inc(hid_lo_ready, 1)
                    split_at(6)
                    dve.wait_ge(y_free[b], i * 16 + 16)
                    dve.wait_ge(unit_used, u0 + 6)
                    nc.vector.tensor_copy(y_rows[:, b, 512:1024], bank[6][:]).then_inc(y_dve, 1)

            with dve.If(overflowing(dve)):
                with dve.Fori(0, N_OVER) as v:
                    dve.wait_ge(over_products, v * 4 + 2)
                    dve.wait_ge(over_copies, v * 4 + 2)
                    nc.vector.tensor_tensor(hid[:], gate[:], bank[3][:], ALU.mult).then_inc(over_hid, 1)
            dve.wait_ge(y_landed, 16)
            for k in range(2):
                for b in range(TB):
                    last = nc.vector.scalar_tensor_tensor(res[:, b], y_pairs[:, b, k], weight[:, k, b:b + 1], res[:, b],
                                                          ALU.mult, ALU.add)
                    if k == 0:
                        steps.mark(last)
                    else:
                        last.then_inc(res2_ready, 1)
                dve.wait_ge(dve_step, steps.value())
            dve.wait_ge(sq_ready, 4 * TB)
            nc.vector.tensor_scalar(rms2[:, 5], rms2[:, 4], 1.0 / D, EPS, ALU.mult, ALU.add).then_inc(rms_arg, 1)
            dve.wait_ge(root_ready, 4)
            chain(nc.vector.reciprocal(rms2[:, 7], rms2[:, 6]))
            for b in range(TB):
                nc.vector.tensor_scalar(xn[:, b], res[:, b], rms2[:, 7, b:b + 1], None, ALU.mult).then_inc(xn_ready, 1)
            dve.wait_ge(xn_ready, 2 * TB)
            for c in range(KC):
                dve.wait_ge(h_turned, c + 1)
                nc.vector.tensor_scalar(hs[:, c], bank[c % 4][:], cols(par2, P2_COLS, "fg")[:, c:c + 1], None, ALU.mult) \
                    .then_inc(h0_ready, 1)

            def norm(k, gains):
                dve.wait_ge(n_root, k + 1)
                chain(nc.vector.reciprocal(rms[:], rms[:]))
                for c in range(KC):
                    if c:
                        dve.wait_ge(u_lo_ready, (2 + k) * KC + c)
                    nc.vector.scalar_tensor_tensor(u_tmp[:], hs[:, c], gains[:, c:c + 1], rms[:], ALU.mult, ALU.mult) \
                        .then_inc(u_ready, 1)
                    dve.wait_ge(u_hi_ready, (2 + k) * KC + c + 1)
                    nc.vector.tensor_tensor(u_lo[:, c], u_tmp[:], u_hi[:, c].bitcast(F32), ALU.subtract) \
                        .then_inc(u_lo_ready, 1)

            def split_trip(n, i, per):
                dve.wait_ge(hi_ready, i * per + (n + 1))
                nc.vector.tensor_tensor(w_lo[:, n % 2], raw[:, n % RAW], w_hi[:, n % 2].bitcast(F32), ALU.subtract) \
                    .then_inc(lo_ready, 1)

            def add_rows(n0, per_half, ready):
                for half in range(2):
                    for q in range(per_half):
                        n = n0 + half * per_half + q
                        if n + 1 < N_UNITS:
                            split(n + 1)
                    dve.wait_ge(unit_used, n0 + (half + 1) * per_half)
                    for d in range(4):
                        nc.vector.tensor_tensor(hs[:, 4 * half + d], bank[4 * half + d][:], hs[:, 4 * half + d], ALU.add) \
                            .then_inc(h_added, 1)

            dve.wait_ge(params_landed, 32)
            g_mix, g_ffn = cols(par3, P3_COLS, "n_mix"), cols(par3, P3_COLS, "n_ffn")
            lb_view = lb_tile.rearrange("p (l c) -> p l c", l=3)
            chain(nc.vector.tensor_tensor(lbs[0][:], lb_view[:, 0], lb_view[:, 1], ALU.max))
            chain(nc.vector.tensor_tensor(lbs[0][:], lbs[0][:], lb_view[:, 2], ALU.max))
            nc.vector.tensor_tensor(lb_view, lb_view, lbs[0][:].unsqueeze(1).to_broadcast([P, 3, KC]), ALU.subtract) \
                .then_inc(lb_arg, 1)
            norm(0, g_mix[:, 0:KC])
            dve.wait_ge(lb_exp, 1)
            chain(nc.vector.tensor_tensor(lbs[1][:], lb_view[:, 0], lb_view[:, 1], ALU.add))
            chain(nc.vector.tensor_tensor(lbs[1][:], lbs[1][:], lb_view[:, 2], ALU.add))
            chain(nc.vector.reciprocal(lbs[2][:], lbs[1][:]))
            low, span = lbs[3], lbs[4]
            chain(nc.vector.tensor_tensor(low[:], lb_view[:, 0], lbs[2][:], ALU.mult))
            chain(nc.vector.tensor_scalar(span[:], low[:], -1.0, 1.0, ALU.mult, ALU.add))

            reset = cols(par3, P3_COLS, "reset")
            levels = cols(par3, P3_COLS, "levels").bitcast(U32).rearrange("p (n t) -> p n t", n=8)
            with dve.Fori(0, HH // 2) as p:
                steps.enter(p, HG_STEPS)
                split_trip(U_HG + 1, p, 4)
                for hh in range(2):
                    h = bass.ds(p * 2 + hh, 1)
                    dve.wait_ge(f_sig, p * 2 + (hh + 1))
                    chain(nc.vector.tensor_scalar(fx[:, hh], fx[:, hh], span[:, h], low[:, h], ALU.mult, ALU.add))
                    nc.vector.tensor_scalar(key[:, hh], fx[:, hh], -1.0, 1.0, ALU.mult, ALU.add).then_inc(f_ready, 1)
                split_trip(U_HG + 2, p, 4)
                for hh in range(2):
                    dve.wait_ge(f_log, p * 2 + (hh + 1))
                    nc.vector.tensor_tensor_scan(run[:, hh], reset, fx[:, hh], 0.0, ALU.mult, ALU.add).then_inc(run_ready, 1)
                split_trip(U_HG + 3, p, 4)
                split_trip(U_HG + 4, p, 4)
                for hh in range(2):
                    for n in range(9):
                        if n < 7:
                            w = 64 >> n
                            dve.wait_ge(lev_exp, p * 14 + (7 * hh + n + 1))
                            if n >= 2:
                                dve.wait_ge(lev_ready, p * 16 + (8 * hh + n - 1))
                            view = lambda ap: ap.rearrange("p (n t) -> p n t", t=2 * w)[:, :, 0:w]
                            nc.vector.tensor_tensor(view(k_dec[n % 2][:]), view(fx[:, n % 2]), view(key[:, hh]), ALU.mult) \
                                .then_inc(k_ready, 1)
                        if n >= 1:
                            dve.wait_ge(lev_ready, p * 16 + (8 * hh + n))
                            if n >= 2:
                                dve.wait_ge(lev_taken, p * 16 + (8 * hh + n - 1))
                            nc.vector.memset(turn[:, n - 1:n], 0.0)
                            nc.vector.copy_predicated(ws[:, :, 0:P], levels[:, n - 1].unsqueeze(1).to_broadcast([P, TB, P]),
                                                      bank[4 + (n - 1) % 2][:].rearrange("p (b t) -> p b t", b=TB)) \
                                .then_inc(lev_taken, 1)
                    k_far, q_far = k_dec[0], q_dec[0]
                    dve.wait_ge(far_exp, p * 2 + (hh + 1))
                    chain(nc.vector.tensor_tensor(k_far[:, 0:384], fx[:, 1, 0:384], key[:, hh, 0:384], ALU.mult))
                    nc.vector.tensor_tensor(q_far[:, 0:256], fx[:, 0, 0:256], qry[:, hh, 128:384], ALU.mult)
                    chain(nc.vector.tensor_tensor(q_far[:, 384:512], fx[:, 0, 256:384], qry[:, hh, 384:512], ALU.mult))
                    nc.vector.tensor_scalar(k_far[:, 384:512], k_far[:, 0:128], b_exp[:, 0:1], None, ALU.mult)
                    nc.vector.tensor_scalar(q_far[:, 256:384], q_far[:, 384:512], b_exp[:, 1:2], None, ALU.mult) \
                        .then_inc(far_kq, 1)
                    dve.wait_ge(o_root, p * 2 + (hh + 1))
                    chain(nc.vector.reciprocal(fx[:, 1], fx[:, 1]))
                    chain(nc.vector.scalar_tensor_tensor(fx[:, 0], bank[6][:], cols(par3, P3_COLS, "og"), fx[:, 1],
                                                         ALU.mult, ALU.mult))
                    dve.wait_ge(g_taken, p * 2 + 2)
                    nc.vector.tensor_tensor(fx[:, 0], fx[:, 0], sg[:, hh], ALU.mult).then_inc(o_ready, 1)
                    dve.wait_ge(o_hi_ready, p * 2 + (hh + 1))
                    h = bass.ds(p * 2 + hh, 1)
                    nc.vector.tensor_tensor(o_lo[:, h].rearrange("p h t -> p (h t)"), fx[:, 0],
                                            o_hi[:, h].bitcast(F32).rearrange("p h t -> p (h t)"), ALU.subtract) \
                        .then_inc(o_lo_ready, 1)
            steps.leave(HH // 2)
            add_rows(U_HGO, 2, None)

            def ffn(l, u0):
                base = l * FC
                norm(1 + 2 * l, g_ffn[:, l * KC:l * KC + KC])

                def unit(n, chunk, slot, i=None):
                    def at(v):
                        return v if i is None else i * 4 + v
                    if i is None:
                        split(n + 1)
                    else:
                        split_trip(n + 1, i, 4)
                    s = n % 2
                    dve.wait_ge(f_silu, at(chunk + 1))
                    nc.vector.tensor_tensor(f_hid[s][:], f_gate[s][:], bank[2 * s + 1][:], ALU.mult).then_inc(f_prod, 1)
                    dve.wait_ge(f_hi, at(chunk + 1))
                    c = slice(slot, slot + 1) if i is None else bass.ds(i * 4 + slot, 1)
                    nc.vector.tensor_tensor(hid2_lo[:, c].rearrange("p c t -> p (c t)"), f_hid[s][:],
                                            hid2_hi[:, c].bitcast(F32).rearrange("p c t -> p (c t)"), ALU.subtract) \
                        .then_inc(f_lo, 1)

                with dve.Fori(0, FA // 4) as i:
                    for j in range(4):
                        unit(u0 + j, base + j, j, i)
                add_rows(u0 + FA, 3, None)
                u1 = u0 + FA + 6
                with dve.Fori(0, 2) as i:
                    for j in range(4):
                        unit(u1 + j, base + FA + j, j, i)
                for j in range(8, FC - FA):
                    unit(u1 + j, base + FA + j, j)
                add_rows(u1 + FC - FA, 3, None)

            ffn(0, U_FF0)

            norm(2, g_mix[:, KC:2 * KC])
            cos, sin = cols(par3, P3_COLS, "cos"), cols(par3, P3_COLS, "sin")
            band = cols(par3, P3_COLS, "band")
            for g in range(3):
                for half in range(2):
                    split(U_QKV + 6 * g + half + 1)
                for pair in range(2):
                    for kind in range(2):
                        n = U_QKV + 6 * g + 2 + 2 * pair + kind
                        split(n + 1)
                        for half in range(2):
                            m = 8 * g + 4 * pair + 2 * kind + half
                            src = bank[2 * kind + half]
                            if half == 0:
                                dve.wait_ge(proj_ready, PROJ_ATTN + m // 2 + 1)
                            else:
                                dve.wait_ge(unit_used, n + 1)
                            if m >= 2:
                                dve.wait_ge(rope_ready, m - 1)
                            nc.vector.tensor_tensor(r_cos[m % 2][:], src[:], cos, ALU.mult)
                            nc.vector.tensor_tensor(r_sin[m % 2][0:64, :], src[64:128, :], sin[64:128], ALU.mult)
                            nc.vector.tensor_tensor(r_sin[m % 2][64:128, :], src[0:64, :], sin[0:64], ALU.mult) \
                                .then_inc(rope_mul, 1)
                    for half in range(2):
                        m = AH * g + 2 * pair + half
                        h = 2 * pair + half
                        at = 4 + 2 * (m % 2)
                        pr = prob_of(g, h)
                        dve.wait_ge(sc_ready, m + 1)
                        if g == 0:
                            nc.vector.tensor_tensor(pr[:, 0], bank[at][:, 0:256], band[:, 0:256], ALU.add)
                            nc.vector.tensor_tensor(pr[:, 1], bank[at][:, 256:512], band[:, 256:512], ALU.add)
                            chain(nc.vector.tensor_tensor(pr[:, 2:4], bank[at + 1][:].rearrange("p (b s) -> p b s", b=2),
                                                          band[:, 256:512].unsqueeze(1).to_broadcast([P, 2, 256]), ALU.add))
                        else:
                            mask = band[:, 512 + (g - 1) * P:512 + g * P]
                            chain(nc.vector.tensor_tensor(pr, bank[at][:].rearrange("p (b s) -> p b s", b=TB),
                                                          mask.unsqueeze(1).to_broadcast([P, TB, P]), ALU.add))
                        nc.vector.tensor_reduce(stat[g][:, :, h], pr, AX.X, ALU.max).then_inc(sc_max, 1)
                    for half in range(2):
                        m = AH * g + 2 * pair + half
                        h = 2 * pair + half
                        dve.wait_ge(sc_exp, m + 1)
                        nc.vector.tensor_reduce(stat[g][:, :, AH + h], prob_of(g, h), AX.X, ALU.add).then_inc(sc_sum, 1)
            dve.wait_ge(sc_sum, 3 * AH)
            dve.wait_ge(order_landed, 32)
            nat = [stat[0], stat_nat[1], stat_nat[2]]
            chain(nc.vector.tensor_tensor(top[:], nat[0][:, :, 0:AH], nat[1][:, :, 0:AH], ALU.max))
            chain(nc.vector.tensor_tensor(top[:], top[:], nat[2][:, :, 0:AH], ALU.max))
            for g in range(3):
                last = nc.vector.tensor_tensor(share[:, g], nat[g][:, :, 0:AH], top[:], ALU.subtract)
            last.then_inc(share_arg, 1)
            dve.wait_ge(share_exp, 1)
            chain(nc.vector.tensor_tensor(den[:], share[:, 0], nat[0][:, :, AH:], ALU.mult))
            for g in (1, 2):
                chain(nc.vector.tensor_tensor(top[:], share[:, g], nat[g][:, :, AH:], ALU.mult))
                chain(nc.vector.tensor_tensor(den[:], den[:], top[:], ALU.add))
            chain(nc.vector.reciprocal(den[:], den[:]))
            for g in range(3):
                nc.vector.tensor_tensor(share[:, g], share[:, g], den[:], ALU.mult).then_inc(share_ready, 1)
            for m in range(3 * AH):
                g = m // AH
                at = 4 * (m % 2)
                dve.wait_ge(ao_hi_ready, m + 1)
                nc.vector.tensor_tensor(natural_order(ao_lo[:, m], g), group_order(bank[at + 2][:], g),
                                        natural_order(ao_hi[:, m].bitcast(F32), g), ALU.subtract).then_inc(ao_lo_ready, 1)
            add_rows(U_AO, 3, None)

            ffn(1, U_FF1)
            dve.wait_ge(sq_ready, 6 * TB)
            chain(nc.vector.tensor_tensor(out_rms[:, 2], out_rms[:, 0], out_rms[:, 1], ALU.add))
            nc.vector.tensor_scalar(out_rms[:, 3], out_rms[:, 2], 1.0 / D, EPS, ALU.mult, ALU.add).then_inc(rms_arg, 1)
            dve.wait_ge(root_ready, 5)
            chain(nc.vector.reciprocal(out_rms[:, 5], out_rms[:, 4]))
            for b in range(TB):
                if b >= 2:
                    dve.wait_ge(out_stored[b % 2], 16)
                for half in range(2):
                    c = slice(half * T, half * T + T)
                    last = nc.vector.scalar_tensor_tensor(out_tile[b % 2][:, c], bank[2 * b + half][:], out_rms[:, 5, b:b + 1],
                                                          cols(par3, P3_COLS, "fin")[:, c], ALU.mult, ALU.mult)
                last.then_inc(fin_ready, 1)


        @block.gpsimd
        def _(pool):
            nc.gpsimd.memset(no_pairs[:], NO_PAIR).then_inc(rows_set, 1)
            pool.wait_ge(rows_set, 1)
            pool.dma_start(slot_table.rearrange("(p n) c -> p (n c)", p=P), no_pairs[:]).then_inc(table_written, 16)
            pool.wait_ge(y_lo_ready, 8)
            pool.dma_start(par2[:], phase2_in).then_inc(params_landed, 16)
            pool.wait_ge(xn_ready, TB)
            pool.dma_start(token_rows.rearrange("(b p) d -> p b d", p=P), xn[:]).then_inc(tokens_stored, 16)
            pool.wait_ge(table_written, 16)
            pool.wait_ge(dest_ready, 1)
            nc.gpsimd.memset(slots[:, NE], NO_PAIR).then_inc(rows_set, 1)
            nc.gpsimd.memset(x_rows[:], 0.0).then_inc(rows_set, 1)
            pool.wait_ge(rows_set, 3)
            for b in range(TB):
                for k in range(2):
                    nc.gpsimd.indirect_dma_start(
                        out=slot_table, out_offset=bass.IndirectOffsetOnAxis(ap=dest[:, k, b:b + 1], axis=0),
                        in_=pairs[:, b, k], in_offset=None).then_inc(table_written, 16)
            pool.wait_ge(table_written, 16 + 16 * 2 * TB)
            pool.dma_start(slots[:, 0:NE], slot_table[0:MAIN].rearrange("(s e) c -> s e c", s=P)).then_inc(slots_landed, 16)
            pool.dma_start(over_slots[:], slot_table[MAIN:].rearrange("(s v) c -> s v c", s=P)).then_inc(slots_landed, 16)
            pool.wait_ge(slots_landed, 32)
            pool.wait_ge(tokens_stored, 16)
            for b in range(2):
                pool.dma_start(y_mark[b:b + 1, :], no_pairs[b:b + 1, 0:8]).then_inc(y_free[b], 16)

            def gather(e):
                nc.gpsimd.indirect_dma_start(
                    out=x_rows[:, e % 2], out_offset=None, in_=token_rows,
                    in_offset=bass.IndirectOffsetOnAxis(ap=slots[:, e, 0:1], axis=0),
                    bounds_check=T - 1, oob_is_err=False).then_inc(x_gathered[e % 2], 16)

            gather(0)
            gather(1)
            for e in range(NE):
                pool.wait_ge(y_act, e + 1)
                pool.wait_ge(y_dve, e + 1)
                nc.gpsimd.indirect_dma_start(
                    out=pair_rows, out_offset=bass.IndirectOffsetOnAxis(ap=slots[:, e, 1:2], axis=0),
                    in_=y_rows[:, e % 2], in_offset=None, bounds_check=2 * T - 1, oob_is_err=False) \
                    .then_inc(y_free[e % 2], 16)
                if e + 2 <= NE:
                    pool.wait_ge(xe_turned, e + 1)
                    gather(e + 2)
            for b in range(2):
                pool.wait_ge(y_free[b], 16 * (NE // 2 + 1))
            with pool.If(overflowing(pool)):
                for v in range(N_OVER):
                    at_unit = pool.value_load(over_int[0:1, v:v + 1]) * PER_EXPERT + U_MOE
                    pool.dma_start(over_weights[:], weights_in[bass.ds(at_unit, 4)].rearrange("u p n -> p u n"))                         .then_inc(over_w, 16)
                    nc.gpsimd.indirect_dma_start(
                        out=x_rows[:, 0], out_offset=None, in_=token_rows,
                        in_offset=bass.IndirectOffsetOnAxis(ap=over_slots[:, v, 0:1], axis=0),
                        bounds_check=T - 1, oob_is_err=False).then_inc(over_x, 16)
                    pool.wait_ge(over_products, v * 4 + 2)
                    pool.dma_start(over_weights[:, 0:2], weights_in[bass.ds(at_unit + 4, 2)].rearrange("u p n -> p u n"))                         .then_inc(over_w, 16)
                    pool.wait_ge(over_copies, v * 4 + 4)
                    nc.gpsimd.indirect_dma_start(
                        out=pair_rows, out_offset=bass.IndirectOffsetOnAxis(ap=over_slots[:, v, 1:2], axis=0),
                        in_=y_rows[:, 0], in_offset=None, bounds_check=2 * T - 1, oob_is_err=False).then_inc(over_stored, 16)
                    pool.wait_ge(over_stored, v * 16 + 16)
            pool.dma_start(y_pairs[:], pair_rows.rearrange("(b p k) d -> p b k d", p=P, k=2)).then_inc(y_landed, 16)
            pool.wait_ge(y_landed, 16)

            pool.wait_ge(h0_ready, KC)
            pool.dma_start(par3[:], phase3_in).then_inc(params_landed, 16)
            pool.wait_ge(u_lo_ready, 3 * KC)
            for tile in (k_dec[0], k_dec[1], q_dec[0], q_dec[1], ws):
                nc.gpsimd.memset(tile[:], 0.0).then_inc(set_up, 1)
            with pool.Fori(0, HH // 2) as p:
                for hh in range(2):
                    if hh == 0:
                        pool.wait_ge(run_ready, p * 2 + 2)
                        pool.wait_ge(q_taken, p * 2 + 2)
                    else:
                        pool.wait_ge(o_lo_ready, p * 2 + 1)
                    for n in range(7):
                        w = 64 >> n
                        r3 = run[:, hh].rearrange("p (n t) -> p n t", t=2 * w)
                        x3 = fx[:, n % 2].rearrange("p (n t) -> p n t", t=2 * w)
                        ref = r3[:, :, w - 1:w].to_broadcast([P, T // (2 * w), w])
                        if n >= 2:
                            pool.wait_ge(k_ready, p * 14 + (7 * hh + n - 1))
                            pool.wait_ge(q_ready, p * 14 + (7 * hh + n - 1))
                        nc.gpsimd.tensor_tensor(x3[:, :, 0:w], ref, r3[:, :, 0:w], ALU.subtract)
                        nc.gpsimd.tensor_tensor(x3[:, :, w:], r3[:, :, w:], ref, ALU.subtract).then_inc(gap_to_ref, 1)
                        if n >= 1:
                            query_part(pool, p, hh, n - 1)
                    query_part(pool, p, hh, 6)

            def rope(m):
                pool.wait_ge(rope_mul, m + 1)
                kind, half = (m // 2) % 2, m % 2
                g = m // 8
                dst = (q_rot, k_rot)[kind][half]
                nc.gpsimd.tensor_tensor(group_order(dst[:], g), natural_order(r_cos[m % 2][:], g),
                                        natural_order(r_sin[m % 2][:], g), ALU.add).then_inc(rope_ready, 1)

            def sub_max(m):
                g, h = m // AH, m % AH
                pool.wait_ge(sc_max, m + 1)
                pr = prob_of(g, h)
                nc.gpsimd.tensor_tensor(pr, pr, stat[g][:, :, h:h + 1].to_broadcast(list(pr.shape)), ALU.subtract) \
                    .then_inc(sc_gap, 1)

            for pair in range(6):
                if pair:
                    pool.wait_ge(sc_ready, 2 * pair)
                for m in range(4):
                    rope(4 * pair + m)
                for half in range(2):
                    sub_max(2 * pair + half)
            pool.wait_ge(sc_sum, 3 * AH)
            for g in (1, 2):
                pool.dma_start(stat_rows[g - 1].rearrange("(p b) n -> p b n", b=TB), stat[g][:]).then_inc(order_stored, 16)
            pool.wait_ge(order_stored, 32)
            for g in (1, 2):
                pool.dma_start(stat_nat[g][:], stat_rows[g - 1].rearrange("(b p) n -> p b n", p=P)).then_inc(order_landed, 16)
            pool.wait_ge(share_ready, 3)
            for g in (1, 2):
                pool.dma_start(share_rows[g - 1].rearrange("(b p) n -> p b n", p=P), share[:, g]).then_inc(order_stored, 16)
            pool.wait_ge(order_stored, 64)
            for g in (1, 2):
                pool.dma_start(share_g[g][:], share_rows[g - 1].rearrange("(p b) n -> p b n", b=TB)).then_inc(order_landed, 16)
            for m in range(3 * AH):
                g, h = m // AH, m % AH
                if m == AH:
                    pool.wait_ge(order_landed, 64)
                factor = share[:, 0, :, h:h + 1] if g == 0 else share_g[g][:, :, h:h + 1]
                pr = prob_of(g, h)
                nc.gpsimd.tensor_tensor(pr, pr, factor.to_broadcast(list(pr.shape)), ALU.mult).then_inc(p_ready, 1)


def unit_cols(w):
    return w.reshape(KC, P, -1, 256).transpose(2, 1, 0, 3).reshape(-1, P, UNIT)


def unit_rows(w):
    k, n = w.shape
    short = -k % 512
    if short:
        w = np.concatenate([w, np.zeros((short, n), w.dtype)])
    return w.reshape(-1, 4, P, n // 512, 512).transpose(3, 0, 2, 1, 4).reshape(-1, P, UNIT)


def unit_experts(w_gate, w_up, w_down):
    def tall(w):
        return w.reshape(NE, 2, 4, P, FE).transpose(0, 1, 3, 2, 4).reshape(NE, 2, P, UNIT)
    down = w_down.reshape(NE, 2, 2, P, D).transpose(0, 1, 3, 2, 4).reshape(NE, 2, P, UNIT)
    return np.concatenate([tall(w_gate), tall(w_up), down], axis=1).reshape(-1, P, UNIT)


def unit_ffn(w_in, w_down):
    pair = np.concatenate([w_in[:, :FF].reshape(D, FC, P), w_in[:, FF:].reshape(D, FC, P)], axis=2)
    up = unit_cols(pair.reshape(D, FC * 256))
    cut = FA * P
    return [up[:FA], unit_rows(w_down[:cut]), up[FA:], unit_rows(w_down[cut:])]


def weight_stream(a):
    w = a["w_in"][0]
    q = HALF
    parts = [unit_cols(np.ascontiguousarray(w[:, :2 * q])), unit_cols(np.ascontiguousarray(w[:, 5 * q + 8:])),
             unit_cols(np.ascontiguousarray(w[:, 4 * q + 8:5 * q + 8])), unit_cols(np.ascontiguousarray(w[:, 3 * q:4 * q])),
             unit_cols(np.ascontiguousarray(w[:, 2 * q:3 * q])), unit_rows(a["w_out"][0]),
             unit_experts(a["w_gate"][0], a["w_up"][0], a["w_down"][0])]
    hg = unit_cols(a["hgrn_w_in_2"][0]).reshape(4, 4, P, UNIT)
    parts.append(np.ascontiguousarray(hg[[1, 0, 2, 3]].transpose(1, 0, 2, 3)).reshape(-1, P, UNIT))
    parts.append(unit_rows(a["hgrn_w_out_2"][0]))
    parts += unit_ffn(a["ffn_w_in_2"][0], a["ffn_w_down_2"][0])
    qkv = unit_cols(a["attn_w_qkv_2"][0]).reshape(3, 3, 2, P, UNIT)
    for g in range(3):
        parts.append(np.stack([qkv[2, g, 0], qkv[2, g, 1], qkv[0, g, 0], qkv[1, g, 0], qkv[0, g, 1], qkv[1, g, 1]]))
    parts.append(unit_rows(a["attn_w_out_2"][0]))
    parts += unit_ffn(a["ffn_w_in_2"][1], a["ffn_w_down_2"][1])
    out = np.concatenate(parts)
    assert out.shape[0] == N_UNITS
    return out


def pack(cols, n, parts):
    out = np.zeros((P, n), np.float32)
    for name, value in parts.items():
        at, size = cols[name]
        out[:value.shape[0], at:at + size] = value.reshape(value.shape[0], size)
    return out


def chunk_cols(v):
    return np.moveaxis(v.reshape(v.shape[:-1] + (-1, P)), -1, 0).reshape(P, -1)


def constants():
    s, t = np.arange(P)[:, None], np.arange(P)[None, :]
    sel = np.zeros((H1, H1, P))
    for h in range(H1):
        sel[h, h] = 1
    return pack(C_COLS, C_N, {
        "ident": s == t, "upper": s <= t, "strict": s < t, "ones": np.ones((P, P)), "blocks64": s // 64 == t // 64,
        "negmask": np.where(s <= t, 0, NEG), "sel": sel.reshape(H1, -1), "eps": np.full((P, 1), EPS),
        "iota32": np.broadcast_to(np.arange(NE), (P, NE))})


def phase1(a):
    w_if = np.zeros((KC, P, P), np.float32)
    src = a["w_in"][0][:, 4 * HALF:4 * HALF + 8].reshape(KC, P, 8)
    w_if[:, :, 0:4], w_if[:, :, 32:36] = src[..., :4], src[..., 4:]
    b_f = np.zeros((P, 1), np.float32)
    b_f[32:36, 0] = a["b_fgate"][0]
    return pack(P1_COLS, P1_N, {
        "n1g": chunk_cols(a["norm1_g"][0]), "conv": chunk_cols(a["conv_qk"][0]), "b_i": a["b_igate"][0][:, None],
        "b_f": b_f, "g_ml": chunk_cols(a["g_mlstm_out"][0]), "g_v": chunk_cols(a["g_gmlp_v"][0]),
        "g_gm": chunk_cols(a["g_gmlp_out"][0]),
        "b_sp": np.repeat(a["b_spatial"][0], 64, axis=0).reshape(4, P, P).transpose(1, 0, 2).reshape(P, -1),
        "w_sp": a["w_spatial"][0].transpose(2, 0, 1).reshape(P, -1),
        "w_if": w_if.transpose(1, 0, 2).reshape(P, -1), "one_row": np.ones((P, T))})


def phase2(a):
    w_r = np.concatenate([a["w_router_group"][0], a["w_router_expert"][0]], axis=1)
    b_r = np.concatenate([a["b_router_group"][0], a["b_router_expert"][0]])
    token = np.arange(T).reshape(TB, P).T
    pairs = np.stack([np.stack([token, 2 * token + k], axis=-1) for k in range(2)], axis=2)
    return pack(P2_COLS, P2_N, {
        "n2g": np.broadcast_to(a["norm2_g"][0], (P, D)), "w_r": w_r.reshape(KC, P, 36).transpose(1, 0, 2).reshape(P, -1),
        "b_r": np.broadcast_to(b_r, (P, 36)), "fg": chunk_cols(a["final_g"]), "pairs": pairs.reshape(P, -1)})


def phase3(a):
    s, t = np.arange(P)[:, None], np.arange(P)[None, :]
    levels = np.zeros((P, 8, P), np.uint32)
    for n, w in enumerate((64, 32, 16, 8, 4, 2, 1)):
        levels[:, n] = (s // (2 * w) == t // (2 * w)) & (s % (2 * w) < w) & (t % (2 * w) >= w)
    levels[:, 7] = s == t
    inv = (1.0 / (np.float32(10000.0) ** (np.arange(0, P, 2, dtype=np.float32) / np.float32(P)))).astype(np.float32)
    ang = (np.arange(T, dtype=np.float32)[:, None] * inv[None, :]).T
    cos, sin = np.cos(ang), np.sin(ang)
    key, query = t, s
    causal = np.where(key <= query, 0, NEG)
    never = np.full((P, P), NEG)
    band = np.concatenate([causal, never, np.where(key >= query, 0, NEG), causal,
                           causal, np.where((key <= query) & ((key - query) % (DIL[2] // STEP[2]) == 0), 0, NEG)], axis=1)
    reset = np.ones(T)
    reset[::P] = 0
    return pack(P3_COLS, P3_N, {
        "n_mix": chunk_cols(a["norm_mix_2"]), "n_ffn": chunk_cols(a["norm_ffn_2"]),
        "lb": chunk_cols(a["hgrn_lb_logits_2"]), "og": a["hgrn_out_norm_2"][0][:, None],
        "fin": np.broadcast_to(a["final_norm_2"], (P, D)),
        "levels": levels.view(np.float32), "cos": np.concatenate([cos, cos]), "sin": np.concatenate([sin, -sin]),
        "band": band, "reset": np.broadcast_to(reset, (P, T))})


def kernel(**inputs):
    import concourse.bacc as bacc
    from concourse.bass_utils import run_bass_kernel_spmd

    a = {name: np.asarray(value) for name, value in inputs.items()}
    nc = bacc.Bacc("TRN2", target_bir_lowering=False, num_devices=1)
    arrays = {"x_in": np.ascontiguousarray(a["x"][0]), "weights_in": weight_stream(a), "constants_in": constants(),
              "phase1_in": phase1(a), "phase2_in": phase2(a), "phase3_in": phase3(a)}
    aps = [nc.dram_tensor(name, v.shape, F32, kind="ExternalInput").ap() for name, v in arrays.items()]
    out = nc.dram_tensor("out_0", (T, D), F32, kind="ExternalOutput").ap()
    build(nc, *aps, out)
    r = run_bass_kernel_spmd(nc, [arrays], core_ids=[0])
    return r.results[0]["out_0"].reshape(1, T, D)
```

```python
from contextlib import ExitStack

import numpy as np

import concourse.bass as bass
from concourse import mybir

ALU = mybir.AluOpType
ACT = mybir.ActivationFunctionType
AX = mybir.AxisListType
F32 = mybir.dt.float32
F32R = mybir.dt.float32r
I32 = mybir.dt.int32
U32 = mybir.dt.uint32

P = 128
T = 512
TB = T // P
D = 1024
KC = D // P
EPS = 1e-6
H1 = 4
HALF = D // 2
NG = 8
NE = 32
EG = 4
PER = NE // EG
FE = 512
HH = 8
FF = 2816
FC = FF // P
AH = 4
DIL = (1, 4, 16)
STEP = (1, 4, 4)
AW = 3 * AH * P
DH_SCALE = float(P) ** -0.5
NEG = -1.0e30
UNIT = 2048
RAW = 4
FA = 12

U_IN = 0
N_IN = 12
U_OUT = U_IN + N_IN
N_OUT = 4
U_MOE = U_OUT + N_OUT
PER_EXPERT = 6
U_HG = U_MOE + NE * PER_EXPERT
U_HGO = U_HG + 16
U_FF0 = U_HGO + 4
N_FF = FC + 12
U_QKV = U_FF0 + N_FF
U_AO = U_QKV + 18
U_FF1 = U_AO + 6
N_UNITS = U_FF1 + N_FF

def columns(*sizes):
    at, out = 0, {}
    for name, n in sizes:
        out[name] = (at, n)
        at += n
    return out, at

C_COLS, C_N = columns(("ident", P), ("upper", P), ("strict", P), ("ones", P), ("blocks64", P), ("negmask", P),
                      ("sel", H1 * P), ("eps", 1), ("iota32", NE))
P1_COLS, P1_N = columns(("n1g", KC), ("conv", 4 * KC), ("b_i", 1), ("b_f", 1), ("g_ml", 4), ("g_v", 4), ("g_gm", 4),
                        ("b_sp", 4 * P), ("w_sp", NG * P), ("w_if", KC * P), ("one_row", T))
P2_COLS, P2_N = columns(("n2g", D), ("w_r", KC * 36), ("b_r", 36), ("fg", KC), ("pairs", 4 * TB))
P3_COLS, P3_N = columns(("n_mix", 2 * KC), ("n_ffn", 2 * KC), ("lb", 3 * KC), ("og", 1), ("fin", D),
                        ("levels", 8 * P), ("cos", T), ("sin", T), ("band", 3 * 256), ("reset", T))


class Count:

    def __init__(self, sem):
        self.sem, self.n, self.per_trip, self.trip, self.start = sem, 0, 0, None, 0

    def value(self, back=0):
        n = self.n - back
        return n if self.trip is None else self.trip * self.per_trip + n

    def mark(self, instruction):
        instruction.then_inc(self.sem, 1)
        self.n += 1
        return self.value()

    def enter(self, trip, per_trip, first=0):
        self.trip, self.per_trip, self.start = trip, per_trip, self.n
        self.n -= first * per_trip

    def leave(self, trips, first=0):
        assert self.n + first * self.per_trip - self.start == self.per_trip, (self.n, self.start, self.per_trip)
        self.trip = None
        self.n = self.start + trips * self.per_trip


def build(nc, x_in, weights_in, constants_in, phase1_in, phase2_in, phase3_in, out):
    with ExitStack() as ctx:
        def sem(name):
            return ctx.enter_context(nc.semaphore(name))

        arena_at = nc.sbuf_base + -nc.sbuf_base % 32
        at_raw = arena_at
        at_hi = at_raw + RAW * UNIT * 4
        at_lo = at_hi + 2 * UNIT * 4
        at_res = at_lo + 2 * UNIT * 4
        at_con = at_res + TB * D * 4
        at_par = at_con + (C_N * 4 + 31) // 32 * 32
        at_a = at_par + (max(P1_N, P2_N, P3_N) * 4 + 31) // 32 * 32
        at_b = at_a + 24 * T * 4
        at_x = at_b + 28 * T * 4
        arena_end = at_x + 608
        ctx.enter_context(nc.sbuf_tensor("arena", [P, arena_end - arena_at], mybir.dt.uint8))

        def place(name, shape, at, dt=F32):
            return nc.alloc_sbuf_tensor_at(name, [P] + shape, dt, offset=at)

        KB2 = T * 4
        raw = place("raw", [RAW, UNIT], at_raw)
        w_hi = place("w_hi", [2, UNIT], at_hi, F32R)
        w_lo = place("w_lo", [2, UNIT], at_lo, F32R)
        res = place("res", [TB, D], at_res)
        con = place("con", [C_N], at_con)
        par1 = place("par1", [P1_N], at_par)

        def cols(tile, table, name):
            at, n = table[name]
            return tile[:, at:at + n]

        ident, ones = cols(con, C_COLS, "ident"), cols(con, C_COLS, "ones")
        eps = cols(con, C_COLS, "eps")

        u_hi = place("u_hi", [KC, T], at_a, F32R)
        u_lo = place("u_lo", [KC, T], at_a + KC * KB2, F32R)
        at_a2 = at_a + 16 * KB2

        xs = place("xs", [TB, D], at_b)
        qk = place("qk", [KC, T], at_b)
        so = place("so", [4, T], at_b + 8 * KB2)
        ug = place("ug", [4, T], at_b + 12 * KB2)
        vm = place("vm", [TB, HALF], at_b + 16 * KB2)
        vg = place("vg", [TB, HALF], at_b + 20 * KB2)
        junk = place("junk", [D], at_b + 20 * KB2)
        dec = place("dec", [TB, T], at_b + 24 * KB2)
        wif_hi = place("wif_hi", [KC, P], at_b + 24 * KB2, F32R)
        wif_lo = place("wif_lo", [KC, P], at_b + 26 * KB2, F32R)
        neg_m = place("neg_m", [T], at_a2)
        e_neg_m = place("e_neg_m", [T], at_a2 + KB2)
        r_f, r_i, r_e, r_sum = [place(f"row{n}", [T], at_a2 + (2 + n) * KB2) for n in range(4)]
        ml_a, ml_b, gm_a, gm_b = [place(f"tile{n}", [T], at_a2 + (2 + n) * KB2) for n in range(4)]
        g_col = place("g_col", [TB, H1], at_a2 + 6 * KB2)
        small = place("small", [16, TB], at_a2 + 6 * KB2 + 64)
        y_tmp = place("y_tmp", [T], at_a2 + 7 * KB2)


        par2 = place("par2", [P2_N], at_par)
        xn = place("xn", [TB, D], at_b)
        x_rows = place("x_rows", [2, D], at_b + 8 * KB2)
        xe_hi = place("xe_hi", [KC, P], at_b + 12 * KB2, F32R)
        xe_lo = place("xe_lo", [KC, P], at_b + 14 * KB2, F32R)
        gate = place("gate", [FE], at_b + 16 * KB2)
        hid = place("hid", [FE], at_b + 17 * KB2)
        hid_hi = place("hid_hi", [4, P], at_b + 18 * KB2, F32R)
        hid_lo = place("hid_lo", [4, P], at_b + 19 * KB2, F32R)
        y_rows = place("y_rows", [2, D], at_b + 20 * KB2)
        w_hi_more = place("w_hi_more", [2, UNIT], at_a, F32R)
        w_lo_more = place("w_lo_more", [2, UNIT], at_a + 2 * UNIT * 4, F32R)

        def hi_slot(c):
            return w_hi[:, c % 4] if c % 4 < 2 else w_hi_more[:, c % 4 - 2]

        def lo_slot(c):
            return w_lo[:, c % 4] if c % 4 < 2 else w_lo_more[:, c % 4 - 2]

        wr_hi = place("wr_hi", [KC, 36], at_b + 24 * KB2, F32R)
        wr_lo = place("wr_lo", [KC, 36], at_b + 24 * KB2 + 1152, F32R)
        logit_t = place("logit_t", [T], at_b + 16 * KB2)
        at_r = [at_a2]

        def overflowing(eng):
            eng.wait_ge(dest_ready, 1)
            return eng.value_load(over_int[0:1, N_OVER:N_OVER + 1]) > 0

        def tiny(name, shape, dt=F32):
            t = place(name, shape, at_r[0], dt)
            at_r[0] += -(-int(np.prod(shape)) * 4 // 32) * 32
            assert at_r[0] <= at_b
            return t

        rms2 = tiny("rms2", [8, TB])
        logit, gap = tiny("logit", [TB, 36]), tiny("gap", [TB, EG])
        in_group, chosen = tiny("in_group", [TB, EG]), tiny("chosen", [TB, EG, PER])
        le1, le2 = tiny("le1", [TB, PER]), tiny("le2", [TB, PER])
        first, second = tiny("first", [TB, PER]), tiny("second", [TB, PER])
        best = tiny("best", [8, TB])
        weight = tiny("weight", [2, TB])
        owns = tiny("owns", [2, TB, NE])
        both, row, lift = tiny("both", [TB, NE]), tiny("row", [TB, NE]), tiny("lift", [TB, NE])
        blocks, over = tiny("blocks", [TB, NE]), tiny("over", [TB, NE])
        n_over, over_end, over_start = tiny("n_over", [NE]), tiny("over_end", [NE]), tiny("over_start", [NE])
        over_cmp, over_e = tiny("over_cmp", [8, NE]), tiny("over_e", [8])
        over_int = tiny("over_int", [16], I32)
        so_far, before_all = tiny("so_far", [TB, NE]), tiny("before_all", [TB, NE])
        dest_f, dest = tiny("dest_f", [2, TB]), tiny("dest", [2, TB], I32)
        pairs = tiny("pairs", [TB, 2, 2], I32)
        slots = tiny("slots", [NE + 1, 2], I32)
        over_slots = tiny("over_slots", [8, 2], I32)
        y_pairs = place("y_pairs", [TB, 2, D], at_a)

        MAIN = P * NE
        N_OVER = 8
        NO_PAIR = 4096
        token_rows = nc.dram_tensor("token_rows", [T, D], F32, kind="Internal").ap()
        pair_rows = nc.dram_tensor("pair_rows", [2 * T, D], F32, kind="Internal").ap()
        slot_table = nc.dram_tensor("slot_table", [MAIN + N_OVER * P, 2], I32, kind="Internal").ap()
        hs = place("hs", [KC, T], at_res)

        over_weights = place("over_weights", [4, UNIT], at_a)
        over_xe = place("over_xe", [KC, P], at_b + 12 * KB2)
        over_hidt = place("over_hidt", [4, P], at_b + 18 * KB2)

        no_pairs = place("no_pairs", [80], at_x, I32)
        y_mark = place("y_mark", [8], at_x + 320, I32)

        par3 = place("par3", [P3_N], at_par)
        sq = [place(f"sq{n}", [T], at_a2 + n * KB2) for n in range(2)]
        rms = place("rms", [T], at_a2 + 2 * KB2)
        u_tmp = [place(f"u_tmp{n}", [T], at_a2 + (3 + n) * KB2) for n in range(3)]
        o_hi = place("o_hi", [HH, T], at_b, F32R)
        o_lo = place("o_lo", [HH, T], at_b + 8 * KB2, F32R)
        fx = place("fx", [2, T], at_b + 16 * KB2)
        key = place("key", [2, T], at_b + 18 * KB2)
        run = place("run", [2, T], at_b + 20 * KB2)
        qry = place("qry", [2, T], at_b + 22 * KB2)
        far_q = place("far_q", [T], at_b + 24 * KB2)
        far_k = place("far_k", [T], at_b + 25 * KB2)
        o_raw = place("o_raw", [HH, T], at_b)
        o_tmp = place("o_tmp", [HH, T], at_b + 8 * KB2)
        val = place("val", [TB, 256], at_b + 26 * KB2)
        ws = place("ws", [TB, T], at_a2)
        k_dec = [place(f"k_dec{n}", [T], at_a2 + (4 + 2 * n) * KB2) for n in range(2)]
        q_dec = [place(f"q_dec{n}", [T], at_a2 + (5 + 2 * n) * KB2) for n in range(2)]
        b_exp = place("b_exp", [2], at_x + 352)
        turn = place("turn", [8], at_x + 576)
        lbs = [place(f"lbs{n}", [KC], at_x + 384 + 32 * n) for n in range(6)]
        hid2_hi = place("hid2_hi", [FA, T], at_b, F32R)
        hid2_lo = place("hid2_lo", [FA, T], at_b + FA * KB2, F32R)
        f_gate = [place(f"f_gate{n}", [T], at_a2 + (4 + n) * KB2) for n in range(2)]
        f_hid = [place(f"f_hid{n}", [T], at_a2 + (6 + n) * KB2) for n in range(2)]
        prob = place("prob", [8192], at_b)
        vals = place("vals", [3, TB, AH * P], at_b + 16 * KB2)
        q_rot = [place(f"q_rot{n}", [T], at_a2 + n * KB2) for n in range(2)]
        k_rot = [place(f"k_rot{n}", [T], at_a2 + (2 + n) * KB2) for n in range(2)]
        r_cos = [place(f"r_cos{n}", [T], at_a2 + (4 + n) * KB2) for n in range(2)]
        r_sin = [place(f"r_sin{n}", [T], at_a2 + (6 + n) * KB2) for n in range(2)]
        ao_hi = place("ao_hi", [3 * AH, T], at_a, F32R)
        ao_lo = place("ao_lo", [3 * AH, T], at_a + 3 * AH * KB2, F32R)
        at_stat = at_par + P3_COLS["levels"][0] * 4
        at_stat += -at_stat % 32
        stat = [place(f"stat{g}", [TB, 8], at_stat + 128 * g) for g in range(3)]
        stat_nat = [place(f"stat_nat{g}", [TB, 8], at_stat + 384 + 128 * g) for g in range(3)]
        share = place("share", [3, TB, AH], at_stat + 768)
        share_g = [place(f"share_g{g}", [TB, AH], at_stat + 960 + 64 * g) for g in range(3)]
        top = place("top", [TB, AH], at_stat + 1152)
        den = place("den", [TB, AH], at_stat + 1216)
        out_tile = [place(f"out_tile{n}", [D], at_b + 2 * n * KB2) for n in range(2)]
        out_sq = place("out_sq", [T], at_b + 4 * KB2)
        out_rms = place("out_rms", [8, TB], at_b + 5 * KB2)
        stat_rows = nc.dram_tensor("stat_rows", [2, T, 8], F32, kind="Internal").ap()
        share_rows = nc.dram_tensor("share_rows", [2, T, AH], F32, kind="Internal").ap()

        def prob_of(g, h):
            width = (256, P, P)[g]
            at = h * 1024 if g == 0 else 4096 + (g - 1) * 2048 + h * 512
            return prob[:, at:at + TB * width].rearrange("p (b s) -> p b s", b=TB)

        def group_order(ap, g):
            return ap.rearrange("q (r p) -> q p r", r=STEP[g])

        def natural_order(ap, g):
            return ap.rearrange("q (p r) -> q p r", r=STEP[g])

        def head_of(tile, p, hh):
            return tile[:, bass.ds(p * 2 + hh, 1)].rearrange("p h t -> p (h t)")

        lb_tile = cols(par3, P3_COLS, "lb")
        HG_STEPS = 2 + 2 * 2 + 2
        PROJ_ATTN = 4 * (HH // 2) + FC

        def norm_bank(k):
            return bank[0 if k else 7]

        def query_part(pool, p, hh, n):
            w = 64 >> n
            pool.wait_ge(lev_exp, p * 14 + (7 * hh + n + 1))
            if n >= 2:
                pool.wait_ge(lev_ready, p * 16 + (8 * hh + n - 1))

            def view(ap):
                return ap.rearrange("p (n t) -> p n t", t=2 * w)[:, :, w:]
            nc.gpsimd.tensor_tensor(view(q_dec[n % 2][:]), view(fx[:, n % 2]), view(qry[:, hh]), ALU.mult).then_inc(q_ready, 1)

        bank = [ctx.enter_context(nc.psum_tensor(f"bank{n}", [P, T], F32)) for n in range(8)]

        raw_landed = [sem(f"raw_landed{n}") for n in range(RAW)]
        hi_ready, lo_ready, unit_used = sem("hi_ready"), sem("lo_ready"), sem("unit_used")
        x_landed, con_landed, params_landed = sem("x_landed"), sem("con_landed"), sem("params_landed")
        act_step, dve_step = sem("act_step"), sem("dve_step")
        out_stored = [sem("out_stored0"), sem("out_stored1")]
        sq_ready, rms_arg, root_ready, xs_ready = sem("sq_ready"), sem("rms_arg"), sem("root_ready"), sem("xs_ready")
        turned, u_hi_ready, u_lo_ready = sem("turned"), sem("u_hi_ready"), sem("u_lo_ready")
        narrow_hi, narrow_lo, gates_ready = sem("narrow_hi"), sem("narrow_lo"), sem("gates_ready")
        in_ready, in_conv, in_act, qk_ready = sem("in_ready"), sem("in_conv"), sem("in_act"), sem("qk_ready")
        soft_arg, soft_log, rows_ready, em_ready = sem("soft_arg"), sem("soft_log"), sem("rows_ready"), sem("em_ready")
        g_turned, g_col_ready = sem("g_turned"), sem("g_col_ready")
        vg_ready, wsp_ready = sem("vg_ready"), sem("wsp_ready")
        m_spread, s_ready, dec_arg, dec_ready, s_weighted = (sem("m_spread"), sem("s_ready"), sem("dec_arg"),
                                                             sem("dec_ready"), sem("s_weighted"))
        num_ready, nq_abs, h_ready, h_sq, h_ss, h_root, ym_ready, ym_hi = [
            sem(n) for n in ("num_ready", "nq_abs", "h_ready", "h_sq", "h_ss", "h_root", "ym_ready", "ym_hi")]
        mix_ready, gated_ready, gated_sq, gated_ss, gated_root, yg_ready, yg_hi, y_lo_ready = [
            sem(n) for n in ("mix_ready", "gated_ready", "gated_sq", "gated_ss", "gated_root", "yg_ready", "yg_hi",
                             "y_lo_ready")]
        out1_ready, res1_ready = sem("out1_ready"), sem("res1_ready")


        xn_ready, tokens_stored = sem("xn_ready"), sem("tokens_stored")
        logits_ready, logits_copied = sem("logits_ready"), sem("logits_copied")
        router_arg, router_exp = sem("router_arg"), sem("router_exp")
        owns_ready, before_ready, dest_ready = sem("owns_ready"), sem("before_ready"), sem("dest_ready")
        table_written, slots_landed = sem("table_written"), sem("slots_landed")
        rows_set = sem("rows_set")
        x_gathered = [sem("x_gathered0"), sem("x_gathered1")]
        y_free = [sem("y_free0"), sem("y_free1")]
        xe_turned, xe_hi_ready, xe_lo_ready = sem("xe_turned"), sem("xe_hi_ready"), sem("xe_lo_ready")
        silu_ready, hid_ready, hid_turned, hid_hi_ready, hid_lo_ready = [
            sem(n) for n in ("silu_ready", "hid_ready", "hid_turned", "hid_hi_ready", "hid_lo_ready")]
        y_ready, res2_ready = sem("y_ready"), sem("res2_ready")
        y_landed = [sem(f"y_landed{b}") for b in range(TB)]
        h_turned, h0_ready = sem("h_turned"), sem("h0_ready")
        over_x, over_w, over_stored = sem("over_x"), sem("over_w"), sem("over_stored")
        over_products, over_copies, over_hid = sem("over_products"), sem("over_copies"), sem("over_hid")

        n_sq, n_sum, n_root, u_ready = sem("n_sq"), sem("n_sum"), sem("n_root"), sem("u_ready")
        h_added = sem("h_added")
        lb_arg, lb_exp, lb_ready = sem("lb_arg"), sem("lb_exp"), sem("lb_ready")
        proj_ready, f_sig, f_ready, f_log, run_ready = (sem("proj_ready"), sem("f_sig"), sem("f_ready"), sem("f_log"),
                                                        sem("run_ready"))
        q_taken, v_taken, g_taken = sem("q_taken"), sem("v_taken"), sem("g_taken")
        set_up, gap_to_ref, lev_exp, k_ready, q_ready = (sem("set_up"), sem("gap_to_ref"), sem("lev_exp"),
                                                         sem("k_ready"), sem("q_ready"))
        lev_ready, lev_taken = sem("lev_ready"), sem("lev_taken")
        far_exp, far_kq, far_ready, far_taken = sem("far_exp"), sem("far_kq"), sem("far_ready"), sem("far_taken")
        o_sum, o_sq, o_gated, o_ss, o_root, o_ready, o_hi_ready, o_lo_ready = [
            sem(n) for n in ("o_sum", "o_sq", "o_gated", "o_ss", "o_root", "o_ready", "o_hi_ready", "o_lo_ready")]
        f_silu, f_prod, f_hi, f_lo = sem("f_silu"), sem("f_prod"), sem("f_hi"), sem("f_lo")
        v_ready, rope_mul, rope_ready, sc_ready, sc_max, sc_gap, sc_exp, sc_sum = [
            sem(n) for n in ("v_ready", "rope_mul", "rope_ready", "sc_ready", "sc_max", "sc_gap", "sc_exp", "sc_sum")]
        order_stored, order_landed, share_arg, share_exp, share_ready = [
            sem(n) for n in ("order_stored", "order_landed", "share_arg", "share_exp", "share_ready")]
        p_ready, p_turned, pt_ready, ao_sum, ao_hi_ready, ao_lo_ready = [
            sem(n) for n in ("p_ready", "p_turned", "pt_ready", "ao_sum", "ao_hi_ready", "ao_lo_ready")]
        fin_turned, fin_ready = sem("fin_turned"), sem("fin_ready")
        block = ctx.enter_context(nc.Block())
        STREAM_END = N_UNITS

        @block.sync
        def _(sp):
            sp.dma_start(res[:], x_in.rearrange("(b p) d -> p b d", p=P)).then_inc(x_landed, 16)
            sp.dma_start(con[:], constants_in).then_inc(con_landed, 16)
            sp.dma_start(par1[:], phase1_in).then_inc(con_landed, 16)
            for n in range(RAW):
                sp.dma_start(raw[:, n], weights_in[n]).then_inc(raw_landed[n], 16)
            with sp.Fori(1, STREAM_END // RAW) as i:
                for j in range(RAW):
                    sp.wait_ge(lo_ready, i * RAW + (j + 1 - RAW))
                    sp.dma_start(raw[:, j], weights_in[bass.ds(i * RAW + j, 1)].rearrange("u p n -> p (u n)")) \
                        .then_inc(raw_landed[j], 16)

            for b in range(TB):
                sp.wait_ge(fin_ready, b + 1)
                sp.dma_start(out[b * P:(b + 1) * P, :], out_tile[b % 2][:]).then_inc(out_stored[b % 2], 16)
            for n in range(2):
                sp.wait_ge(out_stored[n], 32)

        @block.tensor
        def _(pe):
            def unit_wait(n):
                pe.wait_ge(hi_ready, n + 1)
                pe.wait_ge(lo_ready, n + 1)

            def product(out_ap, a_hi, a_lo, b_hi, b_lo, first, last):
                nc.tensor.matmul(out_ap, a_hi, b_hi, start=first, stop=False)
                nc.tensor.matmul(out_ap, a_hi, b_lo, start=False, stop=False)
                return nc.tensor.matmul(out_ap, a_lo, b_hi, start=False, stop=last)

            def feature_chunk(out_ap, s, m, after=None):
                for k in range(KC):
                    if after is not None:
                        normed(after, k)
                    w = slice(k * 256 + m * P, k * 256 + m * P + P)
                    mm = product(out_ap, w_hi[:, s, w], w_lo[:, s, w], u_hi[:, k], u_lo[:, k], k == 0, k == KC - 1)
                return mm

            def token_chunk(out_ap, s, tokens):
                for k in range(KC):
                    w = slice(k * 256, k * 256 + 256)
                    mm = product(out_ap, u_hi[:, k, tokens], u_lo[:, k, tokens], w_hi[:, s, w], w_lo[:, s, w],
                                 k == 0, k == KC - 1)
                return mm

            pe.wait_ge(con_landed, 32)
            pe.wait_ge(xs_ready, TB)
            for c in range(KC):
                if c >= 4:
                    pe.wait_ge(u_lo_ready, c - 3)
                for b in range(TB):
                    mm = nc.tensor.transpose(bank[c % 4][:, b * P:b * P + P], xs[:, b, c * P:c * P + P], ident)
                mm.then_inc(turned, 1)

            pe.wait_ge(narrow_lo, 1)
            pe.wait_ge(u_hi_ready, KC)
            pe.wait_ge(u_lo_ready, KC)
            for k in range(KC):
                mm = product(bank[4][:], wif_hi[:, k], wif_lo[:, k], u_hi[:, k], u_lo[:, k], k == 0, k == KC - 1)
            mm.then_inc(gates_ready, 1)

            def slot_free(q):
                old = q - 4
                if old >= 8:
                    pe.wait_ge(in_act, old - 7)
                elif old >= 0:
                    pe.wait_ge(in_conv, old + 1)

            for n in range(N_IN):
                unit_wait(n)
                if n in (4, 5, 10, 11):
                    for half in range(2):
                        q = 2 * n + half
                        slot_free(q)
                        for b in range(2):
                            tokens = slice((2 * half + b) * P, (2 * half + b) * P + P)
                            mm = token_chunk(bank[q % 4][:, b * 256:b * 256 + 256], n % 2, tokens)
                            if b == 0:
                                continue
                            if half == 0:
                                mm.then_inc(in_ready, 1)
                            else:
                                mm.then_inc(unit_used, 1)
                else:
                    for m in range(2):
                        q = 2 * n + m
                        slot_free(q)
                        mm = feature_chunk(bank[q % 4][:], n % 2, m)
                        mm.then_inc(in_ready if m == 0 else unit_used, 1)

            pe.wait_ge(rows_ready, 1)
            for b in range(TB):
                mm = nc.tensor.transpose(bank[4][:, b * H1:b * H1 + H1], r_i[0:H1, b * P:b * P + P], ident[0:H1, 0:H1])
            mm.then_inc(g_turned, 1)

            pe.wait_ge(in_act, 16)
            pe.wait_ge(qk_ready, KC)
            pe.wait_ge(vg_ready, TB)
            pe.wait_ge(wsp_ready, 1)
            sel = cols(con, C_COLS, "sel")

            def scores(h):
                if h:
                    pe.wait_ge(s_weighted, 3 * h)
                nc.tensor.matmul(bank[0][:], sel[0:H1, h * P:h * P + P], neg_m[0:H1, :], start=True, stop=True) \
                    .then_inc(m_spread, 1)
                for j in range(TB):
                    at = (bank[1][:], bank[2][:, 0:384], bank[3][:, 0:256], bank[3][:, 256:384])[j]
                    mm = nc.tensor.matmul(at, qk[:, 4 + h, j * P:j * P + P], qk[:, h, j * P:], start=True, stop=True)
                mm.then_inc(s_ready, 1)

            def mixing(h):
                if h:
                    pe.wait_ge(gated_root, h)
                for b in range(TB):
                    for g in range(2):
                        mm = nc.tensor.matmul(bank[7][64 * g:64 * g + 64, b * P:b * P + P],
                                              vg[:, b, h * P + 64 * g:h * P + 64 * g + 64],
                                              cols(par1, P1_COLS, "w_sp")[:, (2 * h + g) * P:(2 * h + g + 1) * P],
                                              start=True, stop=True)
                mm.then_inc(mix_ready, 1)

            scores(0)
            mixing(0)
            pe.wait_ge(em_ready, 1)
            for h in range(H1):
                pe.wait_ge(s_weighted, 3 * h + 3)
                if h:
                    pe.wait_ge(h_root, h)
                for j in range(TB):
                    nc.tensor.matmul(bank[4][:, j * P:], vm[:, j, h * P:h * P + P], dec[:, j, j * P:],
                                     start=j == 0, stop=j == TB - 1)
                for j in range(TB):
                    nc.tensor.matmul(bank[5][:, j * P:], ones, dec[:, j, j * P:], start=j == 0, stop=j == TB - 1)
                nc.tensor.matmul(bank[6][:], sel[0:H1, h * P:h * P + P], e_neg_m[0:H1, :], start=True, stop=True) \
                    .then_inc(num_ready, 1)
                if h + 1 < H1:
                    scores(h + 1)
                pe.wait_ge(gated_sq, h + 1)
                nc.tensor.matmul(bank[7][:], cols(con, C_COLS, "blocks64"), gm_b[:], start=True, stop=True) \
                    .then_inc(gated_ss, 1)
                if h + 1 < H1:
                    mixing(h + 1)
                pe.wait_ge(h_sq, h + 1)
                nc.tensor.matmul(bank[6][:], ones, ml_b[:], start=True, stop=True).then_inc(h_ss, 1)

            pe.wait_ge(y_lo_ready, 8)
            pe.wait_ge(h_root, H1)
            pe.wait_ge(gated_root, H1)
            for half in range(2):
                for part in range(2):
                    n = U_OUT + 2 * half + part
                    unit_wait(n)
                    for b in range(TB):
                        for k in range(4):
                            y = (4 * part + k, slice(b * P, b * P + P))
                            w = slice(k * 512, k * 512 + 512)
                            mm = product(bank[4 * half + b][:], u_hi[:, y[0], y[1]], u_lo[:, y[0], y[1]],
                                         w_hi[:, n % 2, w], w_lo[:, n % 2, w], part == 0 and k == 0,
                                         part == 1 and k == 3)
                    mm.then_inc(unit_used, 1)


            pe.wait_ge(xn_ready, TB)
            for c in range(KC):
                if c >= 4:
                    pe.wait_ge(u_lo_ready, KC + c - 3)
                for b in range(TB):
                    mm = nc.tensor.transpose(bank[c % 4][:, b * P:b * P + P], xn[:, b, c * P:c * P + P], ident)
                mm.then_inc(turned, 1)
            pe.wait_ge(narrow_hi, 2)
            pe.wait_ge(narrow_lo, 2)
            pe.wait_ge(u_hi_ready, 2 * KC)
            pe.wait_ge(u_lo_ready, 2 * KC)
            for k in range(KC):
                mm = product(bank[4][0:36, :], wr_hi[:, k], wr_lo[:, k], u_hi[:, k], u_lo[:, k], k == 0, k == KC - 1)
            mm.then_inc(logits_ready, 1)
            pe.wait_ge(logits_copied, 1)
            for b in range(TB):
                mm = nc.tensor.transpose(bank[6][:, b * 36:b * 36 + 36], logit_t[0:36, b * P:b * P + P], ident[0:36, 0:36])
            mm.then_inc(logits_ready, 1)
            pe.wait_ge(owns_ready, 1)
            everyone = both[:].rearrange("p b e -> p (b e)")
            nc.tensor.matmul(bank[5][:, 0:TB * NE], cols(con, C_COLS, "strict"), everyone, start=True, stop=True)
            nc.tensor.matmul(bank[5][:, TB * NE:2 * TB * NE], ones, everyone, start=True, stop=True).then_inc(before_ready, 1)

            def turn_rows(b):
                for c in range(KC):
                    mm = nc.tensor.transpose(bank[c // 4][:, (c % 4) * P:(c % 4) * P + P],
                                             x_rows[:, b, c * P:c * P + P], ident)
                mm.then_inc(xe_turned, 1)

            def up_units(b, wait):
                for j in range(4):
                    wait(j)
                    hi, lo = hi_slot(PER_EXPERT * b + j), lo_slot(PER_EXPERT * b + j)
                    for k in range(4):
                        c = 4 * (j % 2) + k
                        w = slice(k * FE, k * FE + FE)
                        mm = product(bank[2 + j // 2][:], xe_hi[:, c], xe_lo[:, c], hi[:, w], lo[:, w], c == 0, c == KC - 1)
                    mm.then_inc(unit_used, 1)

            def turn_hidden():
                for c in range(4):
                    mm = nc.tensor.transpose(bank[4][:, c * P:c * P + P], hid[:, c * P:c * P + P], ident)
                mm.then_inc(hid_turned, 1)

            def down_units(b, wait):
                for j in range(4, 6):
                    wait(j)
                    hi, lo = hi_slot(PER_EXPERT * b + j), lo_slot(PER_EXPERT * b + j)
                    for k in range(2):
                        c = 2 * (j - 4) + k
                        for half in range(2):
                            w = slice(k * D + half * 512, k * D + half * 512 + 512)
                            mm = product(bank[5 + half][:], hid_hi[:, c], hid_lo[:, c], hi[:, w], lo[:, w], c == 0, c == 3)
                    mm.then_inc(unit_used, 1)

            pe.wait_ge(dest_ready, 1)
            pe.wait_ge(x_gathered[0], 16)
            turn_rows(0)
            with pe.Fori(0, NE // 2) as i:
                for b in range(2):
                    n0 = U_MOE + PER_EXPERT * b
                    e = i * 2 + b

                    def wait(j):
                        pe.wait_ge(hi_ready, i * (2 * PER_EXPERT) + (n0 + j + 1))
                        pe.wait_ge(lo_ready, i * (2 * PER_EXPERT) + (n0 + j + 1))

                    pe.wait_ge(xe_hi_ready, e + 1)
                    pe.wait_ge(xe_lo_ready, e + 1)
                    up_units(b, wait)
                    pe.wait_ge(hid_ready, e + 1)
                    turn_hidden()
                    pe.wait_ge(x_gathered[1 - b], i * 16 + 16 * (b + 1))
                    turn_rows(1 - b)
                    pe.wait_ge(hid_hi_ready, e + 1)
                    pe.wait_ge(hid_lo_ready, e + 1)
                    down_units(b, wait)

            with pe.If(overflowing(pe)):
                with pe.Fori(0, N_OVER) as v:
                    pe.wait_ge(over_x, v * 16 + 16)
                    for c in range(KC):
                        mm = nc.tensor.transpose(bank[c // 4][:, (c % 4) * P:(c % 4) * P + P],
                                                 x_rows[:, 0, c * P:c * P + P], ident)
                    mm.then_inc(over_products, 1)
                    pe.wait_ge(over_w, v * 32 + 16)
                    pe.wait_ge(over_copies, v * 4 + 1)
                    for j in range(4):
                        for k in range(4):
                            c = 4 * (j % 2) + k
                            mm = nc.tensor.matmul(bank[2 + j // 2][:], over_xe[:, c], over_weights[:, j, k * FE:k * FE + FE],
                                                  start=c == 0, stop=c == KC - 1)
                    mm.then_inc(over_products, 1)
                    pe.wait_ge(over_hid, v + 1)
                    for c in range(4):
                        mm = nc.tensor.transpose(bank[4][:, c * P:c * P + P], hid[:, c * P:c * P + P], ident)
                    mm.then_inc(over_products, 1)
                    pe.wait_ge(over_w, v * 32 + 32)
                    pe.wait_ge(over_copies, v * 4 + 3)
                    for c in range(4):
                        for half in range(2):
                            w = (c % 2) * D + half * 512
                            mm = nc.tensor.matmul(bank[5 + half][:], over_hidt[:, c], over_weights[:, c // 2, w:w + 512],
                                                  start=c == 0, stop=c == 3)
                    mm.then_inc(over_products, 1)
            pe.wait_ge(xn_ready, 2 * TB)
            for c in range(KC):
                if c >= 4:
                    pe.wait_ge(h0_ready, c - 3)
                for b in range(TB):
                    mm = nc.tensor.transpose(bank[c % 4][:, b * P:b * P + P], xn[:, b, c * P:c * P + P], ident)
                mm.then_inc(h_turned, 1)


            def norm(k):
                at = norm_bank(k)
                for c in range(KC):
                    pe.wait_ge(n_sq, KC * k + c + 1)
                    nc.tensor.matmul(at[:], ones, sq[c % 2][:], start=c == 0, stop=c == KC - 1).then_inc(n_sum, 1)

            def normed(k, c):
                pe.wait_ge(u_hi_ready, (2 + k) * KC + c + 1)
                pe.wait_ge(u_lo_ready, (2 + k) * KC + c + 1)

            def out_rows(n0, n_chunks, src_hi, src_lo):
                for half in range(2):
                    for q in range(-(-n_chunks // 4)):
                        n = n0 + half * -(-n_chunks // 4) + q
                        unit_wait(n)
                        for d in range(4):
                            for k in range(min(4, n_chunks - 4 * q)):
                                c = 4 * q + k
                                w = slice(k * 512 + d * P, k * 512 + d * P + P)
                                mm = product(bank[4 * half + d][:], w_hi[:, n % 2, w], w_lo[:, n % 2, w], src_hi[:, c],
                                             src_lo[:, c], c == 0, c == n_chunks - 1)
                        mm.then_inc(unit_used, 1)

            norm(0)
            with pe.Fori(0, HH // 2) as p:
                for j in range(4):
                    pe.wait_ge(hi_ready, p * 4 + (U_HG + j + 1))
                    pe.wait_ge(lo_ready, p * 4 + (U_HG + j + 1))
                    if j == 1:
                        pe.wait_ge(f_sig, p * 2 + 1)
                    if j == 2:
                        pe.wait_ge(f_ready, p * 2 + 2)
                    if j == 3:
                        pe.wait_ge(q_taken, p * 2 + 2)
                    for half in range(2):
                        out_bank = bank[(2 * j + half) % 4]
                        if j == 2:
                            for b in range(2):
                                tokens = slice((2 * half + b) * P, (2 * half + b) * P + P)
                                mm = token_chunk(out_bank[:, b * 256:b * 256 + 256], j % 2, tokens)
                        else:
                            mm = feature_chunk(out_bank[:], j % 2, half, 0 if (j, half) == (0, 0) else None)
                        mm.then_inc(proj_ready if half == 0 else unit_used, 1)
                    if j >= 2:
                        pe.wait_ge(far_kq, p * 2 + (j - 1))
                        if j == 2:
                            pe.wait_ge(set_up, 5)
                        if j == 3:
                            pe.wait_ge(far_taken, p * 2 + 1)
                        nc.tensor.matmul(bank[6][:, 0:128], far_k[:, 0:128], far_q[:, 0:128], start=True, stop=True)
                        nc.tensor.matmul(bank[6][:, 128:384], far_k[:, 384:512], far_q[:, 128:384], start=True, stop=True)
                        nc.tensor.matmul(bank[7][:, 0:256], far_k[:, 128:256], far_q[:, 128:384], start=True, stop=True)
                        nc.tensor.matmul(bank[7][:, 256:384], far_k[:, 256:384], far_q[:, 384:512], start=True, stop=True)                             .then_inc(far_ready, 1)

                def head_square(hh):
                    pe.wait_ge(o_sq, p * 2 + (hh + 1))
                    pe.wait_ge(o_gated, p * 2 + (hh + 1))
                    nc.tensor.matmul(bank[2 + hh][:], ones, (far_q, far_k)[hh][:], start=True, stop=True).then_inc(o_ss, 1)

                for hh in range(2):
                    for n in range(8):
                        if n < 7:
                            pe.wait_ge(k_ready, p * 14 + (7 * hh + n + 1))
                            pe.wait_ge(q_ready, p * 14 + (7 * hh + n + 1))
                        if n >= 2:
                            pe.wait_ge(lev_taken, p * 16 + (8 * hh + n - 1))
                        for b in range(TB):
                            t = slice(b * P, b * P + P)
                            left, right = (k_dec[n % 2][:, t], q_dec[n % 2][:, t]) if n < 7 else (key[:, hh, t], qry[:, hh, t])
                            mm = nc.tensor.matmul(bank[4 + n % 2][:, t], left, right, start=True, stop=True)
                        mm.then_inc(lev_ready, 1)
                        if hh == 1 and n == 1:
                            head_square(0)
                    pe.wait_ge(lev_taken, p * 16 + (8 * hh + 8))
                    pe.wait_ge(far_taken, p * 2 + (hh + 1))
                    if hh == 0:
                        pe.wait_ge(v_taken, p * 2 + 2)
                    for b in range(TB):
                        mm = nc.tensor.matmul(bank[hh][:, b * P:], val[:, b, hh * P:hh * P + P], ws[:, b, 0:T - b * P],
                                              start=b == 0, stop=b == TB - 1)
                    mm.then_inc(o_sum, 1)
                head_square(1)
            pe.wait_ge(o_hi_ready, HH)
            pe.wait_ge(o_lo_ready, HH)
            out_rows(U_HGO, HH, o_hi, o_lo)

            def ffn(l, u0):
                norm(1 + 2 * l)

                def unit(n, done, i=None):
                    def at(v):
                        return v if i is None else i * 4 + v
                    s = n % 2
                    pe.wait_ge(hi_ready, at(n + 1))
                    pe.wait_ge(lo_ready, at(n + 1))
                    if not (l == 0 and done < 2 and i is None):
                        pe.wait_ge(f_prod, at(done - 1))
                    feature_chunk(bank[2 * s][:], s, 0, 1 + 2 * l if n == u0 and i is None else None).then_inc(proj_ready, 1)
                    feature_chunk(bank[2 * s + 1][:], s, 1).then_inc(unit_used, 1)

                base = l * FC
                pe.wait_ge(h_added, 8 + 24 * l)
                for j in range(4):
                    unit(u0 + j, base + j)
                with pe.Fori(1, FA // 4) as i:
                    for j in range(4):
                        unit(u0 + j, base + j, i)
                pe.wait_ge(f_hi, base + FA)
                pe.wait_ge(f_lo, base + FA)
                out_rows(u0 + FA, FA, hid2_hi, hid2_lo)
                pe.wait_ge(h_added, 16 + 24 * l)
                u1 = u0 + FA + 6
                with pe.Fori(0, 2) as i:
                    for j in range(4):
                        unit(u1 + j, base + FA + j, i)
                for j in range(8, FC - FA):
                    unit(u1 + j, base + FA + j)
                pe.wait_ge(f_hi, base + FC)
                pe.wait_ge(f_lo, base + FC)
                out_rows(u1 + FC - FA, FC - FA, hid2_hi, hid2_lo)

            ffn(0, U_FF0)

            norm(2)
            pe.wait_ge(h_added, 24)

            def tokens_of(tile, k, g, b):
                if g == 0:
                    return tile[:, k, b * P:b * P + P]
                return tile[:, k].rearrange("q (p r) -> q r p", r=STEP[g])[:, b]

            for g in range(3):
                for half in range(2):
                    n = U_QKV + 6 * g + half
                    unit_wait(n)
                    if g or half:
                        pe.wait_ge(v_ready, 2 * (2 * g + half))
                    if g:
                        pe.wait_ge(rope_mul, 8 * g)
                    for b in range(TB):
                        for k in range(KC):
                            if (g, half, b) == (0, 0, 0):
                                normed(2, k)
                            w = slice(k * 256, k * 256 + 256)
                            mm = product(bank[b // 2][:, b % 2 * 256:b % 2 * 256 + 256], tokens_of(u_hi, k, g, b),
                                         tokens_of(u_lo, k, g, b), w_hi[:, n % 2, w], w_lo[:, n % 2, w], k == 0, k == KC - 1)
                    mm.then_inc(unit_used, 1)
                for pair in range(2):
                    first_chunk = 8 * g + 4 * pair
                    for kind in range(2):
                        n = U_QKV + 6 * g + 2 + 2 * pair + kind
                        unit_wait(n)
                        if kind == 0:
                            pe.wait_ge(v_ready, 4 * (g + 1))
                        if first_chunk:
                            pe.wait_ge(rope_mul, first_chunk - 2 + 2 * kind)
                        feature_chunk(bank[2 * kind][:], n % 2, 0).then_inc(proj_ready, 1)
                        feature_chunk(bank[2 * kind + 1][:], n % 2, 1).then_inc(unit_used, 1)
                    for half in range(2):
                        m = AH * g + 2 * pair + half
                        pe.wait_ge(rope_ready, first_chunk + 4)
                        if m >= 2:
                            pe.wait_ge(sc_max, m - 1)
                        at = 4 + 2 * (m % 2)
                        for b in range(TB):
                            q = q_rot[half][:, b * P:b * P + P]
                            if g == 0:
                                s0 = max(b - 1, 0) * P
                                mm = nc.tensor.matmul(bank[at + b // 2][:, b % 2 * 256:b % 2 * 256 + 256], q,
                                                      k_rot[half][:, s0:s0 + 256], start=True, stop=True)
                            else:
                                mm = nc.tensor.matmul(bank[at][:, b * P:b * P + P], q, k_rot[half][:, b * P:b * P + P],
                                                      start=True, stop=True)
                        mm.then_inc(sc_ready, 1)
            pe.wait_ge(sc_max, 3 * AH)
            for m in range(3 * AH):
                g, h = m // AH, m % AH
                at = 4 * (m % 2)
                pe.wait_ge(p_ready, m + 1)
                if m >= 2:
                    pe.wait_ge(ao_lo_ready, m - 1)
                pr = prob_of(g, h)
                tiles = [(b, s) for b in range(TB) for s in range(2 if g == 0 and b else 1)]
                for n, (b, s) in enumerate(tiles):
                    mm = nc.tensor.transpose(bank[at + n // 4][:, n % 4 * P:n % 4 * P + P], pr[:, b, s * P:s * P + P], ident)
                mm.then_inc(p_turned, 1)
                pe.wait_ge(pt_ready, m + 1)
                flat = pr.rearrange("p b s -> p (b s)")
                for n, (b, s) in enumerate(tiles):
                    from_block = b - 1 + s if g == 0 and b else b
                    mm = nc.tensor.matmul(bank[at + 2][:, b * P:b * P + P], vals[:, g, from_block, h * P:h * P + P],
                                          flat[:, n * P:n * P + P], start=s == 0, stop=s == 1 or not (g == 0 and b))
                mm.then_inc(ao_sum, 1)
            pe.wait_ge(ao_hi_ready, 3 * AH)
            pe.wait_ge(ao_lo_ready, 3 * AH)
            out_rows(U_AO, 3 * AH, ao_hi, ao_lo)

            ffn(1, U_FF1)
            pe.wait_ge(h_added, 48)
            for b in range(TB):
                for c in range(KC):
                    mm = nc.tensor.transpose(bank[2 * b + c // 4][:, c % 4 * P:c % 4 * P + P], hs[:, c, b * P:b * P + P], ident)
                mm.then_inc(fin_turned, 1)

        @block.scalar
        def _(act):
            steps = Count(act_step)

            def chain(instruction):
                act.wait_ge(act_step, steps.mark(instruction))

            def split(n):
                act.wait_ge(raw_landed[n % RAW], 16 * (n // RAW + 1))
                if n >= 2:
                    act.wait_ge(unit_used, n - 1)
                nc.scalar.activation(w_hi[:, n % 2], raw[:, n % RAW], ACT.Copy).then_inc(hi_ready, 1)

            act.wait_ge(x_landed, 16)
            for b in range(TB):
                if b:
                    act.wait_ge(sq_ready, b)
                nc.scalar.activation(junk[:], res[:, b], ACT.Square, accum_out=small[:, 0, b:b + 1]).then_inc(sq_ready, 1)
            act.wait_ge(rms_arg, 1)
            nc.scalar.activation(small[:, 2], small[:, 1], ACT.Sqrt).then_inc(root_ready, 1)
            act.wait_ge(con_landed, 32)
            nc.scalar.activation(wif_hi[:], cols(par1, P1_COLS, "w_if").rearrange("p (k c) -> p k c", k=KC), ACT.Copy) \
                .then_inc(narrow_hi, 1)
            split(0)
            for c in range(KC):
                act.wait_ge(turned, c + 1)
                nc.scalar.activation(u_hi[:, c], bank[c % 4][:], ACT.Copy,
                                     scale=cols(par1, P1_COLS, "n1g")[:, c:c + 1]).then_inc(u_hi_ready, 1)

            for n in range(N_IN):
                split(n + 1)
                for half in range(2):
                    q = 2 * n + half
                    ready = (in_ready, n + 1) if half == 0 else (unit_used, n + 1)
                    if q < 8:
                        act.wait_ge(in_conv, q + 1)
                        nc.scalar.activation(qk[:, q], qk[:, q], ACT.Silu).then_inc(qk_ready, 1)
                        continue
                    act.wait_ge(*ready)
                    if n in (4, 5):
                        dst = vg[:, 2 * half:2 * half + 2, (n - 4) * 256:(n - 4) * 256 + 256]
                        src, f = bank[q % 4][:].rearrange("p (b c) -> p b c", b=2), ACT.Gelu_apprx_tanh
                    elif n in (6, 7):
                        dst, src, f = ug[:, q - 12], bank[q % 4][:], ACT.Gelu_apprx_tanh
                    elif n in (8, 9):
                        dst, src, f = so[:, q - 16], bank[q % 4][:], ACT.Sigmoid
                    else:
                        dst = vm[:, 2 * half:2 * half + 2, (n - 10) * 256:(n - 10) * 256 + 256]
                        src, f = bank[q % 4][:].rearrange("p (b c) -> p b c", b=2), ACT.Copy
                    nc.scalar.activation(dst, src, f).then_inc(in_act, 1)
                if n == 1:
                    act.wait_ge(soft_arg, 1)
                    chain(nc.scalar.activation(r_e[0:H1, :], r_e[0:H1, :], ACT.Exp))
                    nc.scalar.activation(r_e[0:H1, :], r_e[0:H1, :], ACT.Ln, bias=1.0).then_inc(soft_log, 1)
                if n == 3:
                    act.wait_ge(rows_ready, 1)
                    nc.scalar.activation(e_neg_m[0:H1, :], e_neg_m[0:H1, :], ACT.Exp, scale=-1.0).then_inc(em_ready, 1)
                if n == 5:
                    act.wait_ge(in_act, 4)
                    for b in range(TB):
                        if b:
                            act.wait_ge(sq_ready, TB + b)
                        nc.scalar.activation(y_tmp[:], vg[:, b], ACT.Square, accum_out=small[:, 4, b:b + 1]) \
                            .then_inc(sq_ready, 1)
                if n == 7:
                    act.wait_ge(rms_arg, 2)
                    nc.scalar.activation(small[:, 6], small[:, 5], ACT.Sqrt).then_inc(root_ready, 1)

            for h in range(H1 + 1):
                if h:
                    if h >= 2:
                        act.wait_ge(y_lo_ready, 2 * h - 2)
                    act.wait_ge(num_ready, h)
                    nc.scalar.activation(ml_a[:], bank[5][:], ACT.Abs).then_inc(nq_abs, 1)
                    act.wait_ge(gated_ready, h)
                    nc.scalar.activation(gm_b[:], gm_a[:], ACT.Square).then_inc(gated_sq, 1)
                if h < H1:
                    act.wait_ge(dec_arg, 4 * h + 4)
                    for j in range(TB):
                        last = nc.scalar.activation(dec[:, j, j * P:], dec[:, j, j * P:], ACT.Exp)
                    last.then_inc(dec_ready, 1)
                if h:
                    act.wait_ge(gated_ss, h)
                    nc.scalar.activation(gm_b[:], bank[7][:], ACT.Sqrt, scale=1.0 / 64, bias=eps).then_inc(gated_root, 1)
                    act.wait_ge(h_ready, h)
                    nc.scalar.activation(ml_b[:], ml_a[:], ACT.Square).then_inc(h_sq, 1)
                    act.wait_ge(h_ss, h)
                    nc.scalar.activation(ml_b[:], bank[6][:], ACT.Sqrt, scale=1.0 / P, bias=eps).then_inc(h_root, 1)
                    act.wait_ge(yg_ready, h)
                    nc.scalar.activation(u_hi[:, 3 + h], gm_a[:], ACT.Copy).then_inc(yg_hi, 1)
                    act.wait_ge(ym_ready, h)
                    nc.scalar.activation(u_hi[:, h - 1], ml_a[:], ACT.Copy).then_inc(ym_hi, 1)
            for n in range(U_OUT, U_OUT + N_OUT):
                if n + 1 < STREAM_END:
                    split(n + 1)


            for b in range(TB):
                act.wait_ge(res1_ready, TB + b + 1)
                if b:
                    act.wait_ge(sq_ready, 2 * TB + b)
                nc.scalar.activation(y_rows[:, 0], res[:, b], ACT.Square, accum_out=rms2[:, 0, b:b + 1]).then_inc(sq_ready, 1)
            act.wait_ge(rms_arg, 3)
            nc.scalar.activation(rms2[:, 2], rms2[:, 1], ACT.Sqrt).then_inc(root_ready, 1)
            act.wait_ge(params_landed, 16)
            nc.scalar.activation(wr_hi[:], cols(par2, P2_COLS, "w_r").rearrange("p (k c) -> p k c", k=KC), ACT.Copy) \
                .then_inc(narrow_hi, 1)
            for c in range(KC):
                act.wait_ge(turned, KC + c + 1)
                nc.scalar.activation(u_hi[:, c], bank[c % 4][:], ACT.Copy).then_inc(u_hi_ready, 1)
            act.wait_ge(logits_ready, 1)
            nc.scalar.activation(logit_t[0:36, :], bank[4][0:36, :], ACT.Copy).then_inc(logits_copied, 1)
            act.wait_ge(router_arg, 1)
            nc.scalar.activation(gap[:], gap[:], ACT.Exp).then_inc(router_exp, 1)
            act.wait_ge(router_arg, 2)
            nc.scalar.activation(best[:, 5], best[:, 4], ACT.Exp).then_inc(router_exp, 1)

            def expert_tokens():
                nc.scalar.activation(xe_hi[:, 0:4], bank[0][:].rearrange("p (c t) -> p c t", c=4), ACT.Copy)
                nc.scalar.activation(xe_hi[:, 4:8], bank[1][:].rearrange("p (c t) -> p c t", c=4), ACT.Copy) \
                    .then_inc(xe_hi_ready, 1)

            def split_of(i, c):
                act.wait_ge(raw_landed[c % RAW], i * (16 * 2 * PER_EXPERT // RAW) + 16 * ((U_MOE + c) // RAW + 1))
                act.wait_ge(unit_used, i * (2 * PER_EXPERT) + (U_MOE + c - 3))
                nc.scalar.activation(hi_slot(c), raw[:, c % RAW], ACT.Copy).then_inc(hi_ready, 1)

            def expert_pair(i, last):
                for b in range(2):
                    e = i * 2 + b
                    u0 = i * (2 * PER_EXPERT) + (U_MOE + PER_EXPERT * b)
                    c0 = PER_EXPERT * b
                    end = last and b == 1
                    split_of(i, c0 + 4)
                    act.wait_ge(unit_used, u0 + 2)
                    nc.scalar.activation(gate[:], bank[2][:], ACT.Silu).then_inc(silu_ready, 1)
                    split_of(i, c0 + 5)
                    if not end:
                        split_of(i, c0 + 6)
                        split_of(i, c0 + 7)
                    act.wait_ge(hid_turned, e + 1)
                    nc.scalar.activation(hid_hi[:], bank[4][:].rearrange("p (c t) -> p c t", c=4), ACT.Copy)                         .then_inc(hid_hi_ready, 1)
                    act.wait_ge(xe_turned, e + 2)
                    expert_tokens()
                    if not end:
                        split_of(i, c0 + 8)
                    act.wait_ge(y_free[b], i * 16 + 16)
                    act.wait_ge(unit_used, u0 + 6)
                    nc.scalar.activation(y_rows[:, b, 0:512], bank[5][:], ACT.Copy)
                    nc.scalar.activation(y_rows[:, b, 512:1024], bank[6][:], ACT.Copy).then_inc(y_ready, 1)
                    if not end:
                        split_of(i, c0 + 9)

            split_of(0, 1)
            act.wait_ge(logits_ready, 1)
            split_of(0, 2)
            split_of(0, 3)
            act.wait_ge(xe_turned, 1)
            expert_tokens()
            with act.Fori(0, NE // 2 - 1) as i:
                expert_pair(i, False)
            expert_pair(NE // 2 - 1, True)
            split(U_HG)

            with act.If(overflowing(act)):
                with act.Fori(0, N_OVER) as v:
                    act.wait_ge(over_products, v * 4 + 1)
                    nc.scalar.activation(over_xe[:, 0:4], bank[0][:].rearrange("p (c t) -> p c t", c=4), ACT.Copy)
                    nc.scalar.activation(over_xe[:, 4:8], bank[1][:].rearrange("p (c t) -> p c t", c=4), ACT.Copy) \
                        .then_inc(over_copies, 1)
                    act.wait_ge(over_products, v * 4 + 2)
                    nc.scalar.activation(gate[:], bank[2][:], ACT.Silu).then_inc(over_copies, 1)
                    act.wait_ge(over_products, v * 4 + 3)
                    nc.scalar.activation(over_hidt[:], bank[4][:].rearrange("p (c t) -> p c t", c=4), ACT.Copy) \
                        .then_inc(over_copies, 1)
                    act.wait_ge(over_products, v * 4 + 4)
                    nc.scalar.activation(y_rows[:, 0, 0:512], bank[5][:], ACT.Copy)
                    nc.scalar.activation(y_rows[:, 0, 512:1024], bank[6][:], ACT.Copy).then_inc(over_copies, 1)
            for b in range(TB):
                act.wait_ge(res2_ready, b + 1)
                if b:
                    act.wait_ge(sq_ready, 3 * TB + b)
                nc.scalar.activation(x_rows[:, 0], res[:, b], ACT.Square, accum_out=rms2[:, 4, b:b + 1]).then_inc(sq_ready, 1)
            act.wait_ge(rms_arg, 4)
            nc.scalar.activation(rms2[:, 6], rms2[:, 5], ACT.Sqrt).then_inc(root_ready, 1)


            def norm(k, wait_chunk):
                for c in range(KC):
                    wait_chunk(c)
                    if c >= 2:
                        act.wait_ge(n_sum, KC * k + c - 1)
                    nc.scalar.activation(sq[c % 2][:], hs[:, c], ACT.Square).then_inc(n_sq, 1)
                act.wait_ge(n_sum, KC * k + KC)
                nc.scalar.activation(rms[:], norm_bank(k)[:], ACT.Sqrt, scale=1.0 / D, bias=eps).then_inc(n_root, 1)
                for c in range(KC):
                    act.wait_ge(u_ready, KC * k + c + 1)
                    nc.scalar.activation(u_hi[:, c], u_tmp[c % 3][:], ACT.Copy).then_inc(u_hi_ready, 1)

            def split_trip(n, i, per):
                act.wait_ge(raw_landed[n % RAW], i * (16 * per // RAW) + 16 * (n // RAW + 1))
                act.wait_ge(unit_used, i * per + (n - 1))
                nc.scalar.activation(w_hi[:, n % 2], raw[:, n % RAW], ACT.Copy).then_inc(hi_ready, 1)

            norm(0, lambda c: act.wait_ge(h0_ready, c + 1))
            act.wait_ge(lb_arg, 1)
            nc.scalar.activation(lb_tile, lb_tile, ACT.Exp).then_inc(lb_exp, 1)

            def far_exponentials(p, hh):
                act.wait_ge(run_ready, p * 2 + (hh + 1))
                nc.scalar.activation(far_q[:, 0:256], run[:, hh, 128:384], ACT.Exp)
                nc.scalar.activation(far_q[:, 384:512], run[:, hh, 384:512], ACT.Exp)
                for b in range(3):
                    end = run[:, hh, b * P + P - 1:b * P + P]
                    nc.scalar.activation(far_k[:, b * P:b * P + P], run[:, hh, b * P:b * P + P], ACT.Exp, bias=end, scale=-1.0)
                nc.scalar.activation(b_exp[:], run[:, hh, 255:384:128], ACT.Exp).then_inc(far_exp, 1)

            def far_scores(p, hh):
                act.wait_ge(far_ready, p * 2 + (hh + 1))
                nc.scalar.activation(ws[:, 0, 128:512], bank[6][:, 0:384], ACT.Copy)
                nc.scalar.activation(ws[:, 1, 128:384], bank[7][:, 0:256], ACT.Copy)
                nc.scalar.activation(ws[:, 2, 128:256], bank[7][:, 256:384], ACT.Copy).then_inc(far_taken, 1)

            def head_squares(p, hh):
                act.wait_ge(o_sum, p * 2 + (hh + 1))
                nc.scalar.activation((far_q, far_k)[hh][:], bank[hh][:], ACT.Square).then_inc(o_sq, 1)

            with act.Fori(0, HH // 2) as p:
                split_trip(U_HG + 1, p, 4)
                act.wait_ge(lo_ready, p * 4 + (U_HG + 2))
                act.wait_ge(proj_ready, p * 4 + 1)
                nc.scalar.activation(fx[:, 0], bank[0][:], ACT.Sigmoid).then_inc(f_sig, 1)
                act.wait_ge(unit_used, p * 4 + (U_HG + 1))
                nc.scalar.activation(fx[:, 1], bank[1][:], ACT.Sigmoid).then_inc(f_sig, 1)
                split_trip(U_HG + 2, p, 4)
                for hh in range(2):
                    act.wait_ge(f_ready, p * 2 + (hh + 1))
                    nc.scalar.activation(fx[:, hh], fx[:, hh], ACT.Ln).then_inc(f_log, 1)
                act.wait_ge(unit_used, p * 4 + (U_HG + 2))
                for hh in range(2):
                    nc.scalar.activation(qry[:, hh], bank[2 + hh][:], ACT.Silu).then_inc(q_taken, 1)
                far_exponentials(p, 0)
                split_trip(U_HG + 3, p, 4)
                act.wait_ge(unit_used, p * 4 + (U_HG + 3))
                for hh in range(2):
                    nc.scalar.activation(val[:, 2 * hh:2 * hh + 2], bank[hh][:].rearrange("p (b c) -> p b c", b=2), ACT.Copy)                         .then_inc(v_taken, 1)
                far_scores(p, 0)
                far_exponentials(p, 1)
                split_trip(U_HG + 4, p, 4)
                act.wait_ge(unit_used, p * 4 + (U_HG + 4))
                for hh in range(2):
                    nc.scalar.activation(head_of(o_raw, p, hh), bank[2 + hh][:], ACT.Silu).then_inc(g_taken, 1)
                for hh in range(2):
                    for n in range(7):
                        act.wait_ge(gap_to_ref, p * 14 + (7 * hh + n + 1))
                        nc.scalar.activation(fx[:, n % 2], fx[:, n % 2], ACT.Exp).then_inc(lev_exp, 1)
                        if hh == 1 and n == 1:
                            head_squares(p, 0)
                            far_scores(p, 1)
                head_squares(p, 1)
                for hh in range(2):
                    norm_of = (far_q, far_k)[hh]
                    act.wait_ge(o_ss, p * 2 + (hh + 1))
                    nc.scalar.activation(norm_of[:], bank[2 + hh][:], ACT.Sqrt, scale=1.0 / P, bias=eps).then_inc(o_root, 1)
                for hh in range(2):
                    act.wait_ge(o_ready, p * 2 + (hh + 1))
                    nc.scalar.activation(head_of(o_hi, p, hh), head_of(o_tmp, p, hh), ACT.Copy).then_inc(o_hi_ready, 1)
            for n in range(U_HGO, U_HGO + 4):
                split(n + 1)

            def ffn(l, u0):
                base = l * FC
                norm(1 + 2 * l, lambda c: act.wait_ge(h_added, 24 * l + c + 1))

                def unit(n, chunk, slot, i=None):
                    def at(v):
                        return v if i is None else i * 4 + v
                    if i is None:
                        split(n + 1)
                    else:
                        split_trip(n + 1, i, 4)
                    s = n % 2
                    act.wait_ge(unit_used, at(n + 1))
                    nc.scalar.activation(f_gate[s][:], bank[2 * s][:], ACT.Silu).then_inc(f_silu, 1)
                    act.wait_ge(f_prod, at(chunk + 1))
                    dst = hid2_hi[:, slot] if i is None else hid2_hi[:, bass.ds(i * 4 + slot, 1)].rearrange("p c t -> p (c t)")
                    nc.scalar.activation(dst, f_hid[s][:], ACT.Copy).then_inc(f_hi, 1)

                with act.Fori(0, FA // 4) as i:
                    for j in range(4):
                        unit(u0 + j, base + j, j, i)
                for n in range(u0 + FA, u0 + FA + 6):
                    split(n + 1)
                u1 = u0 + FA + 6
                with act.Fori(0, 2) as i:
                    for j in range(4):
                        unit(u1 + j, base + FA + j, j, i)
                for j in range(8, FC - FA):
                    unit(u1 + j, base + FA + j, j)
                for n in range(u1 + FC - FA, u1 + FC - FA + 6):
                    if n + 1 < N_UNITS:
                        split(n + 1)

            ffn(0, U_FF0)

            norm(2, lambda c: act.wait_ge(h_added, 16 + c + 1))
            for g in range(3):
                for half in range(2):
                    n = U_QKV + 6 * g + half
                    split(n + 1)
                    act.wait_ge(unit_used, n + 1)
                    for b in range(2):
                        nc.scalar.activation(vals[:, g, 2 * b:2 * b + 2, half * 256:half * 256 + 256],
                                             bank[b][:].rearrange("p (b c) -> p b c", b=2), ACT.Copy).then_inc(v_ready, 1)
                for pair in range(2):
                    for kind in range(2):
                        split(U_QKV + 6 * g + 2 + 2 * pair + kind + 1)
                    for half in range(2):
                        m = AH * g + 2 * pair + half
                        act.wait_ge(sc_gap, m + 1)
                        pr = prob_of(g, 2 * pair + half)
                        nc.scalar.activation(pr, pr, ACT.Exp, scale=DH_SCALE).then_inc(sc_exp, 1)
            act.wait_ge(share_arg, 1)
            for g in range(3):
                last = nc.scalar.activation(share[:, g], share[:, g], ACT.Exp, scale=DH_SCALE)
            last.then_inc(share_exp, 1)
            for m in range(3 * AH):
                g, h = m // AH, m % AH
                at = 4 * (m % 2)
                act.wait_ge(p_turned, m + 1)
                flat = prob_of(g, h).rearrange("p b s -> p (b s)")
                last = nc.scalar.activation(flat[:, 0:T], bank[at][:], ACT.Copy)
                if g == 0:
                    last = nc.scalar.activation(flat[:, T:T + 384], bank[at + 1][:, 0:384], ACT.Copy)
                last.then_inc(pt_ready, 1)
                act.wait_ge(ao_sum, m + 1)
                nc.scalar.activation(natural_order(ao_hi[:, m], g), group_order(bank[at + 2][:], g), ACT.Copy) \
                    .then_inc(ao_hi_ready, 1)
            for n in range(U_AO, U_AO + 6):
                split(n + 1)

            ffn(1, U_FF1)
            for b in range(TB):
                act.wait_ge(fin_turned, b + 1)
                for half in range(2):
                    if b or half:
                        act.wait_ge(sq_ready, 4 * TB + 2 * b + half)
                    nc.scalar.activation(out_sq[:], bank[2 * b + half][:], ACT.Square,
                                         accum_out=out_rms[:, half, b:b + 1]).then_inc(sq_ready, 1)
            act.wait_ge(rms_arg, 5)
            nc.scalar.activation(out_rms[:, 4], out_rms[:, 3], ACT.Sqrt).then_inc(root_ready, 1)

        @block.vector
        def _(dve):
            steps = Count(dve_step)

            def chain(instruction):
                dve.wait_ge(dve_step, steps.mark(instruction))

            def split(n):
                dve.wait_ge(hi_ready, n + 1)
                nc.vector.tensor_tensor(w_lo[:, n % 2], raw[:, n % RAW], w_hi[:, n % 2].bitcast(F32), ALU.subtract) \
                    .then_inc(lo_ready, 1)

            dve.wait_ge(sq_ready, TB)
            nc.vector.tensor_scalar(small[:, 1], small[:, 0], 1.0 / D, EPS, ALU.mult, ALU.add).then_inc(rms_arg, 1)
            dve.wait_ge(root_ready, 1)
            chain(nc.vector.reciprocal(small[:, 3], small[:, 2]))
            for b in range(TB):
                nc.vector.tensor_scalar(xs[:, b], res[:, b], small[:, 3, b:b + 1], None, ALU.mult).then_inc(xs_ready, 1)
            dve.wait_ge(narrow_hi, 1)
            nc.vector.tensor_tensor(wif_lo[:], cols(par1, P1_COLS, "w_if").rearrange("p (k c) -> p k c", k=KC),
                                    wif_hi[:].bitcast(F32), ALU.subtract).then_inc(narrow_lo, 1)
            split(0)
            for c in range(KC):
                dve.wait_ge(u_hi_ready, c + 1)
                nc.vector.scalar_tensor_tensor(u_lo[:, c], bank[c % 4][:], cols(par1, P1_COLS, "n1g")[:, c:c + 1],
                                               u_hi[:, c].bitcast(F32), ALU.mult, ALU.subtract).then_inc(u_lo_ready, 1)
            nc.vector.tensor_tensor(cols(par1, P1_COLS, "w_sp").rearrange("p (g t) -> p g t", g=NG),
                                    cols(par1, P1_COLS, "w_sp").rearrange("p (g t) -> p g t", g=NG),
                                    cols(con, C_COLS, "upper").unsqueeze(1).to_broadcast([P, NG, P]), ALU.mult) \
                .then_inc(wsp_ready, 1)

            def gate_rows_first():
                dve.wait_ge(gates_ready, 1)
                chain(nc.vector.tensor_scalar(r_f[0:H1, :], bank[4][32:36, :], cols(par1, P1_COLS, "b_f")[32:36], None,
                                              ALU.add))
                nc.vector.tensor_scalar(r_i[0:H1, :], bank[4][0:H1, :], cols(par1, P1_COLS, "b_i")[0:H1], None, ALU.add)
                nc.vector.scalar_tensor_tensor(r_e[0:H1, :], r_f[0:H1, :], -1.0, r_f[0:H1, :], ALU.mult, ALU.min) \
                    .then_inc(soft_arg, 1)

            def gate_rows_second():
                one = cols(par1, P1_COLS, "one_row")[0:H1]
                dve.wait_ge(soft_log, 1)
                chain(nc.vector.scalar_tensor_tensor(r_f[0:H1, :], r_f[0:H1, :], 0.0, r_e[0:H1, :], ALU.min, ALU.subtract))
                chain(nc.vector.tensor_tensor_scan(r_sum[0:H1, :], one, r_f[0:H1, :], 0.0, ALU.mult, ALU.add))
                chain(nc.vector.tensor_tensor(r_i[0:H1, :], r_i[0:H1, :], r_sum[0:H1, :], ALU.subtract))
                chain(nc.vector.tensor_tensor_scan(neg_m[0:H1, :], one, r_i[0:H1, :], 0.0, ALU.mult, ALU.max))
                chain(nc.vector.tensor_tensor(e_neg_m[0:H1, :], r_sum[0:H1, :], neg_m[0:H1, :], ALU.add))
                nc.vector.tensor_scalar(neg_m[0:H1, :], neg_m[0:H1, :], -1.0, None, ALU.mult).then_inc(rows_ready, 1)

            for n in range(N_IN):
                split(n + 1)
                for half in range(2):
                    q = 2 * n + half
                    if q >= 8:
                        continue
                    dve.wait_ge(in_ready if half == 0 else unit_used, n + 1)
                    src = bank[q % 4]
                    tap = [cols(par1, P1_COLS, "conv")[:, i * KC + q:i * KC + q + 1] for i in range(4)]
                    chain(nc.vector.tensor_scalar(qk[:, q], src[:], tap[3], None, ALU.mult))
                    for back in (1, 2, 3):
                        last = nc.vector.scalar_tensor_tensor(qk[:, q, back:], src[:, 0:T - back], tap[3 - back],
                                                              qk[:, q, back:], ALU.mult, ALU.add)
                        if back < 3:
                            chain(last)
                    last.then_inc(in_conv, 1)
                if n == 0:
                    gate_rows_first()
                if n == 2:
                    gate_rows_second()
                if n == 6:
                    dve.wait_ge(sq_ready, 2 * TB)
                    nc.vector.tensor_scalar(small[:, 5], small[:, 4], 1.0 / HALF, EPS, ALU.mult, ALU.add) \
                        .then_inc(rms_arg, 1)
                if n == 8:
                    dve.wait_ge(root_ready, 2)
                    chain(nc.vector.reciprocal(small[:, 7], small[:, 6]))
                    for b in range(TB):
                        nc.vector.tensor_scalar(vg[:, b], vg[:, b], small[:, 7, b:b + 1], None, ALU.mult) \
                            .then_inc(vg_ready, 1)
            dve.wait_ge(g_turned, 1)
            chain(nc.vector.tensor_copy(g_col[:], bank[4][:, 0:TB * H1].rearrange("p (b h) -> p b h", b=TB)))

            def decay_exponents(h):
                dve.wait_ge(m_spread, h + 1)
                if h:
                    dve.wait_ge(num_ready, h)
                for j in range(TB):
                    g = g_col[:, j, h:h + 1]
                    if j < TB - 1:
                        nc.vector.tensor_scalar(dec[:, j, (j + 1) * P:], bank[0][:, (j + 1) * P:], g, None, ALU.add)
                    nc.vector.scalar_tensor_tensor(dec[:, j, j * P:(j + 1) * P], bank[0][:, j * P:(j + 1) * P], g,
                                                   cols(con, C_COLS, "negmask"), ALU.add, ALU.add).then_inc(dec_arg, 1)

            def weigh_scores(h):
                dve.wait_ge(s_ready, h + 1)
                dve.wait_ge(dec_ready, h + 1)
                for j in range(TB):
                    at = (bank[1][:], bank[2][:, 0:384], bank[3][:, 0:256], bank[3][:, 256:384])[j]
                    last = nc.vector.scalar_tensor_tensor(dec[:, j, j * P:], at, DH_SCALE, dec[:, j, j * P:],
                                                          ALU.mult, ALU.mult)
                    if j:
                        last.then_inc(s_weighted, 1)

            def gate_mixed(h):
                dve.wait_ge(mix_ready, h + 1)
                if h:
                    dve.wait_ge(y_lo_ready, 2 * h - 1)
                bias = cols(par1, P1_COLS, "b_sp")[:, h * P:(h + 1) * P].unsqueeze(1).to_broadcast([P, TB, P])
                chain(nc.vector.scalar_tensor_tensor(gm_a[:].rearrange("p (b t) -> p b t", b=TB),
                                                     bank[7][:].rearrange("p (b t) -> p b t", b=TB),
                                                     cols(par1, P1_COLS, "g_v")[:, h:h + 1], bias, ALU.mult, ALU.add))
                nc.vector.tensor_tensor(gm_a[:], gm_a[:], ug[:, h], ALU.mult).then_inc(gated_ready, 1)

            def head_output(h):
                dve.wait_ge(nq_abs, h + 1)
                chain(nc.vector.tensor_tensor(ml_a[:], ml_a[:], bank[6][:], ALU.max))
                chain(nc.vector.reciprocal(ml_a[:], ml_a[:]))
                chain(nc.vector.tensor_tensor(ml_a[:], bank[4][:], ml_a[:], ALU.mult))
                nc.vector.tensor_tensor(ml_a[:], ml_a[:], so[:, h], ALU.mult).then_inc(h_ready, 1)

            def norms(h):
                dve.wait_ge(gated_root, h + 1)
                chain(nc.vector.reciprocal(gm_b[:], gm_b[:]))
                nc.vector.scalar_tensor_tensor(gm_a[:], gm_a[:], cols(par1, P1_COLS, "g_gm")[:, h:h + 1], gm_b[:],
                                               ALU.mult, ALU.mult).then_inc(yg_ready, 1)
                dve.wait_ge(h_root, h + 1)
                chain(nc.vector.reciprocal(ml_b[:], ml_b[:]))
                nc.vector.scalar_tensor_tensor(ml_a[:], ml_a[:], cols(par1, P1_COLS, "g_ml")[:, h:h + 1], ml_b[:],
                                               ALU.mult, ALU.mult).then_inc(ym_ready, 1)
                dve.wait_ge(yg_hi, h + 1)
                nc.vector.tensor_tensor(u_lo[:, 4 + h], gm_a[:], u_hi[:, 4 + h].bitcast(F32), ALU.subtract) \
                    .then_inc(y_lo_ready, 1)
                dve.wait_ge(ym_hi, h + 1)
                nc.vector.tensor_tensor(u_lo[:, h], ml_a[:], u_hi[:, h].bitcast(F32), ALU.subtract) \
                    .then_inc(y_lo_ready, 1)

            for h in range(H1 + 1):
                if h < H1:
                    decay_exponents(h)
                if h:
                    head_output(h - 1)
                if h < H1:
                    weigh_scores(h)
                if h:
                    norms(h - 1)
                if h < H1:
                    gate_mixed(h)

            for half in range(2):
                for part in range(2):
                    n = U_OUT + 2 * half + part
                    if n + 1 < STREAM_END:
                        split(n + 1)
                dve.wait_ge(unit_used, U_OUT + 2 * half + 2)
                for b in range(TB):
                    c = slice(half * 512, half * 512 + 512)
                    nc.vector.tensor_tensor(res[:, b, c], bank[4 * half + b][:], res[:, b, c], ALU.add) \
                        .then_inc(res1_ready, 1)

            dve.wait_ge(sq_ready, 3 * TB)
            nc.vector.tensor_scalar(rms2[:, 1], rms2[:, 0], 1.0 / D, EPS, ALU.mult, ALU.add).then_inc(rms_arg, 1)
            dve.wait_ge(root_ready, 3)
            chain(nc.vector.reciprocal(rms2[:, 3], rms2[:, 2]))
            dve.wait_ge(params_landed, 16)
            for b in range(TB):
                nc.vector.scalar_tensor_tensor(xn[:, b], res[:, b], rms2[:, 3, b:b + 1], cols(par2, P2_COLS, "n2g"),
                                               ALU.mult, ALU.mult).then_inc(xn_ready, 1)
            dve.wait_ge(narrow_hi, 2)
            nc.vector.tensor_tensor(wr_lo[:], cols(par2, P2_COLS, "w_r").rearrange("p (k c) -> p k c", k=KC),
                                    wr_hi[:].bitcast(F32), ALU.subtract).then_inc(narrow_lo, 1)
            for c in range(KC):
                dve.wait_ge(u_hi_ready, KC + c + 1)
                nc.vector.tensor_tensor(u_lo[:, c], bank[c % 4][:], u_hi[:, c].bitcast(F32), ALU.subtract) \
                    .then_inc(u_lo_ready, 1)

            def over_last(tile, n):
                return tile.unsqueeze(2).to_broadcast([P, TB, n])

            def iota(n):
                return cols(con, C_COLS, "iota32")[:, 0:n].unsqueeze(1).to_broadcast([P, TB, n])

            def first_largest(out, values, largest, n):
                chain(nc.vector.tensor_tensor(out, values, over_last(largest, n), ALU.is_equal))
                chain(nc.vector.scalar_tensor_tensor(out, out, -64.0, iota(n), ALU.mult, ALU.add))
                chain(nc.vector.tensor_reduce(best[:, 7], out, AX.X, ALU.min))
                chain(nc.vector.tensor_tensor(out, out, over_last(best[:, 7], n), ALU.is_equal))

            chain(nc.vector.tensor_copy(pairs[:], cols(par2, P2_COLS, "pairs").rearrange("p (b k c) -> p b k c", b=TB, k=2)))
            dve.wait_ge(logits_ready, 2)
            chain(nc.vector.tensor_tensor(logit[:], bank[6][:, 0:TB * 36].rearrange("p (b c) -> p b c", b=TB),
                                          cols(par2, P2_COLS, "b_r").unsqueeze(1).to_broadcast([P, TB, 36]), ALU.add))
            chain(nc.vector.tensor_reduce(best[:, 0], logit[:, :, 0:EG], AX.X, ALU.max))
            nc.vector.tensor_tensor(gap[:], logit[:, :, 0:EG], over_last(best[:, 0], EG), ALU.subtract).then_inc(router_arg, 1)
            first_largest(in_group[:], logit[:, :, 0:EG], best[:, 0], EG)
            chain(nc.vector.tensor_tensor(chosen[:], logit[:, :, EG:].rearrange("p b (g j) -> p b g j", g=EG),
                                          in_group[:].unsqueeze(3).to_broadcast([P, TB, EG, PER]), ALU.mult))
            chain(nc.vector.tensor_reduce(le1[:], chosen[:].rearrange("p b g j -> p b j g"), AX.X, ALU.add))
            chain(nc.vector.tensor_reduce(best[:, 2], le1[:], AX.X, ALU.max))
            first_largest(first[:], le1[:], best[:, 2], PER)
            chain(nc.vector.scalar_tensor_tensor(le2[:], first[:], NEG, le1[:], ALU.mult, ALU.add))
            chain(nc.vector.tensor_reduce(best[:, 3], le2[:], AX.X, ALU.max))
            nc.vector.tensor_tensor(best[:, 4], best[:, 3], best[:, 2], ALU.subtract).then_inc(router_arg, 1)
            first_largest(second[:], le2[:], best[:, 3], PER)
            for k, choice in enumerate((first, second)):
                chain(nc.vector.tensor_tensor(owns[:, k].rearrange("p b (g j) -> p b g j", g=EG),
                                              in_group[:].unsqueeze(3).to_broadcast([P, TB, EG, PER]),
                                              choice[:].unsqueeze(2).to_broadcast([P, TB, EG, PER]), ALU.mult))
            nc.vector.tensor_tensor(both[:], owns[:, 0], owns[:, 1], ALU.add).then_inc(owns_ready, 1)
            dve.wait_ge(router_exp, 1)
            chain(nc.vector.tensor_reduce(best[:, 1], gap[:], AX.X, ALU.add))
            dve.wait_ge(router_exp, 2)
            chain(nc.vector.scalar_tensor_tensor(best[:, 6], best[:, 5], 1.0, best[:, 1], ALU.add, ALU.mult))
            chain(nc.vector.reciprocal(weight[:, 0], best[:, 6]))
            chain(nc.vector.tensor_tensor(weight[:, 1], weight[:, 0], best[:, 5], ALU.mult))

            dve.wait_ge(before_ready, 1)
            in_block = bank[5][:, 0:TB * NE].rearrange("p (b e) -> p b e", b=TB)
            of_block = bank[5][:, TB * NE:2 * TB * NE].rearrange("p (b e) -> p b e", b=TB)
            chain(nc.vector.tensor_copy(so_far[:, 0], of_block[:, 0]))
            for b in range(1, TB):
                chain(nc.vector.tensor_tensor(so_far[:, b], of_block[:, b], so_far[:, b - 1], ALU.add))
            nc.vector.tensor_copy(before_all[:, 0], in_block[:, 0])
            chain(nc.vector.tensor_tensor(before_all[:, 1:], in_block[:, 1:], so_far[:, 0:TB - 1], ALU.add))
            before, count = before_all[:], so_far[:, TB - 1]
            chain(nc.vector.tensor_scalar(n_over[:], count, float(P), None, ALU.is_gt))
            chain(nc.vector.scalar_tensor_tensor(n_over[:], count, float(2 * P), n_over[:], ALU.is_gt, ALU.add))
            chain(nc.vector.scalar_tensor_tensor(n_over[:], count, float(3 * P), n_over[:], ALU.is_gt, ALU.add))
            chain(nc.vector.tensor_tensor_scan(over_end[:], ones[:, 0:NE], n_over[:], 0.0, ALU.mult, ALU.add))
            chain(nc.vector.tensor_tensor(over_start[:], over_end[:], n_over[:], ALU.subtract))
            chain(nc.vector.tensor_scalar(blocks[:], before, float(P), None, ALU.is_ge))
            chain(nc.vector.tensor_scalar(over[:], blocks[:], 1.0, None, ALU.mult))
            for n in (2, 3):
                chain(nc.vector.scalar_tensor_tensor(blocks[:], before, float(n * P), blocks[:], ALU.is_ge, ALU.add))
            chain(nc.vector.scalar_tensor_tensor(lift[:], blocks[:], -float(P), before, ALU.mult, ALU.add))
            chain(nc.vector.scalar_tensor_tensor(lift[:], lift[:], float(N_OVER), blocks[:], ALU.mult, ALU.add))
            chain(nc.vector.scalar_tensor_tensor(lift[:], lift[:], float(MAIN - 1),
                                                 over_start[:].unsqueeze(1).to_broadcast([P, TB, NE]), ALU.add, ALU.add))
            chain(nc.vector.scalar_tensor_tensor(row[:], before, float(NE), iota(NE), ALU.mult, ALU.add))
            chain(nc.vector.tensor_tensor(lift[:], lift[:], row[:], ALU.subtract))
            chain(nc.vector.tensor_tensor(lift[:], lift[:], over[:], ALU.mult))
            chain(nc.vector.tensor_tensor(row[:], row[:], lift[:], ALU.add))
            for k in range(2):
                chain(nc.vector.tensor_tensor(lift[:], owns[:, k], row[:], ALU.mult))
                chain(nc.vector.tensor_reduce(dest_f[:, k], lift[:], AX.X, ALU.add))
            chain(nc.vector.tensor_tensor(over_cmp[:], over_end[:].unsqueeze(1).to_broadcast([P, 8, NE]),
                                          cols(con, C_COLS, "iota32")[:, 0:8].unsqueeze(2).to_broadcast([P, 8, NE]), ALU.is_le))
            chain(nc.vector.tensor_reduce(over_e[:], over_cmp[:], AX.X, ALU.add))
            chain(nc.vector.tensor_scalar(over_e[:], over_e[:], float(NE - 1), None, ALU.min))
            chain(nc.vector.tensor_copy(over_int[:, 0:8], over_e[:]))
            chain(nc.vector.tensor_copy(over_int[:, 8:9], over_end[:, NE - 1:NE]))
            nc.vector.tensor_copy(dest[:], dest_f[:]).then_inc(dest_ready, 1)

            def expert_tokens():
                nc.vector.tensor_tensor(xe_lo[:, 0:4], bank[0][:].rearrange("p (c t) -> p c t", c=4),
                                        xe_hi[:, 0:4].bitcast(F32), ALU.subtract)
                nc.vector.tensor_tensor(xe_lo[:, 4:8], bank[1][:].rearrange("p (c t) -> p c t", c=4),
                                        xe_hi[:, 4:8].bitcast(F32), ALU.subtract).then_inc(xe_lo_ready, 1)

            def split_of(i, c):
                dve.wait_ge(hi_ready, i * (2 * PER_EXPERT) + (U_MOE + c + 1))
                nc.vector.tensor_tensor(lo_slot(c), raw[:, c % RAW], hi_slot(c).bitcast(F32), ALU.subtract).then_inc(lo_ready, 1)

            def expert_pair(i, last):
                for b in range(2):
                    e = i * 2 + b
                    u0 = i * (2 * PER_EXPERT) + (U_MOE + PER_EXPERT * b)
                    c0 = PER_EXPERT * b
                    end = last and b == 1
                    split_of(i, c0 + 4)
                    split_of(i, c0 + 5)
                    dve.wait_ge(silu_ready, e + 1)
                    dve.wait_ge(unit_used, u0 + 4)
                    nc.vector.tensor_tensor(hid[:], gate[:], bank[3][:], ALU.mult).then_inc(hid_ready, 1)
                    if not end:
                        split_of(i, c0 + 6)
                    dve.wait_ge(hid_hi_ready, e + 1)
                    nc.vector.tensor_tensor(hid_lo[:], bank[4][:].rearrange("p (c t) -> p c t", c=4),
                                            hid_hi[:].bitcast(F32), ALU.subtract).then_inc(hid_lo_ready, 1)
                    if not end:
                        split_of(i, c0 + 7)
                    dve.wait_ge(xe_hi_ready, e + 2)
                    expert_tokens()
                    if not end:
                        split_of(i, c0 + 8)
                        split_of(i, c0 + 9)

            for c in (1, 2, 3):
                split_of(0, c)
            dve.wait_ge(xe_hi_ready, 1)
            expert_tokens()
            with dve.Fori(0, NE // 2 - 1) as i:
                expert_pair(i, False)
            expert_pair(NE // 2 - 1, True)
            split(U_HG)

            with dve.If(overflowing(dve)):
                with dve.Fori(0, N_OVER) as v:
                    dve.wait_ge(over_products, v * 4 + 2)
                    dve.wait_ge(over_copies, v * 4 + 2)
                    nc.vector.tensor_tensor(hid[:], gate[:], bank[3][:], ALU.mult).then_inc(over_hid, 1)
            for b in range(TB):
                dve.wait_ge(y_landed[b], 16)
                chain(nc.vector.scalar_tensor_tensor(res[:, b], y_pairs[:, b, 0], weight[:, 0, b:b + 1], res[:, b],
                                                     ALU.mult, ALU.add))
                nc.vector.scalar_tensor_tensor(res[:, b], y_pairs[:, b, 1], weight[:, 1, b:b + 1], res[:, b],
                                               ALU.mult, ALU.add).then_inc(res2_ready, 1)
            dve.wait_ge(sq_ready, 4 * TB)
            nc.vector.tensor_scalar(rms2[:, 5], rms2[:, 4], 1.0 / D, EPS, ALU.mult, ALU.add).then_inc(rms_arg, 1)
            dve.wait_ge(root_ready, 4)
            chain(nc.vector.reciprocal(rms2[:, 7], rms2[:, 6]))
            for b in range(TB):
                nc.vector.tensor_scalar(xn[:, b], res[:, b], rms2[:, 7, b:b + 1], None, ALU.mult).then_inc(xn_ready, 1)
            dve.wait_ge(xn_ready, 2 * TB)
            for c in range(KC):
                dve.wait_ge(h_turned, c + 1)
                nc.vector.tensor_scalar(hs[:, c], bank[c % 4][:], cols(par2, P2_COLS, "fg")[:, c:c + 1], None, ALU.mult) \
                    .then_inc(h0_ready, 1)

            def norm(k, gains):
                dve.wait_ge(n_root, k + 1)
                chain(nc.vector.reciprocal(rms[:], rms[:]))

                def second_part(c):
                    dve.wait_ge(u_hi_ready, (2 + k) * KC + c + 1)
                    nc.vector.tensor_tensor(u_lo[:, c], u_tmp[c % 3][:], u_hi[:, c].bitcast(F32), ALU.subtract)                         .then_inc(u_lo_ready, 1)

                for c in range(KC):
                    if c >= 3:
                        dve.wait_ge(u_lo_ready, (2 + k) * KC + c - 2)
                    nc.vector.scalar_tensor_tensor(u_tmp[c % 3][:], hs[:, c], gains[:, c:c + 1], rms[:], ALU.mult, ALU.mult)                         .then_inc(u_ready, 1)
                    if c:
                        second_part(c - 1)
                second_part(KC - 1)

            def split_trip(n, i, per):
                dve.wait_ge(hi_ready, i * per + (n + 1))
                nc.vector.tensor_tensor(w_lo[:, n % 2], raw[:, n % RAW], w_hi[:, n % 2].bitcast(F32), ALU.subtract) \
                    .then_inc(lo_ready, 1)

            def add_rows(n0, per_half, ready):
                for half in range(2):
                    for q in range(per_half):
                        n = n0 + half * per_half + q
                        if n + 1 < N_UNITS:
                            split(n + 1)
                    dve.wait_ge(unit_used, n0 + (half + 1) * per_half)
                    for d in range(4):
                        nc.vector.tensor_tensor(hs[:, 4 * half + d], bank[4 * half + d][:], hs[:, 4 * half + d], ALU.add) \
                            .then_inc(h_added, 1)

            dve.wait_ge(params_landed, 32)
            g_mix, g_ffn = cols(par3, P3_COLS, "n_mix"), cols(par3, P3_COLS, "n_ffn")
            lb_view = lb_tile.rearrange("p (l c) -> p l c", l=3)
            chain(nc.vector.tensor_tensor(lbs[0][:], lb_view[:, 0], lb_view[:, 1], ALU.max))
            chain(nc.vector.tensor_tensor(lbs[0][:], lbs[0][:], lb_view[:, 2], ALU.max))
            nc.vector.tensor_tensor(lb_view, lb_view, lbs[0][:].unsqueeze(1).to_broadcast([P, 3, KC]), ALU.subtract) \
                .then_inc(lb_arg, 1)
            norm(0, g_mix[:, 0:KC])
            dve.wait_ge(lb_exp, 1)
            chain(nc.vector.tensor_tensor(lbs[1][:], lb_view[:, 0], lb_view[:, 1], ALU.add))
            chain(nc.vector.tensor_tensor(lbs[1][:], lbs[1][:], lb_view[:, 2], ALU.add))
            chain(nc.vector.reciprocal(lbs[2][:], lbs[1][:]))
            low, span = lbs[3], lbs[4]
            chain(nc.vector.tensor_tensor(low[:], lb_view[:, 0], lbs[2][:], ALU.mult))
            chain(nc.vector.tensor_scalar(span[:], low[:], -1.0, 1.0, ALU.mult, ALU.add))

            reset = cols(par3, P3_COLS, "reset")
            levels = cols(par3, P3_COLS, "levels").bitcast(U32).rearrange("p (n t) -> p n t", n=8)
            def far_sides(p, hh):
                dve.wait_ge(q_taken, p * 2 + (hh + 1))
                dve.wait_ge(far_exp, p * 2 + (hh + 1))
                nc.vector.tensor_tensor(far_q[:, 0:256], far_q[:, 0:256], qry[:, hh, 128:384], ALU.mult)
                chain(nc.vector.tensor_tensor(far_q[:, 384:512], far_q[:, 384:512], qry[:, hh, 384:512], ALU.mult))
                chain(nc.vector.tensor_tensor(far_k[:, 0:384], far_k[:, 0:384], key[:, hh, 0:384], ALU.mult))
                nc.vector.tensor_scalar(far_k[:, 384:512], far_k[:, 0:128], b_exp[:, 0:1], None, ALU.mult)
                nc.vector.tensor_scalar(far_q[:, 256:384], far_q[:, 384:512], b_exp[:, 1:2], None, ALU.mult)                     .then_inc(far_kq, 1)

            def gate_outputs(p, hh):
                dve.wait_ge(g_taken, p * 2 + (hh + 1))
                dve.wait_ge(o_sq, p * 2 + (hh + 1))
                raw_out = head_of(o_raw, p, hh)
                nc.vector.scalar_tensor_tensor(raw_out, bank[hh][:], cols(par3, P3_COLS, "og"), raw_out, ALU.mult, ALU.mult)                     .then_inc(o_gated, 1)

            with dve.Fori(0, HH // 2) as p:
                steps.enter(p, HG_STEPS)
                split_trip(U_HG + 1, p, 4)
                for hh in range(2):
                    h = bass.ds(p * 2 + hh, 1)
                    dve.wait_ge(f_sig, p * 2 + (hh + 1))
                    chain(nc.vector.tensor_scalar(fx[:, hh], fx[:, hh], span[:, h], low[:, h], ALU.mult, ALU.add))
                    nc.vector.tensor_scalar(key[:, hh], fx[:, hh], -1.0, 1.0, ALU.mult, ALU.add).then_inc(f_ready, 1)
                split_trip(U_HG + 2, p, 4)
                for hh in range(2):
                    dve.wait_ge(f_log, p * 2 + (hh + 1))
                    nc.vector.tensor_tensor_scan(run[:, hh], reset, fx[:, hh], 0.0, ALU.mult, ALU.add).then_inc(run_ready, 1)
                far_sides(p, 0)
                split_trip(U_HG + 3, p, 4)
                far_sides(p, 1)
                split_trip(U_HG + 4, p, 4)
                for hh in range(2):
                    for n in range(9):
                        if n < 7:
                            w = 64 >> n
                            dve.wait_ge(lev_exp, p * 14 + (7 * hh + n + 1))
                            if n >= 2:
                                dve.wait_ge(lev_ready, p * 16 + (8 * hh + n - 1))
                            view = lambda ap: ap.rearrange("p (n t) -> p n t", t=2 * w)[:, :, 0:w]
                            nc.vector.tensor_tensor(view(k_dec[n % 2][:]), view(fx[:, n % 2]), view(key[:, hh]), ALU.mult)                                 .then_inc(k_ready, 1)
                        if hh == 1 and n == 1:
                            gate_outputs(p, 0)
                        if n >= 1:
                            dve.wait_ge(lev_ready, p * 16 + (8 * hh + n))
                            if n >= 2:
                                dve.wait_ge(lev_taken, p * 16 + (8 * hh + n - 1))
                            nc.vector.memset(turn[:, n - 1:n], 0.0)
                            nc.vector.copy_predicated(ws[:, :, 0:P], levels[:, n - 1].unsqueeze(1).to_broadcast([P, TB, P]),
                                                      bank[4 + (n - 1) % 2][:].rearrange("p (b t) -> p b t", b=TB))                                 .then_inc(lev_taken, 1)
                gate_outputs(p, 1)
                for hh in range(2):
                    norm_of = (far_q, far_k)[hh]
                    dve.wait_ge(o_root, p * 2 + (hh + 1))
                    chain(nc.vector.reciprocal(norm_of[:], norm_of[:]))
                    nc.vector.tensor_tensor(head_of(o_tmp, p, hh), head_of(o_raw, p, hh), norm_of[:], ALU.mult)                         .then_inc(o_ready, 1)
                for hh in range(2):
                    dve.wait_ge(o_hi_ready, p * 2 + (hh + 1))
                    nc.vector.tensor_tensor(head_of(o_lo, p, hh), head_of(o_tmp, p, hh), head_of(o_hi, p, hh).bitcast(F32),
                                            ALU.subtract).then_inc(o_lo_ready, 1)
            steps.leave(HH // 2)
            add_rows(U_HGO, 2, None)

            def ffn(l, u0):
                base = l * FC
                norm(1 + 2 * l, g_ffn[:, l * KC:l * KC + KC])

                def unit(n, chunk, slot, i=None):
                    def at(v):
                        return v if i is None else i * 4 + v
                    if i is None:
                        split(n + 1)
                    else:
                        split_trip(n + 1, i, 4)
                    s = n % 2
                    dve.wait_ge(f_silu, at(chunk + 1))
                    nc.vector.tensor_tensor(f_hid[s][:], f_gate[s][:], bank[2 * s + 1][:], ALU.mult).then_inc(f_prod, 1)
                    dve.wait_ge(f_hi, at(chunk + 1))
                    c = slice(slot, slot + 1) if i is None else bass.ds(i * 4 + slot, 1)
                    nc.vector.tensor_tensor(hid2_lo[:, c].rearrange("p c t -> p (c t)"), f_hid[s][:],
                                            hid2_hi[:, c].bitcast(F32).rearrange("p c t -> p (c t)"), ALU.subtract) \
                        .then_inc(f_lo, 1)

                with dve.Fori(0, FA // 4) as i:
                    for j in range(4):
                        unit(u0 + j, base + j, j, i)
                add_rows(u0 + FA, 3, None)
                u1 = u0 + FA + 6
                with dve.Fori(0, 2) as i:
                    for j in range(4):
                        unit(u1 + j, base + FA + j, j, i)
                for j in range(8, FC - FA):
                    unit(u1 + j, base + FA + j, j)
                add_rows(u1 + FC - FA, 3, None)

            ffn(0, U_FF0)

            norm(2, g_mix[:, KC:2 * KC])
            cos, sin = cols(par3, P3_COLS, "cos"), cols(par3, P3_COLS, "sin")
            band = cols(par3, P3_COLS, "band")
            for g in range(3):
                for half in range(2):
                    split(U_QKV + 6 * g + half + 1)
                for pair in range(2):
                    for kind in range(2):
                        n = U_QKV + 6 * g + 2 + 2 * pair + kind
                        split(n + 1)
                        for half in range(2):
                            m = 8 * g + 4 * pair + 2 * kind + half
                            src = bank[2 * kind + half]
                            if half == 0:
                                dve.wait_ge(proj_ready, PROJ_ATTN + m // 2 + 1)
                            else:
                                dve.wait_ge(unit_used, n + 1)
                            if m >= 2:
                                dve.wait_ge(rope_ready, m - 1)
                            nc.vector.tensor_tensor(r_cos[m % 2][:], src[:], cos, ALU.mult)
                            nc.vector.tensor_tensor(r_sin[m % 2][0:64, :], src[64:128, :], sin[64:128], ALU.mult)
                            nc.vector.tensor_tensor(r_sin[m % 2][64:128, :], src[0:64, :], sin[0:64], ALU.mult) \
                                .then_inc(rope_mul, 1)
                    for half in range(2):
                        m = AH * g + 2 * pair + half
                        h = 2 * pair + half
                        at = 4 + 2 * (m % 2)
                        pr = prob_of(g, h)
                        dve.wait_ge(sc_ready, m + 1)
                        if g == 0:
                            nc.vector.tensor_tensor(pr[:, 0], bank[at][:, 0:256], band[:, 0:256], ALU.add)
                            nc.vector.tensor_tensor(pr[:, 1], bank[at][:, 256:512], band[:, 256:512], ALU.add)
                            chain(nc.vector.tensor_tensor(pr[:, 2:4], bank[at + 1][:].rearrange("p (b s) -> p b s", b=2),
                                                          band[:, 256:512].unsqueeze(1).to_broadcast([P, 2, 256]), ALU.add))
                        else:
                            mask = band[:, 512 + (g - 1) * P:512 + g * P]
                            chain(nc.vector.tensor_tensor(pr, bank[at][:].rearrange("p (b s) -> p b s", b=TB),
                                                          mask.unsqueeze(1).to_broadcast([P, TB, P]), ALU.add))
                        nc.vector.tensor_reduce(stat[g][:, :, h], pr, AX.X, ALU.max).then_inc(sc_max, 1)
                    for half in range(2):
                        m = AH * g + 2 * pair + half
                        h = 2 * pair + half
                        dve.wait_ge(sc_exp, m + 1)
                        nc.vector.tensor_reduce(stat[g][:, :, AH + h], prob_of(g, h), AX.X, ALU.add).then_inc(sc_sum, 1)
            dve.wait_ge(sc_sum, 3 * AH)
            dve.wait_ge(order_landed, 32)
            nat = [stat[0], stat_nat[1], stat_nat[2]]
            chain(nc.vector.tensor_tensor(top[:], nat[0][:, :, 0:AH], nat[1][:, :, 0:AH], ALU.max))
            chain(nc.vector.tensor_tensor(top[:], top[:], nat[2][:, :, 0:AH], ALU.max))
            for g in range(3):
                last = nc.vector.tensor_tensor(share[:, g], nat[g][:, :, 0:AH], top[:], ALU.subtract)
            last.then_inc(share_arg, 1)
            dve.wait_ge(share_exp, 1)
            chain(nc.vector.tensor_tensor(den[:], share[:, 0], nat[0][:, :, AH:], ALU.mult))
            for g in (1, 2):
                chain(nc.vector.tensor_tensor(top[:], share[:, g], nat[g][:, :, AH:], ALU.mult))
                chain(nc.vector.tensor_tensor(den[:], den[:], top[:], ALU.add))
            chain(nc.vector.reciprocal(den[:], den[:]))
            for g in range(3):
                nc.vector.tensor_tensor(share[:, g], share[:, g], den[:], ALU.mult).then_inc(share_ready, 1)
            for m in range(3 * AH):
                g = m // AH
                at = 4 * (m % 2)
                dve.wait_ge(ao_hi_ready, m + 1)
                nc.vector.tensor_tensor(natural_order(ao_lo[:, m], g), group_order(bank[at + 2][:], g),
                                        natural_order(ao_hi[:, m].bitcast(F32), g), ALU.subtract).then_inc(ao_lo_ready, 1)
            add_rows(U_AO, 3, None)

            ffn(1, U_FF1)
            dve.wait_ge(sq_ready, 6 * TB)
            chain(nc.vector.tensor_tensor(out_rms[:, 2], out_rms[:, 0], out_rms[:, 1], ALU.add))
            nc.vector.tensor_scalar(out_rms[:, 3], out_rms[:, 2], 1.0 / D, EPS, ALU.mult, ALU.add).then_inc(rms_arg, 1)
            dve.wait_ge(root_ready, 5)
            chain(nc.vector.reciprocal(out_rms[:, 5], out_rms[:, 4]))
            for b in range(TB):
                if b >= 2:
                    dve.wait_ge(out_stored[b % 2], 16)
                for half in range(2):
                    c = slice(half * T, half * T + T)
                    last = nc.vector.scalar_tensor_tensor(out_tile[b % 2][:, c], bank[2 * b + half][:], out_rms[:, 5, b:b + 1],
                                                          cols(par3, P3_COLS, "fin")[:, c], ALU.mult, ALU.mult)
                last.then_inc(fin_ready, 1)


        @block.gpsimd
        def _(pool):
            nc.gpsimd.memset(no_pairs[:], NO_PAIR).then_inc(rows_set, 1)
            pool.wait_ge(rows_set, 1)
            pool.dma_start(slot_table.rearrange("(p n) c -> p (n c)", p=P), no_pairs[:]).then_inc(table_written, 16)
            for b in range(2):
                pool.dma_start(y_mark[b:b + 1, :], no_pairs[b:b + 1, 0:8]).then_inc(y_free[b], 16)
            pool.wait_ge(y_lo_ready, 8)
            pool.dma_start(par2[:], phase2_in).then_inc(params_landed, 16)
            pool.wait_ge(xn_ready, TB)
            pool.dma_start(token_rows.rearrange("(b p) d -> p b d", p=P), xn[:]).then_inc(tokens_stored, 16)
            nc.gpsimd.memset(slots[:, NE], NO_PAIR).then_inc(rows_set, 1)
            nc.gpsimd.memset(x_rows[:], 0.0).then_inc(rows_set, 1)
            pool.wait_ge(rows_set, 3)
            pool.wait_ge(table_written, 16)
            pool.wait_ge(dest_ready, 1)
            for b in range(TB):
                for k in range(2):
                    nc.gpsimd.indirect_dma_start(
                        out=slot_table, out_offset=bass.IndirectOffsetOnAxis(ap=dest[:, k, b:b + 1], axis=0),
                        in_=pairs[:, b, k], in_offset=None).then_inc(table_written, 16)
            pool.wait_ge(table_written, 16 + 16 * 2 * TB)
            pool.dma_start(slots[:, 0:NE], slot_table[0:MAIN].rearrange("(s e) c -> s e c", s=P)).then_inc(slots_landed, 16)
            pool.dma_start(over_slots[:], slot_table[MAIN:].rearrange("(s v) c -> s v c", s=P)).then_inc(slots_landed, 16)
            pool.wait_ge(slots_landed, 32)
            pool.wait_ge(tokens_stored, 16)

            def gather(e):
                nc.gpsimd.indirect_dma_start(
                    out=x_rows[:, e % 2], out_offset=None, in_=token_rows,
                    in_offset=bass.IndirectOffsetOnAxis(ap=slots[:, e, 0:1], axis=0),
                    bounds_check=T - 1, oob_is_err=False).then_inc(x_gathered[e % 2], 16)

            gather(0)
            gather(1)
            for e in range(NE):
                pool.wait_ge(y_ready, e + 1)
                nc.gpsimd.indirect_dma_start(
                    out=pair_rows, out_offset=bass.IndirectOffsetOnAxis(ap=slots[:, e, 1:2], axis=0),
                    in_=y_rows[:, e % 2], in_offset=None, bounds_check=2 * T - 1, oob_is_err=False) \
                    .then_inc(y_free[e % 2], 16)
                if e + 2 <= NE:
                    pool.wait_ge(xe_turned, e + 1)
                    gather(e + 2)
            for b in range(2):
                pool.wait_ge(y_free[b], 16 * (NE // 2 + 1))
            with pool.If(overflowing(pool)):
                for v in range(N_OVER):
                    at_unit = pool.value_load(over_int[0:1, v:v + 1]) * PER_EXPERT + U_MOE
                    pool.dma_start(over_weights[:], weights_in[bass.ds(at_unit, 4)].rearrange("u p n -> p u n"))                         .then_inc(over_w, 16)
                    nc.gpsimd.indirect_dma_start(
                        out=x_rows[:, 0], out_offset=None, in_=token_rows,
                        in_offset=bass.IndirectOffsetOnAxis(ap=over_slots[:, v, 0:1], axis=0),
                        bounds_check=T - 1, oob_is_err=False).then_inc(over_x, 16)
                    pool.wait_ge(over_products, v * 4 + 2)
                    pool.dma_start(over_weights[:, 0:2], weights_in[bass.ds(at_unit + 4, 2)].rearrange("u p n -> p u n"))                         .then_inc(over_w, 16)
                    pool.wait_ge(over_copies, v * 4 + 4)
                    nc.gpsimd.indirect_dma_start(
                        out=pair_rows, out_offset=bass.IndirectOffsetOnAxis(ap=over_slots[:, v, 1:2], axis=0),
                        in_=y_rows[:, 0], in_offset=None, bounds_check=2 * T - 1, oob_is_err=False).then_inc(over_stored, 16)
                    pool.wait_ge(over_stored, v * 16 + 16)
            for b in range(TB):
                pool.dma_start(y_pairs[:, b], pair_rows[2 * P * b:2 * P * (b + 1)].rearrange("(p k) d -> p k d", k=2))                     .then_inc(y_landed[b], 16)

            pool.wait_ge(h0_ready, KC)
            pool.dma_start(par3[:], phase3_in).then_inc(params_landed, 16)
            pool.wait_ge(u_lo_ready, 3 * KC)
            for tile in (k_dec[0], k_dec[1], q_dec[0], q_dec[1], ws):
                nc.gpsimd.memset(tile[:], 0.0).then_inc(set_up, 1)
            with pool.Fori(0, HH // 2) as p:
                for hh in range(2):
                    if hh == 0:
                        pool.wait_ge(run_ready, p * 2 + 2)
                        pool.wait_ge(q_taken, p * 2 + 2)
                    else:
                        pool.wait_ge(k_ready, p * 14 + 7)
                        pool.wait_ge(q_ready, p * 14 + 7)
                        pool.wait_ge(lev_ready, p * 16 + 7)
                    for n in range(7):
                        w = 64 >> n
                        r3 = run[:, hh].rearrange("p (n t) -> p n t", t=2 * w)
                        x3 = fx[:, n % 2].rearrange("p (n t) -> p n t", t=2 * w)
                        ref = r3[:, :, w - 1:w].to_broadcast([P, T // (2 * w), w])
                        if n >= 2:
                            pool.wait_ge(k_ready, p * 14 + (7 * hh + n - 1))
                            pool.wait_ge(q_ready, p * 14 + (7 * hh + n - 1))
                        nc.gpsimd.tensor_tensor(x3[:, :, 0:w], ref, r3[:, :, 0:w], ALU.subtract)
                        nc.gpsimd.tensor_tensor(x3[:, :, w:], r3[:, :, w:], ref, ALU.subtract).then_inc(gap_to_ref, 1)
                        if n >= 1:
                            query_part(pool, p, hh, n - 1)
                    query_part(pool, p, hh, 6)

            def rope(m):
                pool.wait_ge(rope_mul, m + 1)
                kind, half = (m // 2) % 2, m % 2
                g = m // 8
                dst = (q_rot, k_rot)[kind][half]
                nc.gpsimd.tensor_tensor(group_order(dst[:], g), natural_order(r_cos[m % 2][:], g),
                                        natural_order(r_sin[m % 2][:], g), ALU.add).then_inc(rope_ready, 1)

            def sub_max(m):
                g, h = m // AH, m % AH
                pool.wait_ge(sc_max, m + 1)
                pr = prob_of(g, h)
                nc.gpsimd.tensor_tensor(pr, pr, stat[g][:, :, h:h + 1].to_broadcast(list(pr.shape)), ALU.subtract) \
                    .then_inc(sc_gap, 1)

            for pair in range(6):
                if pair:
                    pool.wait_ge(sc_ready, 2 * pair)
                for m in range(4):
                    rope(4 * pair + m)
                for half in range(2):
                    sub_max(2 * pair + half)
            pool.wait_ge(sc_sum, 3 * AH)
            for g in (1, 2):
                pool.dma_start(stat_rows[g - 1].rearrange("(p b) n -> p b n", b=TB), stat[g][:]).then_inc(order_stored, 16)
            pool.wait_ge(order_stored, 32)
            for g in (1, 2):
                pool.dma_start(stat_nat[g][:], stat_rows[g - 1].rearrange("(b p) n -> p b n", p=P)).then_inc(order_landed, 16)
            pool.wait_ge(share_ready, 3)
            for g in (1, 2):
                pool.dma_start(share_rows[g - 1].rearrange("(b p) n -> p b n", p=P), share[:, g]).then_inc(order_stored, 16)
            pool.wait_ge(order_stored, 64)
            for g in (1, 2):
                pool.dma_start(share_g[g][:], share_rows[g - 1].rearrange("(p b) n -> p b n", b=TB)).then_inc(order_landed, 16)
            for m in range(3 * AH):
                g, h = m // AH, m % AH
                if m == AH:
                    pool.wait_ge(order_landed, 64)
                factor = share[:, 0, :, h:h + 1] if g == 0 else share_g[g][:, :, h:h + 1]
                pr = prob_of(g, h)
                nc.gpsimd.tensor_tensor(pr, pr, factor.to_broadcast(list(pr.shape)), ALU.mult).then_inc(p_ready, 1)


def unit_cols(w):
    return w.reshape(KC, P, -1, 256).transpose(2, 1, 0, 3).reshape(-1, P, UNIT)


def unit_rows(w):
    k, n = w.shape
    short = -k % 512
    if short:
        w = np.concatenate([w, np.zeros((short, n), w.dtype)])
    return w.reshape(-1, 4, P, n // 512, 512).transpose(3, 0, 2, 1, 4).reshape(-1, P, UNIT)


def unit_experts(w_gate, w_up, w_down):
    def tall(w):
        return w.reshape(NE, 2, 4, P, FE).transpose(0, 1, 3, 2, 4).reshape(NE, 2, P, UNIT)
    down = w_down.reshape(NE, 2, 2, P, D).transpose(0, 1, 3, 2, 4).reshape(NE, 2, P, UNIT)
    return np.concatenate([tall(w_gate), tall(w_up), down], axis=1).reshape(-1, P, UNIT)


def unit_ffn(w_in, w_down):
    pair = np.concatenate([w_in[:, :FF].reshape(D, FC, P), w_in[:, FF:].reshape(D, FC, P)], axis=2)
    up = unit_cols(pair.reshape(D, FC * 256))
    cut = FA * P
    return [up[:FA], unit_rows(w_down[:cut]), up[FA:], unit_rows(w_down[cut:])]


def weight_stream(a):
    w = a["w_in"][0]
    q = HALF
    parts = [unit_cols(np.ascontiguousarray(w[:, :2 * q])), unit_cols(np.ascontiguousarray(w[:, 5 * q + 8:])),
             unit_cols(np.ascontiguousarray(w[:, 4 * q + 8:5 * q + 8])), unit_cols(np.ascontiguousarray(w[:, 3 * q:4 * q])),
             unit_cols(np.ascontiguousarray(w[:, 2 * q:3 * q])), unit_rows(a["w_out"][0]),
             unit_experts(a["w_gate"][0], a["w_up"][0], a["w_down"][0])]
    hg = unit_cols(a["hgrn_w_in_2"][0]).reshape(4, 4, P, UNIT)
    parts.append(np.ascontiguousarray(hg[[1, 0, 2, 3]].transpose(1, 0, 2, 3)).reshape(-1, P, UNIT))
    parts.append(unit_rows(a["hgrn_w_out_2"][0]))
    parts += unit_ffn(a["ffn_w_in_2"][0], a["ffn_w_down_2"][0])
    qkv = unit_cols(a["attn_w_qkv_2"][0]).reshape(3, 3, 2, P, UNIT)
    for g in range(3):
        parts.append(np.stack([qkv[2, g, 0], qkv[2, g, 1], qkv[0, g, 0], qkv[1, g, 0], qkv[0, g, 1], qkv[1, g, 1]]))
    parts.append(unit_rows(a["attn_w_out_2"][0]))
    parts += unit_ffn(a["ffn_w_in_2"][1], a["ffn_w_down_2"][1])
    out = np.concatenate(parts)
    assert out.shape[0] == N_UNITS
    return out


def pack(cols, n, parts):
    out = np.zeros((P, n), np.float32)
    for name, value in parts.items():
        at, size = cols[name]
        out[:value.shape[0], at:at + size] = value.reshape(value.shape[0], size)
    return out


def chunk_cols(v):
    return np.moveaxis(v.reshape(v.shape[:-1] + (-1, P)), -1, 0).reshape(P, -1)


def constants():
    s, t = np.arange(P)[:, None], np.arange(P)[None, :]
    sel = np.zeros((H1, H1, P))
    for h in range(H1):
        sel[h, h] = 1
    return pack(C_COLS, C_N, {
        "ident": s == t, "upper": s <= t, "strict": s < t, "ones": np.ones((P, P)), "blocks64": s // 64 == t // 64,
        "negmask": np.where(s <= t, 0, NEG), "sel": sel.reshape(H1, -1), "eps": np.full((P, 1), EPS),
        "iota32": np.broadcast_to(np.arange(NE), (P, NE))})


def phase1(a):
    w_if = np.zeros((KC, P, P), np.float32)
    src = a["w_in"][0][:, 4 * HALF:4 * HALF + 8].reshape(KC, P, 8)
    w_if[:, :, 0:4], w_if[:, :, 32:36] = src[..., :4], src[..., 4:]
    b_f = np.zeros((P, 1), np.float32)
    b_f[32:36, 0] = a["b_fgate"][0]
    return pack(P1_COLS, P1_N, {
        "n1g": chunk_cols(a["norm1_g"][0]), "conv": chunk_cols(a["conv_qk"][0]), "b_i": a["b_igate"][0][:, None],
        "b_f": b_f, "g_ml": chunk_cols(a["g_mlstm_out"][0]), "g_v": chunk_cols(a["g_gmlp_v"][0]),
        "g_gm": chunk_cols(a["g_gmlp_out"][0]),
        "b_sp": np.repeat(a["b_spatial"][0], 64, axis=0).reshape(4, P, P).transpose(1, 0, 2).reshape(P, -1),
        "w_sp": a["w_spatial"][0].transpose(2, 0, 1).reshape(P, -1),
        "w_if": w_if.transpose(1, 0, 2).reshape(P, -1), "one_row": np.ones((P, T))})


def phase2(a):
    w_r = np.concatenate([a["w_router_group"][0], a["w_router_expert"][0]], axis=1)
    b_r = np.concatenate([a["b_router_group"][0], a["b_router_expert"][0]])
    token = np.arange(T).reshape(TB, P).T
    pairs = np.stack([np.stack([token, 2 * token + k], axis=-1) for k in range(2)], axis=2)
    return pack(P2_COLS, P2_N, {
        "n2g": np.broadcast_to(a["norm2_g"][0], (P, D)), "w_r": w_r.reshape(KC, P, 36).transpose(1, 0, 2).reshape(P, -1),
        "b_r": np.broadcast_to(b_r, (P, 36)), "fg": chunk_cols(a["final_g"]), "pairs": pairs.reshape(P, -1)})


def phase3(a):
    s, t = np.arange(P)[:, None], np.arange(P)[None, :]
    levels = np.zeros((P, 8, P), np.uint32)
    for n, w in enumerate((64, 32, 16, 8, 4, 2, 1)):
        levels[:, n] = (s // (2 * w) == t // (2 * w)) & (s % (2 * w) < w) & (t % (2 * w) >= w)
    levels[:, 7] = s == t
    inv = (1.0 / (np.float32(10000.0) ** (np.arange(0, P, 2, dtype=np.float32) / np.float32(P)))).astype(np.float32)
    ang = (np.arange(T, dtype=np.float32)[:, None] * inv[None, :]).T
    cos, sin = np.cos(ang), np.sin(ang)
    key, query = t, s
    causal = np.where(key <= query, 0, NEG)
    never = np.full((P, P), NEG)
    band = np.concatenate([causal, never, np.where(key >= query, 0, NEG), causal,
                           causal, np.where((key <= query) & ((key - query) % (DIL[2] // STEP[2]) == 0), 0, NEG)], axis=1)
    reset = np.ones(T)
    reset[::P] = 0
    return pack(P3_COLS, P3_N, {
        "n_mix": chunk_cols(a["norm_mix_2"]), "n_ffn": chunk_cols(a["norm_ffn_2"]),
        "lb": chunk_cols(a["hgrn_lb_logits_2"]), "og": a["hgrn_out_norm_2"][0][:, None],
        "fin": np.broadcast_to(a["final_norm_2"], (P, D)),
        "levels": levels.view(np.float32), "cos": np.concatenate([cos, cos]), "sin": np.concatenate([sin, -sin]),
        "band": band, "reset": np.broadcast_to(reset, (P, T))})


def kernel(**inputs):
    import concourse.bacc as bacc
    from concourse.bass_utils import run_bass_kernel_spmd

    a = {name: np.asarray(value) for name, value in inputs.items()}
    nc = bacc.Bacc("TRN2", target_bir_lowering=False, num_devices=1)
    arrays = {"x_in": np.ascontiguousarray(a["x"][0]), "weights_in": weight_stream(a), "constants_in": constants(),
              "phase1_in": phase1(a), "phase2_in": phase2(a), "phase3_in": phase3(a)}
    aps = [nc.dram_tensor(name, v.shape, F32, kind="ExternalInput").ap() for name, v in arrays.items()]
    out = nc.dram_tensor("out_0", (T, D), F32, kind="ExternalOutput").ap()
    build(nc, *aps, out)
    r = run_bass_kernel_spmd(nc, [arrays], core_ids=[0])
    return r.results[0]["out_0"].reshape(1, T, D)
```
